# Optimizing a Trainium2 kernel written in Bass

```python
import jax, jax.numpy as jnp
from jax import lax
import numpy as np

D_MODEL = 1024
BATCH = 1
SEQ = 1024
DEPTH = 1

CHUNK = 64
Q_BLOCK = 128
EPS = 1e-6
NEG_INF = -1e30

MLA_HEADS = 4
MLA_NOPE = 128
MLA_ROPE = 64
MLA_V = 128
Q_LORA = 256
KV_LORA = 128
ROPE_THETA = 10000.0

RWKV_HEADS = 8
RWKV_HD = 64
RWKV_W = RWKV_HEADS * RWKV_HD
DECAY_LORA = 64
AAA_LORA = 64
GATE_LORA = 128
LNX_EPS = 64e-5

MLA_OUT = MLA_HEADS * MLA_V
MIX_W = MLA_OUT + RWKV_W

MLA_IN = Q_LORA + KV_LORA + MLA_ROPE
RWKV_IN = 3 * RWKV_W + DECAY_LORA + AAA_LORA + GATE_LORA
IN_COLS = MLA_IN + RWKV_IN

MEM_TOKENS = 256
XA_HEADS = 4
XA_HD = D_MODEL // XA_HEADS

PEER_HEADS = 8
N_KEYS = 128
N_EXPERTS = N_KEYS * N_KEYS
PEER_TOPK = 16
PEER_QDIM = 256
PEER_HALF = PEER_QDIM // 2
TOKEN_BLOCK = 128

kernel_name = "hybrid_mla_rwkv7_peer_block"

def _rmsnorm(x, g):
    xf = x.astype(jnp.float32)
    y = xf * lax.rsqrt(jnp.mean(xf * xf, axis=-1, keepdims=True) + EPS)
    return (y * g.astype(jnp.float32)).astype(x.dtype)

def _split(p, sizes):
    return jnp.split(p, np.cumsum(sizes)[:-1].tolist(), axis=-1)

def _rope(t, positions):
    d = t.shape[-1]
    inv = ROPE_THETA ** (-jnp.arange(0, d, 2, dtype=jnp.float32) / d)
    ang = positions.astype(jnp.float32)[..., None] * inv
    cos, sin = jnp.cos(ang)[:, :, None, :], jnp.sin(ang)[:, :, None, :]
    tf = t.astype(jnp.float32)
    t1, t2 = tf[..., : d // 2], tf[..., d // 2:]
    return jnp.concatenate([t1 * cos - t2 * sin, t1 * sin + t2 * cos], axis=-1).astype(t.dtype)

def _mla_group(p, positions, q_norm_g, kv_norm_g, w_uq, w_ukv):
    B, S, _ = p.shape
    c_q, c_kv, k_r = _split(p, [Q_LORA, KV_LORA, MLA_ROPE])
    q = (_rmsnorm(c_q, q_norm_g) @ w_uq).reshape(B, S, MLA_HEADS, MLA_NOPE + MLA_ROPE)
    kv = (_rmsnorm(c_kv, kv_norm_g) @ w_ukv).reshape(B, S, MLA_HEADS, MLA_NOPE + MLA_V)
    q_nope, q_rope = q[..., :MLA_NOPE], _rope(q[..., MLA_NOPE:], positions)
    k_nope, v = kv[..., :MLA_NOPE], kv[..., MLA_NOPE:]
    k_rope = jnp.broadcast_to(_rope(k_r[:, :, None, :], positions), (B, S, MLA_HEADS, MLA_ROPE))
    q = jnp.concatenate([q_nope, q_rope], axis=-1)
    k = jnp.concatenate([k_nope, k_rope], axis=-1)
    scale = (MLA_NOPE + MLA_ROPE) ** -0.5
    chunk_id = jnp.arange(S) // CHUNK
    outs = []
    for i in range(S // Q_BLOCK):
        s0, s1 = i * Q_BLOCK, (i + 1) * Q_BLOCK
        sc = jnp.einsum('bqhd,bkhd->bhqk', q[:, s0:s1], k[:, :s1],
                        preferred_element_type=jnp.float32) * scale
        mask = chunk_id[s0:s1, None] >= chunk_id[None, :s1]
        sc = jnp.where(mask[None, None], sc, NEG_INF)
        pr = jax.nn.softmax(sc, axis=-1).astype(v.dtype)
        outs.append(jnp.einsum('bhqk,bkhd->bqhd', pr, v[:, :s1]))
    return jnp.concatenate(outs, axis=1).reshape(B, S, MLA_OUT)

def _rwkv_scan(r, w, k, v, kk, a):
    B, S, H, N = r.shape

    def step(state, inp):
        r_t, w_t, k_t, v_t, kk_t, a_t = inp
        sa = jnp.einsum('bhvk,bhk->bhv', state, kk_t)
        state = (state * w_t[:, :, None, :]
                 - sa[..., None] * (kk_t * a_t)[:, :, None, :]
                 + v_t[..., None] * k_t[:, :, None, :])
        return state, jnp.einsum('bhvk,bhk->bhv', state, r_t)

    xs = tuple(jnp.moveaxis(t, 1, 0) for t in (r, w, k, v, kk, a))
    _, ys = lax.scan(step, jnp.zeros((B, H, N, N), jnp.float32), xs)
    return jnp.moveaxis(ys, 0, 1)

def _rwkv7_group(p, shift_mu, w0, w_up, a0, a_up, g_up, k_k, k_a, r_k, lnx_w, lnx_b):
    B, S, _ = p.shape
    f32 = jnp.float32
    p_prev = jnp.pad(p[:, :-1], ((0, 0), (1, 0), (0, 0)))
    p = p + (p_prev - p) * shift_mu
    r, k, v, wd, ad, gd = _split(p, [RWKV_W, RWKV_W, RWKV_W, DECAY_LORA, AAA_LORA, GATE_LORA])
    r, k, v = r.astype(f32), k.astype(f32), v.astype(f32)
    w_pre = (w0 + jnp.tanh(wd) @ w_up).astype(f32)
    decay = jnp.exp(-jnp.exp(-jax.nn.softplus(-w_pre) - 0.5))
    a = jax.nn.sigmoid((a0 + ad @ a_up).astype(f32))
    g = (jax.nn.sigmoid(gd) @ g_up).astype(f32)
    hs = lambda t: t.reshape(B, S, RWKV_HEADS, RWKV_HD)
    kk = hs(k * k_k.astype(f32))
    kk = kk / jnp.maximum(jnp.linalg.norm(kk, axis=-1, keepdims=True), 1e-12)
    k = k * (1.0 + (a - 1.0) * k_a.astype(f32))
    r, k, v, decay, a = hs(r), hs(k), hs(v), hs(decay), hs(a)
    y = _rwkv_scan(r, decay, k, v, kk, a)
    mu = jnp.mean(y, axis=-1, keepdims=True)
    var = jnp.mean(jnp.square(y - mu), axis=-1, keepdims=True)
    y = ((y - mu) * lax.rsqrt(var + LNX_EPS)).reshape(B, S, RWKV_W)
    y = y * lnx_w.astype(f32) + lnx_b.astype(f32)
    bonus = jnp.sum(r * k * r_k.astype(f32), axis=-1, keepdims=True) * v
    y = (y + bonus.reshape(B, S, RWKV_W)) * g
    return y.astype(p.dtype)

def _cross_attention(hn, memn, wq, wk, wv, wo):
    B, S, _ = hn.shape
    M = memn.shape[1]
    q = (hn @ wq).reshape(B, S, XA_HEADS, XA_HD)
    km = (memn @ wk).reshape(B, M, XA_HEADS, XA_HD)
    vm = (memn @ wv).reshape(B, M, XA_HEADS, XA_HD)
    sc = jnp.einsum('bqhd,bmhd->bhqm', q, km, preferred_element_type=jnp.float32) * XA_HD ** -0.5
    pr = jax.nn.softmax(sc, axis=-1).astype(vm.dtype)
    o = jnp.einsum('bhqm,bmhd->bqhd', pr, vm).reshape(B, S, D_MODEL)
    return o @ wo

def _peer(hn, w_query, sub_keys, expert_u, expert_v):
    B, S, D = hn.shape
    q = (hn @ w_query).reshape(B, S, PEER_HEADS, 2, PEER_HALF)
    s = jnp.einsum('bshpd,hpkd->bshpk', q, sub_keys, preferred_element_type=jnp.float32)
    v1, i1 = lax.top_k(s[..., 0, :], PEER_TOPK)
    v2, i2 = lax.top_k(s[..., 1, :], PEER_TOPK)
    cand = (v1[..., :, None] + v2[..., None, :]).reshape(B, S, PEER_HEADS, PEER_TOPK * PEER_TOPK)
    cv, ci = lax.top_k(cand, PEER_TOPK)
    e1 = jnp.take_along_axis(i1, ci // PEER_TOPK, axis=-1)
    e2 = jnp.take_along_axis(i2, ci % PEER_TOPK, axis=-1)
    expert = e1 * N_KEYS + e2
    gate = jax.nn.softmax(cv, axis=-1)
    T = B * S
    nb = T // TOKEN_BLOCK
    HK = PEER_HEADS * PEER_TOPK
    xb = hn.reshape(nb, TOKEN_BLOCK, D)
    ib = expert.reshape(nb, TOKEN_BLOCK, HK)
    gb = gate.reshape(nb, TOKEN_BLOCK, HK)

    def block(args):
        xt, it, gt = args
        u = expert_u[it]
        pre = jnp.einsum('tkd,td->tk', u, xt, preferred_element_type=jnp.float32)
        act = (jax.nn.gelu(pre, approximate=False) * gt).astype(xt.dtype)
        return jnp.einsum('tk,tkd->td', act, expert_v[it])

    return lax.map(block, (xb, ib, gb)).reshape(B, S, D)

def setup_inputs(seed: int = 0) -> dict:
    key = jax.random.key(seed)
    ks = iter(jax.random.split(key, 64))
    f32 = jnp.float32
    L = DEPTH

    def nrm(shape, scale):
        return jax.random.normal(next(ks), shape, f32) * scale

    def gain(shape):
        return 1.0 + nrm(shape, 0.02)

    x = nrm((BATCH, SEQ, D_MODEL), 1.0)
    mem = nrm((BATCH, MEM_TOKENS, D_MODEL), 1.0)
    offsets = jax.random.randint(next(ks), (BATCH, 1), 0, 4096, dtype=jnp.int32)
    positions = offsets + jnp.arange(SEQ, dtype=jnp.int32)[None, :]
    return {
        "x": x,
        "mem": mem,
        "positions": positions,
        "norm_mix_g": gain((L, D_MODEL)),
        "w_in": nrm((L, D_MODEL, IN_COLS), D_MODEL ** -0.5),
        "shift_mu": jax.random.uniform(next(ks), (L, RWKV_IN), f32),
        "q_norm_g": gain((L, Q_LORA)),
        "kv_norm_g": gain((L, KV_LORA)),
        "w_uq": nrm((L, Q_LORA, MLA_HEADS * (MLA_NOPE + MLA_ROPE)), Q_LORA ** -0.5),
        "w_ukv": nrm((L, KV_LORA, MLA_HEADS * (MLA_NOPE + MLA_V)), KV_LORA ** -0.5),
        "rw_w0": nrm((L, RWKV_W), 1.0),
        "rw_w_up": nrm((L, DECAY_LORA, RWKV_W), DECAY_LORA ** -0.5),
        "rw_a0": nrm((L, RWKV_W), 0.5),
        "rw_a_up": nrm((L, AAA_LORA, RWKV_W), AAA_LORA ** -0.5),
        "rw_g_up": nrm((L, GATE_LORA, RWKV_W), GATE_LORA ** -0.5),
        "rw_k_k": 0.85 + nrm((L, RWKV_W), 0.05),
        "rw_k_a": 1.0 + nrm((L, RWKV_W), 0.05),
        "rw_r_k": nrm((L, RWKV_HEADS, RWKV_HD), 0.1),
        "rw_lnx_w": gain((L, RWKV_W)),
        "rw_lnx_b": nrm((L, RWKV_W), 0.02),
        "w_out": nrm((L, MIX_W, D_MODEL), MIX_W ** -0.5),
        "norm_xa_g": gain((L, D_MODEL)),
        "norm_mem_g": gain((L, D_MODEL)),
        "xa_wq": nrm((L, D_MODEL, D_MODEL), D_MODEL ** -0.5),
        "xa_wk": nrm((L, D_MODEL, D_MODEL), D_MODEL ** -0.5),
        "xa_wv": nrm((L, D_MODEL, D_MODEL), D_MODEL ** -0.5),
        "xa_wo": nrm((L, D_MODEL, D_MODEL), D_MODEL ** -0.5),
        "norm_ffn_g": gain((L, D_MODEL)),
        "peer_wq": nrm((L, D_MODEL, PEER_HEADS * PEER_QDIM), D_MODEL ** -0.5),
        "peer_keys": nrm((L, PEER_HEADS, 2, N_KEYS, PEER_HALF), PEER_HALF ** -0.5),
        "expert_u": nrm((L, N_EXPERTS, D_MODEL), D_MODEL ** -0.5),
        "expert_v": nrm((L, N_EXPERTS, D_MODEL), 0.05),
        "final_norm_g": gain((D_MODEL,)),
    }

def reference(x, mem, positions, norm_mix_g, w_in, shift_mu, q_norm_g, kv_norm_g, w_uq, w_ukv,
              rw_w0, rw_w_up, rw_a0, rw_a_up, rw_g_up, rw_k_k, rw_k_a, rw_r_k, rw_lnx_w, rw_lnx_b,
              w_out, norm_xa_g, norm_mem_g, xa_wq, xa_wk, xa_wv, xa_wo,
              norm_ffn_g, peer_wq, peer_keys, expert_u, expert_v, final_norm_g):
    h = x
    for l in range(DEPTH):
        hn = _rmsnorm(h, norm_mix_g[l])
        p = hn @ w_in[l]
        p_mla, p_rwkv = p[..., :MLA_IN], p[..., MLA_IN:]
        y_mla = _mla_group(p_mla, positions, q_norm_g[l], kv_norm_g[l], w_uq[l], w_ukv[l])
        y_rwkv = _rwkv7_group(p_rwkv, shift_mu[l], rw_w0[l], rw_w_up[l], rw_a0[l], rw_a_up[l],
                              rw_g_up[l], rw_k_k[l], rw_k_a[l], rw_r_k[l], rw_lnx_w[l], rw_lnx_b[l])
        h = h + jnp.concatenate([y_mla, y_rwkv], axis=-1) @ w_out[l]
        hn = _rmsnorm(h, norm_xa_g[l])
        memn = _rmsnorm(mem, norm_mem_g[l])
        h = h + _cross_attention(hn, memn, xa_wq[l], xa_wk[l], xa_wv[l], xa_wo[l])
        hn = _rmsnorm(h, norm_ffn_g[l])
        h = h + _peer(hn, peer_wq[l], peer_keys[l], expert_u[l], expert_v[l])
    return _rmsnorm(h, final_norm_g)


_drawn_inputs = setup_inputs


def setup_inputs(seed=0):
    import zlib

    import numpy as np

    out = dict(_drawn_inputs(seed))
    spreads = {}
    factors = {'norm_mix_g': 4.177,
     'q_norm_g': 8.0,
     'kv_norm_g': 8.0,
     'rw_k_k': 32.295,
     'rw_k_a': 2.755,
     'rw_lnx_w': 23.355,
     'rw_lnx_b': 27.335,
     'norm_xa_g': 8.0,
     'norm_mem_g': 8.0,
     'norm_ffn_g': 64.0,
     'expert_u': 2.783,
     'final_norm_g': 7.502}
    for name, (base, spread) in spreads.items():
        noise = np.random.default_rng([zlib.crc32(name.encode()), seed]).standard_normal(out[name].shape)
        drawn = base * np.exp(spread * noise) if base else spread * noise
        out[name] = __import__('jax').numpy.asarray(drawn.astype(out[name].dtype))
    for name, factor in factors.items():
        out[name] = (out[name] * factor).astype(out[name].dtype)
    return out
```

```python
from contextlib import ExitStack

import concourse.bass as bass
import numpy as np
from concourse import mybir

F32 = mybir.dt.float32
F32R = mybir.dt.float32r
I32 = mybir.dt.int32
U32 = mybir.dt.uint32
ALU = mybir.AluOpType
ACT = mybir.ActivationFunctionType
AX = mybir.AxisListType

P = 128
D = 1024
T = 1024
KC = D // P
NT = T // P
HALF = 512
EPS = 1e-6

MLA_HEADS = 4
ROPE = 64
Q_LORA = 256
KV_LORA = 128
RW = 512
PAIRS = 4
CH = 64
LNX_EPS = 64e-5
MEM = 256
XH = 4
PH = 8
NK = 128
TOPK = 16

CQ, CKV, RT, KT, VT, GT, NF = 0, 2, 3, 7, 11, 15, 16
KR, WD, AD = 0, 1, 2

COLS = {}
_at = 0
for _name, _n in (("mix", 8), ("xa", 8), ("mem", 8), ("ffn", 8), ("w0", 4), ("a0", 4), ("kk", 4), ("ka", 4),
                  ("rk", 4), ("lnw", 4), ("lnb", 4), ("qg", 2), ("kvg", 1), ("mu", 16), ("mu64", 3),
                  ("inv", 1), ("fin", 8)):
    COLS[_name] = _at
    _at += _n
NCOLS = _at




class Stage:

    def __init__(self, nc, name):
        self.nc, self.name, self.stack, self.sems = nc, name, ExitStack(), []

    def __enter__(self):
        return self

    def __exit__(self, *e):
        done = self.stack.__exit__(*e)
        if e[0] is None:
            self.nc.clear_and_free_semaphores(self.sems)
            self.nc.all_engine_barrier()
        return done

    def sb(self, name, shape, dt=F32):
        return self.stack.enter_context(self.nc.sbuf_tensor(f"{self.name}_{name}", shape, dt))

    def psum(self, name, shape, dt=F32):
        return self.stack.enter_context(self.nc.psum_tensor(f"{self.name}_{name}", shape, dt))

    def sem(self, name):
        self.sems.append(self.nc.alloc_semaphore(f"{self.name}_{name}"))
        return self.sems[-1]

    def block(self):
        return self.stack.enter_context(self.nc.Block())


def col(consts, name, i=0, rows=P):
    c = COLS[name] + i
    return consts["cols"][0:rows, c:c + 1]


def cols_over(consts, name, n, width):
    c = COLS[name]
    return consts["cols"][:, c:c + n].unsqueeze(2).broadcast_to([P, n, width])


def build_constants(nc, consts, cols_d):
    with Stage(nc, "const") as st:
        loaded, made = st.sem("loaded"), st.sem("made")
        block = st.block()

        @block.sync
        def _(sp):
            sp.dma_start(consts["cols"][:, :], cols_d).then_inc(loaded, 16)
            sp.wait_ge(loaded, 16)

        @block.gpsimd
        def _(pool):
            nc.gpsimd.memset(consts["ones"][:, :], 1.0)
            nc.gpsimd.memset(consts["eps"][:, 0:1], EPS)
            nc.gpsimd.memset(consts["eps"][:, 1:2], LNX_EPS).then_inc(made, 1)
            nc.gpsimd.memset(consts["ident"][:, :], 0.0).then_inc(made, 1)
            pool.wait_ge(made, 2)
            nc.gpsimd.affine_select(out=consts["ident"][:, :], in_=consts["ident"][:, :], compare_op=ALU.not_equal,
                                    fill=1.0, base=0, pattern=[[-1, P]], channel_multiplier=1).then_inc(made, 1)
            bd = consts["headones"]
            nc.gpsimd.memset(bd[:, :], 1.0).then_inc(made, 1)
            pool.wait_ge(made, 4)
            nc.gpsimd.memset(bd[0:64, 64:128], 0.0).then_inc(made, 1)
            nc.gpsimd.memset(bd[64:128, 0:64], 0.0).then_inc(made, 1)
            rot = consts["rot"]
            nc.gpsimd.memset(rot[:, :], 0.0).then_inc(made, 1)
            pool.wait_ge(made, 7)
            nc.gpsimd.affine_select(out=rot[:, 0:32], in_=rot[:, 0:32], compare_op=ALU.not_equal, fill=-1.0,
                                    base=-32, pattern=[[-1, 32]], channel_multiplier=1)
            nc.gpsimd.affine_select(out=rot[:, 32:64], in_=rot[:, 32:64], compare_op=ALU.not_equal, fill=1.0,
                                    base=0, pattern=[[-1, 32]], channel_multiplier=1).then_inc(made, 1)
            m4 = consts["mask4"]
            nc.gpsimd.memset(m4[:, :, :], 1.0).then_inc(made, 1)
            lv = consts["level"]
            nc.gpsimd.memset(lv[:, :, :], 1.0).then_inc(made, 1)
            low = consts["lower"]
            nc.gpsimd.memset(low[:, :], 1.0).then_inc(made, 1)
            up0 = consts["upper0"]
            nc.gpsimd.memset(up0[:, :], 0.0).then_inc(made, 1)
            n = 12
            for i in range(4):
                pool.wait_ge(made, n)
                nc.gpsimd.affine_select(out=m4[:, i, :], in_=m4[:, i, :], compare_op=ALU.is_ge, fill=0.0,
                                        base=-1 if i % 2 == 0 else 0, pattern=[[1, P]],
                                        channel_multiplier=-1).then_inc(made, 1)
                n += 1
                pool.wait_ge(made, n)
                nc.gpsimd.memset(m4[0:64, i, 64:128], 0.0).then_inc(made, 1)
                n += 1
            nc.gpsimd.affine_select(out=low[:, :], in_=low[:, :], compare_op=ALU.is_ge, fill=0.0, base=-1,
                                    pattern=[[-1, P]], channel_multiplier=1).then_inc(made, 1)
            n += 1
            pool.wait_ge(made, n)
            nc.gpsimd.memset(low[64:128, 0:64], 0.0).then_inc(made, 1)
            n += 1
            pool.wait_ge(made, n)
            for l in range(6):
                b = 1 << l
                v = lv[:, l, :].rearrange("p (j y) -> p j y", y=2 * b)
                nc.gpsimd.memset(v[:, :, b:2 * b], 0.0).then_inc(made, 1)
                n += 1
                pool.wait_ge(made, n)
                nc.gpsimd.affine_select(out=v[:, :, 0:b], in_=v[:, :, 0:b], compare_op=ALU.is_ge, fill=0.0,
                                        base=-b, pattern=[[-2 * b, P // (2 * b)], [0, b]],
                                        channel_multiplier=1).then_inc(made, 1)
                n += 1
                pool.wait_ge(made, n)
                nc.gpsimd.affine_select(out=v[:, :, 0:b], in_=v[:, :, 0:b], compare_op=ALU.is_ge, fill=0.0,
                                        base=2 * b - 1, pattern=[[2 * b, P // (2 * b)], [0, b]],
                                        channel_multiplier=-1).then_inc(made, 1)
                n += 1
                pool.wait_ge(made, n)
            v = up0[:, :].rearrange("p (j y) -> p j y", y=2)[:, :, 1]
            nc.gpsimd.affine_select(out=v, in_=v, compare_op=ALU.not_equal, fill=1.0, base=0,
                                    pattern=[[-2, 64]], channel_multiplier=1).then_inc(made, 1)
            sm = consts["scanmask"]
            nc.gpsimd.memset(sm[:, :], 1.0).then_inc(made, 1)
            n += 2
            pool.wait_ge(made, n)
            nc.gpsimd.memset(sm[:, :].rearrange("p (c t) -> p c t", t=CH)[:, :, 0:1], 0.0).then_inc(made, 1)


def norm_stage(nc, consts, name, src, gain, dst, width, load=None):
    halves = [(a, min(HALF, width - a)) for a in range(0, width, HALF)]
    with Stage(nc, name) as st:
        sq = st.sb("sq", [P, 2, width])
        std = st.sb("std", [P, width])
        sums = [st.psum(f"sums{i}", [P, HALF]) for i in range(len(halves))]
        loaded, sq_ready, sq_used = st.sem("loaded"), st.sem("sq_ready"), st.sem("sq_used")
        std_ready, rstd_ready = st.sem("std_ready"), st.sem("rstd_ready")
        block = st.block()

        @block.sync
        def _(sp):
            if load is not None:
                for kc in range(KC):
                    sp.dma_start(src[:, kc, :], load[kc]).then_inc(loaded, 16)

        @block.scalar
        def _(act):
            for kc in range(KC):
                if load is not None:
                    act.wait_ge(loaded, 16 * KC)
                if kc >= 2:
                    act.wait_ge(sq_used, kc - 1)
                nc.scalar.activation(sq[:, kc % 2, :], src[:, kc, :], ACT.Square).then_inc(sq_ready, 1)
            act.wait_ge(sq_used, KC)
            for i, (a, w) in enumerate(halves):
                nc.scalar.activation(std[:, a:a + w], sums[i][:, 0:w], ACT.Sqrt, bias=consts["eps"][:, 0:1],
                                     scale=1.0 / D).then_inc(std_ready, 1)

        @block.tensor
        def _(pe):
            for kc in range(KC):
                pe.wait_ge(sq_ready, kc + 1)
                for i, (a, w) in enumerate(halves):
                    last = nc.tensor.matmul(sums[i][:, 0:w], consts["ones"][:, :], sq[:, kc % 2, a:a + w],
                                            start=(kc == 0), stop=(kc == KC - 1))
                last.then_inc(sq_used, 1)

        @block.vector
        def _(dve):
            if load is not None:
                dve.wait_ge(loaded, 16 * KC)
            dve.wait_ge(std_ready, len(halves))
            nc.vector.reciprocal(std[:, :], std[:, :]).then_inc(rstd_ready, 1)
            dve.wait_ge(rstd_ready, 1)
            for kc in range(KC):
                nc.vector.scalar_tensor_tensor(out=dst[:, kc, :], in0=src[:, kc, :], scalar=col(consts, gain, kc),
                                               in1=std[:, :], op0=ALU.mult, op1=ALU.mult)


def project_in_stage(nc, consts, normed, w_full, w_half, feats_d, feats64_d):
    with Stage(nc, "pin") as st:
        w = [st.sb(f"w{i}", [P, KC, P]) for i in range(2)]
        w64 = st.sb("w64", [P, 3, KC, 64])
        raw = [st.sb(f"raw{i}", [P, T + 1]) for i in range(2)]
        shifted = [st.sb(f"shifted{i}", [P, T]) for i in range(2)]
        diff = st.sb("diff", [P, T])
        mu_tile = st.sb("mu", [P, 2])
        ps = [st.psum(f"ps{i}", [P, 2, HALF]) for i in range(2)]
        w_ready = [st.sem(f"w_ready{i}") for i in range(2)]
        stored = [st.sem(f"stored{i}") for i in range(2)]
        w64_ready = st.sem("w64_ready")
        mm_done, raw_ready, shift_done = st.sem("mm_done"), st.sem("raw_ready"), st.sem("shift_done")
        block = st.block()

        @block.sync
        def _(sp):
            for i in range(2):
                sp.dma_start(w[i][:, :, :], w_full[i]).then_inc(w_ready[i], 16)
            sp.dma_start(w64[:, :, :, :], w_half.rearrange("j p k c -> p j k c")).then_inc(w64_ready, 16)
            with sp.Fori(1, NF // 2) as g:
                for i in range(2):
                    sp.wait_ge(mm_done, g * 2 + (i - 1))
                    sp.dma_start(w[i][:, :, :], w_full[bass.ds(g * 2 + i, 1)].rearrange(
                        "a p k c -> p (a k) c")).then_inc(w_ready[i], 16)
                    sp.wait_ge(shift_done, g * 2 + (i + 1))
                    sp.dma_start(feats_d[bass.ds(g * 2 + (i - 2), 1)].rearrange("a p t -> (a p) t"),
                                 shifted[i][:, :]).then_inc(stored[i], 16)
            for i in range(2):
                sp.wait_ge(shift_done, NF + i + 1)
                sp.dma_start(feats_d[NF - 2 + i], shifted[i][:, :]).then_inc(stored[i], 16)
            for j in range(3):
                sp.wait_ge(shift_done, NF + j + 3)
                sp.dma_start(feats64_d[j], shifted[j % 2][0:64, :]).then_inc(stored[j % 2], 16)
            sp.wait_ge(stored[0], 16 * (NF // 2 + 3))
            sp.wait_ge(stored[1], 16 * (NF // 2 + 2))

        @block.tensor
        def _(pe):
            def tile(i, lhs, out_rows):
                for kc in range(KC):
                    for h in range(2):
                        last = nc.tensor.matmul(ps[i][0:out_rows, h, :], lhs(kc),
                                                normed[:, kc, h * HALF:(h + 1) * HALF],
                                                start=(kc == 0), stop=(kc == KC - 1))
                last.then_inc(mm_done, 1)

            with pe.Fori(0, NF // 2) as g:
                for i in range(2):
                    pe.wait_ge(w_ready[i], g * 16 + 16)
                    pe.wait_ge(raw_ready, g * 2 + (i + 1))
                    tile(i, lambda kc: w[i][:, kc, :], P)
            pe.wait_ge(w64_ready, 16)
            for j in range(3):
                pe.wait_ge(raw_ready, NF + j + 1)
                tile(j % 2, lambda kc: w64[:, j, kc, :], 64)

        @block.scalar
        def _(act):
            for i in range(2):
                nc.scalar.activation(raw[i][:, 0:1], consts["ones"][:, 0:1], ACT.Copy, scale=0.0).then_inc(raw_ready, 1)
            with act.Fori(0, NF // 2) as g:
                for i in range(2):
                    act.wait_ge(mm_done, g * 2 + (i + 1))
                    act.wait_ge(shift_done, g * 2 + (i + 1))
                    nc.scalar.activation(raw[i][:, 1:T + 1], ps[i][:, :, :], ACT.Copy).then_inc(raw_ready, 1)
            for j in range(3):
                act.wait_ge(mm_done, NF + j + 1)
                act.wait_ge(shift_done, NF + j + 1)
                nc.scalar.activation(raw[j % 2][0:64, 1:T + 1], ps[j % 2][0:64, :, :], ACT.Copy).then_inc(raw_ready, 1)

        @block.vector
        def _(dve):
            def shift(i, rows, mu):
                nc.vector.tensor_tensor(diff[0:rows, :], raw[i][0:rows, 0:T], raw[i][0:rows, 1:T + 1], ALU.subtract)
                dve.drain()
                nc.vector.scalar_tensor_tensor(out=shifted[i][0:rows, :], in0=diff[0:rows, :], scalar=mu,
                                               in1=raw[i][0:rows, 1:T + 1],
                                               op0=ALU.mult, op1=ALU.add).then_inc(shift_done, 1)

            for i in range(2):
                nc.vector.memset(mu_tile[:, i:i + 1], 0.0).then_inc(shift_done, 1)
                nc.vector.memset(diff[:, i:i + 1], 0.0).then_inc(stored[i], 16)
            mu0 = COLS["mu"]
            with dve.Fori(0, NF // 2) as g:
                for i in range(2):
                    dve.drain()
                    nc.vector.tensor_copy(mu_tile[:, i:i + 1], consts["cols"][:, bass.ds(g * 2 + (mu0 + i), 1)])
                    dve.drain()
                    dve.wait_ge(raw_ready, g * 2 + (i + 3))
                    dve.wait_ge(stored[i], g * 16 + 16)
                    shift(i, P, mu_tile[:, i:i + 1])
            for j in range(3):
                dve.drain()
                dve.wait_ge(raw_ready, NF + j + 3)
                dve.wait_ge(stored[j % 2], 16 * (NF // 2 + 1 + j // 2))
                shift(j % 2, 64, col(consts, "mu64", j, 64))


TWO_PI = 2.0 * np.pi
TWO_PI_A = 6.28125
TWO_PI_B = float(np.float32(round((TWO_PI - TWO_PI_A) * 2 ** 21) / 2 ** 21))
TWO_PI_C = float(TWO_PI - TWO_PI_A - TWO_PI_B)
ROUNDER = 12582912.0
PI_BELOW = 3.1415925


def mla_prepare_stage(nc, consts, feats, feats_d, feats64_d, positions, cos, sin, krope):
    with Stage(nc, "mprep") as st:
        sq = st.sb("sq", [P, 3, T])
        std = st.sb("std", [P, 2, T])
        pos_i = st.sb("pos_i", [ROPE, T], I32)
        ang = st.sb("ang", [ROPE, T])
        turns = st.sb("turns", [ROPE, T])
        krot = st.sb("krot", [ROPE, T])
        kr = st.sb("kr", [ROPE, T])
        sums = st.psum("sums", [P, 4, HALF])
        rot_ps = st.psum("rot_ps", [P, 2, HALF])
        loaded, sq_ready, sums_ready = st.sem("loaded"), st.sem("sq_ready"), st.sem("sums_ready")
        std_ready, rot_ready, angle_ready = st.sem("std_ready"), st.sem("rot_ready"), st.sem("angle_ready")
        trig_ready, pos_loaded = st.sem("trig_ready"), st.sem("pos_loaded")
        block = st.block()

        @block.sync
        def _(sp):
            sp.dma_start(pos_i[:, :], positions.broadcast_to([ROPE, T])).then_inc(pos_loaded, 16)
            sp.dma_start(feats[:, :, :], feats_d[0:3].rearrange("f p t -> p f t")).then_inc(loaded, 16)
            sp.dma_start(kr[:, :], feats64_d[KR]).then_inc(loaded, 16)

        @block.scalar
        def _(act):
            act.wait_ge(loaded, 32)
            for f in range(3):
                nc.scalar.activation(sq[:, f, :], feats[:, f, :], ACT.Square).then_inc(sq_ready, 1)
            act.wait_ge(sums_ready, 1)
            nc.scalar.activation(std[:, 0, :], sums[:, 0:2, :], ACT.Sqrt, bias=consts["eps"][:, 0:1],
                                 scale=1.0 / Q_LORA).then_inc(std_ready, 1)
            nc.scalar.activation(std[:, 1, :], sums[:, 2:4, :], ACT.Sqrt, bias=consts["eps"][:, 0:1],
                                 scale=1.0 / KV_LORA).then_inc(std_ready, 1)
            for i, out in enumerate((sin, cos)):
                act.wait_ge(angle_ready, i + 1)
                nc.scalar.activation(out[:, :], (krot if i == 0 else turns)[:, :], ACT.Sin).then_inc(trig_ready, 1)

        @block.tensor
        def _(pe):
            pe.wait_ge(loaded, 32)
            for h in range(2):
                nc.tensor.matmul(rot_ps[:, h, :], consts["rot"][:, :], kr[:, h * HALF:(h + 1) * HALF],
                                 start=True, stop=True).then_inc(rot_ready, 1)
            pe.wait_ge(sq_ready, 3)
            for f in range(3):
                for h in range(2):
                    last = nc.tensor.matmul(sums[:, (f // 2) * 2 + h, :], consts["ones"][:, :],
                                            sq[:, f, h * HALF:(h + 1) * HALF], start=(f != 1), stop=(f != 0))
            last.then_inc(sums_ready, 1)

        @block.vector
        def _(dve):
            def reduce_angle(out, quarter):
                nc.vector.tensor_scalar(out[:, :], ang[:, :], float(1.0 / TWO_PI), 0.25 * quarter, ALU.mult, ALU.add)
                dve.drain()
                nc.vector.tensor_scalar(cos[:, :], out[:, :], ROUNDER, -ROUNDER, ALU.add, ALU.add)
                dve.drain()
                nc.vector.scalar_tensor_tensor(out=out[:, :], in0=cos[:, :], scalar=-TWO_PI_A, in1=ang[:, :],
                                               op0=ALU.mult, op1=ALU.add)
                dve.drain()
                for part in (TWO_PI_B, TWO_PI_C):
                    nc.vector.scalar_tensor_tensor(out=out[:, :], in0=cos[:, :], scalar=-part, in1=out[:, :],
                                                   op0=ALU.mult, op1=ALU.add)
                    dve.drain()
                if quarter:
                    nc.vector.tensor_scalar(out[:, :], out[:, :], float(np.pi / 2), None, ALU.add)
                    dve.drain()
                nc.vector.tensor_scalar(out[:, :], out[:, :], PI_BELOW, -PI_BELOW, ALU.min,
                                        ALU.max).then_inc(angle_ready, 1)

            dve.wait_ge(pos_loaded, 16)
            nc.vector.tensor_copy(ang[:, :], pos_i[:, :])
            dve.drain()
            nc.vector.tensor_scalar(ang[:, :], ang[:, :], col(consts, "inv", 0, ROPE), None, ALU.mult)
            dve.drain()
            reduce_angle(krot, 0)
            dve.drain()
            reduce_angle(turns, 1)
            dve.wait_ge(std_ready, 2)
            nc.vector.reciprocal(std[:, :, :], std[:, :, :])
            dve.drain()
            for f, (gain, i) in enumerate((("qg", 0), ("qg", 1), ("kvg", 0))):
                nc.vector.scalar_tensor_tensor(out=feats[:, f, :], in0=feats[:, f, :], scalar=col(consts, gain, i),
                                               in1=std[:, f // 2, :], op0=ALU.mult, op1=ALU.mult)
            dve.wait_ge(trig_ready, 2)
            dve.wait_ge(rot_ready, 2)
            nc.vector.tensor_tensor(krot[:, :], rot_ps[0:ROPE, :, :].rearrange("p h t -> p (h t)"), sin[:, :], ALU.mult)
            nc.vector.tensor_tensor(krope[:, :], kr[:, :], cos[:, :], ALU.mult)
            dve.drain()
            nc.vector.tensor_tensor(krope[:, :], krope[:, :], krot[:, :], ALU.add)


def mla_stage(nc, consts, feats, cos, sin, krope, mix, w_q, w_kv, gates_d):
    scale = float((P + ROPE) ** -0.5)
    fills = 5 + NT
    takes = 4 + NT
    groups = [(i + 4) // 4 for i in range(NT)]
    before = [sum(groups[:i]) for i in range(NT + 1)]
    with Stage(nc, "mla") as st:
        wq = st.sb("wq", [P, 2, P + ROPE])
        wkv = st.sb("wkv", [P, 2 * P])
        qn, kn = st.sb("qn", [P, T]), st.sb("kn", [P, T])
        qraw, qr, qrot = st.sb("qraw", [ROPE, T]), st.sb("qr", [ROPE, T]), st.sb("qrot", [ROPE, T])
        v = st.sb("v", [P, NT, P])
        pr = [st.sb(f"pr{i}", [P, T]) for i in range(2)]
        prT = [st.sb(f"prT{i}", [P, NT, P]) for i in range(2)]
        mx, rsum = st.sb("mx", [P, 2]), st.sb("rsum", [P, 2])
        x = [st.psum(f"x{i}", [P, 2, HALF]) for i in range(2)]
        pt = [st.psum(f"pt{i}", [P, 4, P]) for i in range(2)]
        po = [st.psum(f"po{i}", [P, HALF]) for i in range(2)]
        w_ready, x_full, x_taken = st.sem("w_ready"), st.sem("x_full"), st.sem("x_taken")
        rope_done, max_ready, probs_ready = st.sem("rope_done"), st.sem("max_ready"), st.sem("probs_ready")
        pt_full, pt_taken, po_full, po_taken = (st.sem("pt_full"), st.sem("pt_taken"), st.sem("po_full"),
                                                st.sem("po_taken"))
        block = st.block()

        zeros, zeros_ready, cleared = st.sb("zeros", [P, T]), st.sem("zeros_ready"), st.sem("cleared")

        def keys(i):
            return (i + 1) * P

        @block.gpsimd
        def _(pool):
            nc.gpsimd.memset(zeros[:, :], 0.0).then_inc(zeros_ready, 1)
            pool.wait_ge(zeros_ready, 1)
            with pool.Fori(0, NK) as j:
                pool.dma_start(gates_d[bass.ds(j, 1)].rearrange("a p t -> (a p) t"), zeros[:, :]).then_inc(cleared, 16)
            pool.wait_ge(cleared, 16 * NK)

        @block.sync
        def _(sp):
            sp.dma_start(wq[:, :, :], w_q[0]).then_inc(w_ready, 16)
            sp.dma_start(wkv[:, :], w_kv[0]).then_inc(w_ready, 16)
            with sp.Fori(1, MLA_HEADS) as h:
                sp.wait_ge(x_full, h * fills + (5 - fills))
                sp.dma_start(wq[:, :, :], w_q[bass.ds(h, 1)].rearrange("a p k c -> p (a k) c")).then_inc(w_ready, 16)
                sp.dma_start(wkv[:, :], w_kv[bass.ds(h, 1)].rearrange("a p c -> p (a c)")).then_inc(w_ready, 16)

        @block.tensor
        def _(pe):
            def scores(h, i):
                pe.wait_ge(x_taken, h * takes + (1 + (3 if i == 0 else 3 + i)))
                dst = x[(i + 1) % 2]
                for a in range(0, keys(i), HALF):
                    w = min(HALF, keys(i) - a)
                    nc.tensor.matmul(dst[:, a // HALF, 0:w], qn[:, i * P:(i + 1) * P], kn[:, a:a + w],
                                     start=True, stop=False)
                    last = nc.tensor.matmul(dst[:, a // HALF, 0:w], qr[:, i * P:(i + 1) * P], krope[:, a:a + w],
                                            start=False, stop=True)
                last.then_inc(x_full, 1)

            def transposes(h, i):
                pe.wait_ge(probs_ready, h * NT + (i + 1))
                for g in range(groups[i]):
                    n = before[i] + g
                    pe.wait_ge(pt_taken, h * before[NT] + (n + 1))
                    for j in range(4 * g, min(4 * g + 4, i + 1)):
                        last = nc.tensor.transpose(pt[n % 2][:, j % 4, :], pr[i % 2][:, j * P:(j + 1) * P],
                                                   consts["ident"][:, :])
                    last.then_inc(pt_full, 1)

            def weigh(h, i):
                pe.wait_ge(pt_taken, h * before[NT] + (before[i + 1] + 2))
                pe.wait_ge(po_taken, h * NT + (i + 1))
                for j in range(i + 1):
                    last = nc.tensor.matmul(po[i % 2][:, 0:P], v[:, j, :], prT[i % 2][:, j, :],
                                            start=(j == 0), stop=(j == i))
                last.then_inc(po_full, 1)

            with pe.Fori(0, MLA_HEADS) as h:
                pe.wait_ge(w_ready, h * 32 + 32)
                pe.wait_ge(x_taken, h * takes + 1)
                for kc in range(2):
                    for a in range(2):
                        last = nc.tensor.matmul(x[0][0:ROPE, a, :], wq[:, kc, P:P + ROPE],
                                                feats[:, CQ + kc, a * HALF:(a + 1) * HALF],
                                                start=(kc == 0), stop=(kc == 1))
                last.then_inc(x_full, 1)
                for kc in range(2):
                    for a in range(2):
                        last = nc.tensor.matmul(x[1][:, a, :], wq[:, kc, 0:P],
                                                feats[:, CQ + kc, a * HALF:(a + 1) * HALF],
                                                start=(kc == 0), stop=(kc == 1))
                last.then_inc(x_full, 1)
                pe.wait_ge(x_taken, h * takes + 2)
                for a in range(2):
                    last = nc.tensor.matmul(x[0][:, a, :], consts["rot"][:, :], qraw[:, a * HALF:(a + 1) * HALF],
                                            start=True, stop=True)
                last.then_inc(x_full, 1)
                pe.wait_ge(x_taken, h * takes + 3)
                for a in range(2):
                    last = nc.tensor.matmul(x[1][:, a, :], wkv[:, 0:P], feats[:, CKV, a * HALF:(a + 1) * HALF],
                                            start=True, stop=True)
                last.then_inc(x_full, 1)
                pe.wait_ge(rope_done, h + 2)
                for i in range(NT):
                    last = nc.tensor.matmul(x[0][:, i // 4, (i % 4) * P:(i % 4 + 1) * P],
                                            feats[:, CKV, i * P:(i + 1) * P], wkv[:, P:2 * P], start=True, stop=True)
                last.then_inc(x_full, 1)
                scores(h, 0)
                for i in range(NT):
                    if i + 1 < NT:
                        scores(h, i + 1)
                    transposes(h, i)
                    weigh(h, i)

        @block.scalar
        def _(act):
            def exps(h, i):
                act.wait_ge(max_ready, h * NT + (i + 1))
                nc.scalar.activation(pr[i % 2][:, 0:keys(i)],
                                     x[(i + 1) % 2][:, :, :].rearrange("p a b -> p (a b)")[:, 0:keys(i)], ACT.Exp,
                                     bias=mx[:, i % 2:i % 2 + 1], scale=scale,
                                     accum_out=rsum[:, i % 2:i % 2 + 1]).then_inc(x_taken, 1)

            nc.scalar.activation(rsum[:, 0:1], consts["ones"][:, 0:1], ACT.Copy).then_inc(x_taken, 1)
            nc.scalar.activation(rsum[:, 1:2], consts["ones"][:, 0:1], ACT.Copy).then_inc(pt_taken, 2)
            with act.Fori(0, MLA_HEADS) as h:
                act.wait_ge(x_full, h * fills + 1)
                act.wait_ge(rope_done, h + 1)
                nc.scalar.activation(qraw[:, :], x[0][0:ROPE, :, :].rearrange("p a b -> p (a b)"),
                                     ACT.Copy).then_inc(x_taken, 1)
                act.wait_ge(x_full, h * fills + 2)
                nc.scalar.activation(qn[:, :], x[1][:, :, :].rearrange("p a b -> p (a b)"),
                                     ACT.Copy).then_inc(x_taken, 1)
                act.wait_ge(x_full, h * fills + 4)
                nc.scalar.activation(kn[:, :], x[1][:, :, :].rearrange("p a b -> p (a b)"),
                                     ACT.Copy).then_inc(x_taken, 1)
                act.wait_ge(x_full, h * fills + 5)
                act.wait_ge(po_taken, h * NT + 2)
                nc.scalar.activation(v[:, :, :].rearrange("p a b -> p (a b)"),
                                     x[0][:, :, :].rearrange("p a b -> p (a b)"), ACT.Copy).then_inc(x_taken, 1)
                exps(h, 0)
                for i in range(NT):
                    if i + 1 < NT:
                        exps(h, i + 1)
                    for g in range(groups[i]):
                        n = before[i] + g
                        if i >= 2 and g == 0:
                            act.wait_ge(po_full, h * NT + (i - 1))
                        act.wait_ge(pt_full, h * before[NT] + (n + 1))
                        m = min(4, i + 1 - 4 * g)
                        nc.scalar.activation(prT[i % 2][:, 4 * g:4 * g + m, :], pt[n % 2][:, 0:m, :],
                                             ACT.Copy).then_inc(pt_taken, 1)

        @block.vector
        def _(dve):
            def maxima(h, i):
                dve.wait_ge(x_full, h * fills + (6 + i))
                s = x[(i + 1) % 2][:, :, :].rearrange("p a b -> p (a b)")
                nc.vector.memset(s[0:64, keys(i) - 64:keys(i)], -1e30)
                dve.drain()
                nc.vector.tensor_reduce(mx[:, i % 2:i % 2 + 1], s[:, 0:keys(i)], AX.X, ALU.max)
                dve.drain()
                nc.vector.tensor_scalar(mx[:, i % 2:i % 2 + 1], mx[:, i % 2:i % 2 + 1], -scale, None,
                                        ALU.mult).then_inc(max_ready, 1)

            def normalise(h, i):
                dve.wait_ge(x_taken, h * takes + (1 + 4 + i + 1))
                nc.vector.reciprocal(rsum[:, i % 2:i % 2 + 1], rsum[:, i % 2:i % 2 + 1])
                dve.drain()
                nc.vector.tensor_scalar(pr[i % 2][:, 0:keys(i)], pr[i % 2][:, 0:keys(i)], rsum[:, i % 2:i % 2 + 1],
                                        None, ALU.mult).then_inc(probs_ready, 1)

            def output(h, i):
                dve.wait_ge(po_full, h * NT + (i + 1))
                nc.vector.tensor_copy(mix[:, bass.ds(h, 1), i * P:(i + 1) * P].rearrange("p a t -> p (a t)"),
                                      po[i % 2][:, 0:P]).then_inc(po_taken, 1)

            nc.vector.memset(mx[:, 0:1], 0.0).then_inc(rope_done, 1)
            nc.vector.memset(mx[:, 1:2], 0.0).then_inc(po_taken, 2)
            dve.drain()
            with dve.Fori(0, MLA_HEADS) as h:
                dve.wait_ge(x_taken, h * takes + 2)
                nc.vector.tensor_tensor(qr[:, :], qraw[:, :], cos[:, :], ALU.mult)
                dve.wait_ge(x_full, h * fills + 3)
                nc.vector.tensor_tensor(qrot[:, :], x[0][0:ROPE, :, :].rearrange("p a b -> p (a b)"), sin[:, :],
                                        ALU.mult)
                dve.drain()
                nc.vector.tensor_tensor(qr[:, :], qr[:, :], qrot[:, :], ALU.add).then_inc(rope_done, 1)
                maxima(h, 0)
                for i in range(NT):
                    if i + 1 < NT:
                        maxima(h, i + 1)
                    normalise(h, i)
                    if i >= 1:
                        output(h, i - 1)
                output(h, NT - 1)


def rwkv_stage(nc, consts, feats_d, feats64_d, w_up_d, a_up_d, g_up_d, mix):
    decay = float(np.exp(-0.5))
    W = PAIRS * P
    with Stage(nc, "rwkv") as st:
        w_up, a_up, g_up = st.sb("w_up", [64, RW]), st.sb("a_up", [64, RW]), st.sb("g_up", [P, RW])
        rkv = st.sb("rkv", [P, 12, P])
        gd = st.sb("gd", [P, P])
        wad = st.sb("wad", [64, 2, P])

        def tile4(name, n=1):
            return st.sb(name, [P, PAIRS * n, P])

        sgw, al, gate, cum, prev, rem = (tile4(x) for x in ("sgw", "al", "gate", "cum", "prev", "rem"))
        w_t, w_inv, w_prev, w_rem = (tile4(x) for x in ("w_t", "w_inv", "w_prev", "w_rem"))
        kkr, sqk, nrm, kap, b, ta, k2 = (tile4(x) for x in ("kkr", "sqk", "nrm", "kap", "b", "ta", "k2"))
        ktrt = st.sb("ktrt", [P, PAIRS, 2, P])
        kh, bh, krm, brm, rk, bonus = (tile4(x) for x in ("kh", "bh", "krm", "brm", "rk", "bonus"))
        rhsU = st.sb("rhsU", [P, 2 * PAIRS, P])
        kr_t, br_t, v_t = (tile4(x) for x in ("kr_t", "br_t", "v_t"))
        gm = st.sb("gm", [P, 2 * PAIRS, 4, P])
        lb = [tile4(f"lb{e}") for e in range(2)]
        xi = [tile4(f"xi{e}") for e in range(2)]
        yi = [tile4(f"yi{e}") for e in range(2)]
        tmp = [tile4(f"tmp{e}") for e in range(2)]
        ll = st.sb("ll", [P, 2, 5, PAIRS, P])
        pe_s = [tile4(f"pe_s{e}") for e in range(2)]
        nu = st.sb("nu", [P, 2, 2 * PAIRS, 64])
        at, diag, es = ([tile4(f"{x}{c}") for c in range(2)] for x in ("at", "diag", "es"))
        q1 = tile4("q1")
        state = [tile4(f"state{c}") for c in range(2)]
        ysb, yc, sqy, std = (tile4(x) for x in ("ysb", "yc", "sqy", "std"))
        bank = [st.psum(f"bank{i}", [P, PAIRS, P]) for i in range(8)]

        per_tile = {}

        def sem(name, n):
            per_tile[name] = (st.sem(name), n)
            return name

        for name, n in (("loaded", 48), ("pre", 3), ("biased", 2), ("sig", 2), ("gated", 1), ("cums", 1), ("kk", 1),
                        ("sqk", 1), ("norms", 1), ("sqrt", 1), ("k2", 1), ("exps", 4), ("ktrt", 1), ("khbh", 1),
                        ("rem", 1), ("rk", 2), ("bonus_mm", 1), ("bonus", 1), ("trans", 4), ("trans_taken", 4),
                        ("gram", 8), ("masked", 8), ("lb_mm", 2), ("lb", 2), ("ux", 1), ("ux_taken", 1),
                        ("level", 10), ("inv", 12), ("p_mm", 10), ("p_taken", 10), ("z_mm", 10), ("u_mm", 2),
                        ("nu", 2), ("at_mm", 2), ("e_mm", 2), ("diag", 2), ("at", 2), ("es", 2), ("q_mm", 1),
                        ("q1", 1), ("chain", 2), ("state", 2), ("y_mm", 1), ("y", 1), ("mean", 1), ("yc", 1),
                        ("sqy", 1), ("var", 1), ("std", 1), ("done", 1)):
            sem(name, n)
        w_loaded, mixed = st.sem("w_loaded"), st.sem("mixed")
        block = st.block()

        def inc(ins, name, n=1):
            return ins.then_inc(per_tile[name][0], n)

        def flat(x):
            return x[:, :, :].rearrange("p a b -> p (a b)")

        def over_heads(c):
            return c.unsqueeze(1).broadcast_to([P, PAIRS, P])

        class Tile:
            def __init__(self, eng, t):
                self.eng, self.t = eng, t

            def wait(self, name, k):
                s, n = per_tile[name]
                self.eng.wait_ge(s, self.t * n + k)

            def begin(self):
                self.eng.wait_ge(per_tile["done"][0], self.t + 1)

        @block.sync
        def _(sp):
            sp.dma_start(w_up[:, :], w_up_d).then_inc(w_loaded, 16)
            sp.dma_start(a_up[:, :], a_up_d).then_inc(w_loaded, 16)
            sp.dma_start(g_up[:, :], g_up_d).then_inc(w_loaded, 16)
            with sp.Fori(0, NT) as t:
                Tile(sp, t).begin()
                tok = bass.ds(t * P, P)
                inc(sp.dma_start(rkv[:, :, :], feats_d[RT:GT, :, tok].rearrange("f p t -> p f t")), "loaded", 16)
                inc(sp.dma_start(gd[:, :], feats_d[GT, :, tok]), "loaded", 16)
                inc(sp.dma_start(wad[:, :, :], feats64_d[WD:AD + 1, :, tok].rearrange("f p t -> p f t")), "loaded", 16)

        @block.tensor
        def _(pe):
            pe.wait_ge(w_loaded, 48)
            with pe.Fori(0, NT) as t:
                w = Tile(pe, t)
                w.begin()

                w.wait("gated", 1)
                for f in range(PAIRS):
                    last = nc.tensor.matmul(bank[0][:, f, :], w_up[:, f * P:(f + 1) * P], wad[:, 0, :],
                                            start=True, stop=True)
                inc(last, "pre")
                for f in range(PAIRS):
                    last = nc.tensor.matmul(bank[1][:, f, :], a_up[:, f * P:(f + 1) * P], wad[:, 1, :],
                                            start=True, stop=True)
                inc(last, "pre")
                for f in range(PAIRS):
                    last = nc.tensor.matmul(bank[2][:, f, :], g_up[:, f * P:(f + 1) * P], gd[:, :],
                                            start=True, stop=True)
                inc(last, "pre")
                w.wait("biased", 2)
                w.wait("sqk", 1)
                inc(nc.tensor.matmul(flat(bank[0]), consts["headones"][:, :], flat(sqk), start=True, stop=True),
                    "norms")
                w.wait("rk", 2)
                inc(nc.tensor.matmul(flat(bank[1]), consts["headones"][:, :], flat(rk), start=True, stop=True),
                    "bonus_mm")
                for n, (src, after) in enumerate(((lambda f: ktrt[:, f, 0, :], "ktrt"), (lambda f: krm[:, f, :], "rem"),
                                                  (lambda f: brm[:, f, :], "rem"),
                                                  (lambda f: rkv[:, 8 + f, :], "rem"))):
                    w.wait(after, 1)
                    if n >= 2:
                        w.wait("trans_taken", n - 1)
                    for f in range(PAIRS):
                        last = nc.tensor.transpose(bank[6 + n % 2][:, f, :], src(f), consts["ident"][:, :])
                    inc(last, "trans")
                w.wait("khbh", 1)
                for h in range(2 * PAIRS):
                    f, rows = h // 2, slice(64 * (h % 2), 64 * (h % 2) + 64)
                    if h >= 2:
                        w.wait("masked", h - 1)
                    nc.tensor.matmul(bank[4 + h % 2][:, 0:2, :], kh[rows, f, :], ktrt[rows, f, :, :],
                                     start=True, stop=True)
                    inc(nc.tensor.matmul(bank[4 + h % 2][:, 2:4, :], bh[rows, f, :], ktrt[rows, f, :, :],
                                         start=True, stop=True), "gram")
                for e in range(2):
                    rows = slice(64 * e, 64 * e + 64)
                    w.wait("trans_taken", 3 + e)
                    for f in range(PAIRS):
                        last = nc.tensor.matmul(bank[6 + e][:, f, :], ktrt[rows, f, 0, :], bh[rows, f, :],
                                                start=True, stop=True)
                    inc(last, "lb_mm")
                w.wait("masked", 8)
                for h in range(2 * PAIRS):
                    last = nc.tensor.matmul(bank[3][:, h // 2, 64 * (h % 2):64 * (h % 2) + 64], gm[:, h, 0, :],
                                            flat(v_t)[:, h * 64:(h + 1) * 64], start=True, stop=True)
                inc(last, "ux")
                w.wait("norms", 1)
                w.wait("sqrt", 1)
                w.wait("bonus", 1)
                for l in range(1, 6):
                    for e in range(2):
                        w.wait("level", 2 * (l - 1) + e + 1)
                        w.wait("inv", 2 * (l - 1) + e + 1)
                        for f in range(PAIRS):
                            last = nc.tensor.matmul(bank[e][:, f, :], ll[:, e, l - 1, f, :], xi[e][:, f, :],
                                                    start=True, stop=True)
                        inc(last, "p_mm")
                    if l == 1:
                        w.wait("ux_taken", 1)
                    for e in range(2):
                        w.wait("p_taken", 2 * (l - 1) + e + 1)
                        for f in range(PAIRS):
                            last = nc.tensor.matmul(bank[2 + e][:, f, :], yi[e][:, f, :], pe_s[e][:, f, :],
                                                    start=True, stop=True)
                            if l < 5:
                                last = nc.tensor.matmul(bank[4 + e][:, f, :], pe_s[e][:, f, :], yi[e][:, f, :],
                                                        start=True, stop=True)
                        inc(last, "z_mm")
                for e in range(2):
                    w.wait("inv", 10 + e + 1)
                    for f in range(PAIRS):
                        last = nc.tensor.matmul(bank[e][:, f, :], xi[e][:, f, :], rhsU[:, 2 * f + e, :],
                                                start=True, stop=True)
                    inc(last, "u_mm")
                w.wait("nu", 2)
                for c in range(2):
                    rows = slice(64 * c, 64 * c + 64)
                    for f in range(PAIRS):
                        last = nc.tensor.matmul(bank[c][:, f, :], nu[rows, 0, 2 * f:2 * f + 2, :].rearrange("p h c -> p (h c)"),
                                                br_t[rows, f, :], start=True, stop=True)
                    inc(last, "at_mm")
                    for f in range(PAIRS):
                        nc.tensor.matmul(bank[2 + c][:, f, :], kr_t[rows, f, :], v_t[rows, f, :],
                                         start=True, stop=False)
                        last = nc.tensor.matmul(bank[2 + c][:, f, :], br_t[rows, f, :],
                                                nu[rows, 1, 2 * f:2 * f + 2, :].rearrange("p h c -> p (h c)"), start=False, stop=True)
                    inc(last, "e_mm")
                for h in range(2 * PAIRS):
                    f, rows = h // 2, slice(64 * (h % 2), 64 * (h % 2) + 64)
                    last = nc.tensor.matmul(bank[4][rows, f, :], nu[:, 0, h, :], gm[:, h, 3, :], start=True, stop=True)
                inc(last, "q_mm")
                for h in range(2 * PAIRS):
                    f, rows = h // 2, slice(64 * (h % 2), 64 * (h % 2) + 64)
                    nc.tensor.matmul(bank[5][rows, f, :], flat(v_t)[:, h * 64:(h + 1) * 64], gm[:, h, 1, :],
                                     start=(h < 2), stop=False, skip_group_check=True)
                    nc.tensor.matmul(bank[5][rows, f, :], nu[:, 1, h, :], gm[:, h, 3, :],
                                     start=False, stop=False, skip_group_check=True)
                w.wait("q1", 1)
                for c in range(2):
                    if c == 0:
                        pe.wait_ge(per_tile["state"][0], t * 2 + 1)
                    else:
                        w.wait("state", 2)
                    for f in range(PAIRS):
                        last = nc.tensor.matmul(bank[5][:, f, c * CH:(c + 1) * CH], state[c][:, f, :],
                                                q1[:, f, c * CH:(c + 1) * CH], start=False, stop=(c == 1),
                                                skip_group_check=True)
                    if c == 1:
                        inc(last, "y_mm")
                    w.wait("at", c + 1)
                    for f in range(PAIRS):
                        last = nc.tensor.matmul(bank[6 + c][:, f, :], at[c][:, f, :], state[c][:, f, :],
                                                start=True, stop=True)
                    inc(last, "chain")
                w.wait("y", 1)
                inc(nc.tensor.matmul(flat(bank[0]), consts["headones"][:, :], flat(ysb), start=True, stop=True), "mean")
                w.wait("sqy", 1)
                inc(nc.tensor.matmul(flat(bank[1]), consts["headones"][:, :], flat(sqy), start=True, stop=True), "var")

        @block.scalar
        def _(act):
            with act.Fori(0, NT) as t:
                w = Tile(act, t)
                w.begin()
                w.wait("loaded", 48)
                nc.scalar.activation(wad[:, 0, :], wad[:, 0, :], ACT.Tanh)
                inc(nc.scalar.activation(gd[:, :], gd[:, :], ACT.Sigmoid), "gated")
                w.wait("biased", 1)
                inc(nc.scalar.activation(flat(sgw), flat(sgw), ACT.Sigmoid), "sig")
                w.wait("biased", 2)
                inc(nc.scalar.activation(flat(al), flat(al), ACT.Sigmoid), "sig")
                w.wait("pre", 3)
                nc.scalar.activation(flat(gate), flat(bank[2]), ACT.Copy)
                w.wait("kk", 1)
                inc(nc.scalar.activation(flat(sqk), flat(kkr), ACT.Square), "sqk")
                w.wait("norms", 1)
                inc(nc.scalar.activation(flat(nrm), flat(bank[0]), ACT.Sqrt), "sqrt")
                w.wait("cums", 1)
                for out, x, sign in ((w_prev, prev, -1.0), (w_t, cum, -1.0), (w_inv, cum, 1.0), (w_rem, rem, -1.0)):
                    inc(nc.scalar.activation(flat(out), flat(x), ACT.Exp, scale=sign * decay), "exps")
                for n, dst in enumerate((rhsU[:, :, 0:64], kr_t, br_t, v_t)):
                    w.wait("trans", n + 1)
                    src = bank[6 + n % 2]
                    if n == 0:
                        last = nc.scalar.activation(dst, flat(src).rearrange("p (h c) -> p h c", c=64), ACT.Copy)
                    else:
                        last = nc.scalar.activation(flat(dst), flat(src), ACT.Copy)
                    inc(last, "trans_taken")
                w.wait("ux", 1)
                inc(nc.scalar.activation(rhsU[:, :, 64:128], flat(bank[3]).rearrange("p (h c) -> p h c", c=64),
                                         ACT.Copy), "ux_taken")
                for l in range(1, 6):
                    for e in range(2):
                        w.wait("p_mm", 2 * (l - 1) + e + 1)
                        if l >= 2:
                            w.wait("z_mm", 2 * (l - 2) + e + 1)
                        inc(nc.scalar.activation(flat(pe_s[e]), flat(bank[e]), ACT.Copy), "p_taken")
                for e in range(2):
                    w.wait("u_mm", e + 1)
                    inc(nc.scalar.activation(nu[:, :, :, :].rearrange("p w (f e) c -> p e f w c", e=2)[:, e],
                                             bank[e][:, :, :].rearrange("p f (w c) -> p f w c", w=2), ACT.Copy, scale=-1.0), "nu")
                w.wait("y_mm", 1)
                inc(nc.scalar.activation(flat(ysb), flat(bank[5]), ACT.Copy), "y")
                w.wait("yc", 1)
                inc(nc.scalar.activation(flat(sqy), flat(yc), ACT.Square), "sqy")
                w.wait("var", 1)
                inc(nc.scalar.activation(flat(std), flat(bank[1]), ACT.Sqrt, bias=consts["eps"][:, 1:2],
                                         scale=1.0 / CH), "std")

        @block.gpsimd
        def _(pool):
            with pool.Fori(0, NT) as t:
                w = Tile(pool, t)
                w.begin()
                w.wait("loaded", 48)
                inc(nc.gpsimd.tensor_tensor(kkr[:, :, :], rkv[:, 4:8, :], cols_over(consts, "kk", PAIRS, P), ALU.mult),
                    "kk")
                w.wait("k2", 1)
                inc(nc.gpsimd.tensor_tensor(rk[:, :, :], rkv[:, 0:4, :], k2[:, :, :], ALU.mult), "rk")
                w.wait("rk", 1)
                inc(nc.gpsimd.tensor_tensor(rk[:, :, :], rk[:, :, :], cols_over(consts, "rk", PAIRS, P), ALU.mult),
                    "rk")
                w.wait("exps", 4)
                for c in range(2):
                    end = w_t[:, :, c * CH + CH - 1:c * CH + CH].broadcast_to([P, PAIRS, P])
                    inc(nc.gpsimd.tensor_tensor(diag[c][:, :, :], over_heads(consts["ident"][:, :]), end, ALU.mult),
                        "diag")
                for l in range(1, 6):
                    for e in range(2):
                        if l == 1:
                            w.wait("lb", e + 1)
                        inc(nc.gpsimd.tensor_tensor(ll[:, e, l - 1, :, :], lb[e][:, :, :],
                                                    over_heads(consts["level"][:, l, :]), ALU.mult), "level")

        @block.vector
        def _(dve):
            inc(nc.vector.memset(flat(state[0]), 0.0), "state")
            inc(nc.vector.memset(flat(state[1]), 0.0), "done")
            with dve.Fori(0, NT) as t:
                w = Tile(dve, t)
                w.wait("pre", 1)
                nc.vector.tensor_tensor(sgw[:, :, :], bank[0][:, :, :], cols_over(consts, "w0", PAIRS, P),
                                        ALU.add).then_inc(per_tile["biased"][0], 1)
                w.wait("pre", 2)
                inc(nc.vector.tensor_tensor(al[:, :, :], bank[1][:, :, :], cols_over(consts, "a0", PAIRS, P), ALU.add),
                    "biased")
                w.wait("sig", 1)
                nc.vector.tensor_tensor_scan(flat(cum), consts["scanmask"][:, :], flat(sgw), 0.0, ALU.mult, ALU.add)
                dve.drain()
                nc.vector.tensor_tensor(flat(prev), flat(cum), flat(sgw), ALU.subtract)
                chunks = flat(cum).rearrange("p (c t) -> p c t", t=CH)
                inc(nc.vector.tensor_tensor(flat(rem).rearrange("p (c t) -> p c t", t=CH),
                                            chunks[:, :, CH - 1:CH].broadcast_to([P, 2 * PAIRS, CH]), chunks,
                                            ALU.subtract), "cums")
                w.wait("sig", 2)
                nc.vector.scalar_tensor_tensor(out=ta[:, :, :], in0=al[:, :, :], scalar=-1.0,
                                               in1=cols_over(consts, "ka", PAIRS, P), op0=ALU.add, op1=ALU.mult)
                dve.drain()
                inc(nc.vector.scalar_tensor_tensor(out=k2[:, :, :], in0=ta[:, :, :], scalar=1.0, in1=rkv[:, 4:8, :],
                                                   op0=ALU.add, op1=ALU.mult), "k2")
                w.wait("sqrt", 1)
                nc.vector.tensor_scalar(flat(nrm), flat(nrm), 1e-12, None, ALU.max)
                dve.drain()
                nc.vector.reciprocal(flat(nrm), flat(nrm))
                dve.drain()
                nc.vector.tensor_tensor(flat(kap), flat(kkr), flat(nrm), ALU.mult)
                dve.drain()
                nc.vector.tensor_tensor(flat(b), flat(kap), flat(al), ALU.mult)
                w.wait("exps", 2)
                nc.vector.tensor_tensor(ktrt[:, :, 0, :], kap[:, :, :], w_prev[:, :, :], ALU.mult)
                inc(nc.vector.tensor_tensor(ktrt[:, :, 1, :], rkv[:, 0:4, :], w_t[:, :, :], ALU.mult), "ktrt")
                dve.drain()
                w.wait("exps", 4)
                nc.vector.tensor_tensor(flat(kh), flat(k2), flat(w_inv), ALU.mult)
                inc(nc.vector.tensor_tensor(flat(bh), flat(b), flat(w_inv), ALU.mult), "khbh")
                nc.vector.tensor_tensor(flat(krm), flat(k2), flat(w_rem), ALU.mult)
                inc(nc.vector.tensor_tensor(flat(brm), flat(b), flat(w_rem), ALU.mult), "rem")
                w.wait("bonus_mm", 1)
                inc(nc.vector.tensor_tensor(bonus[:, :, :], bank[1][:, :, :], rkv[:, 8:12, :], ALU.mult), "bonus")
                for h in range(2 * PAIRS):
                    w.wait("gram", h + 1)
                    inc(nc.vector.tensor_tensor(gm[:, h, :, :], bank[4 + h % 2][:, :, :], consts["mask4"][:, :, :],
                                                ALU.mult), "masked")
                for e in range(2):
                    w.wait("lb_mm", e + 1)
                    inc(nc.vector.tensor_tensor(lb[e][:, :, :], bank[6 + e][:, :, :], over_heads(consts["lower"][:, :]),
                                                ALU.mult), "lb")
                dve.drain()
                gv = gm[:, :, :, :].rearrange("p (f e) w c -> p f e w c", e=2)
                for e in range(2):
                    nc.vector.tensor_tensor(tmp[0][:, :, :], gv[:, :, e, 2, :], over_heads(consts["upper0"][:, :]),
                                            ALU.mult)
                    nc.vector.tensor_tensor(tmp[1][:, :, :], lb[e][:, :, :], over_heads(consts["level"][:, 0, :]),
                                            ALU.mult)
                    dve.drain()
                    nc.vector.scalar_tensor_tensor(out=xi[e][:, :, :], in0=tmp[0][:, :, :], scalar=-1.0,
                                                   in1=over_heads(consts["ident"][:, :]), op0=ALU.mult, op1=ALU.add)
                    inc(nc.vector.scalar_tensor_tensor(out=yi[e][:, :, :], in0=tmp[1][:, :, :], scalar=-1.0,
                                                       in1=over_heads(consts["ident"][:, :]), op0=ALU.mult,
                                                       op1=ALU.add), "inv")
                    dve.drain()
                for l in range(1, 6):
                    for e in range(2):
                        w.wait("z_mm", 2 * (l - 1) + e + 1)
                        last = nc.vector.tensor_tensor(flat(xi[e]), flat(xi[e]), flat(bank[2 + e]), ALU.subtract)
                        if l < 5:
                            last = nc.vector.tensor_tensor(flat(yi[e]), flat(yi[e]), flat(bank[4 + e]), ALU.subtract)
                        inc(last, "inv")
                    dve.drain()
                for c in range(2):
                    w.wait("at_mm", c + 1)
                    nc.vector.tensor_tensor(at[c][:, :, :], bank[c][:, :, :], over_heads(consts["headones"][:, :]),
                                            ALU.mult)
                    w.wait("e_mm", c + 1)
                    nc.vector.tensor_tensor(es[c][:, :, :], bank[2 + c][:, :, :], over_heads(consts["headones"][:, :]),
                                            ALU.mult)
                    dve.drain()
                    w.wait("diag", c + 1)
                    inc(nc.vector.tensor_tensor(flat(at[c]), flat(at[c]), flat(diag[c]), ALU.add), "at")
                w.wait("q_mm", 1)
                inc(nc.vector.tensor_tensor(q1[:, :, :], bank[4][:, :, :], ktrt[:, :, 1, :], ALU.add), "q1")
                for c in range(2):
                    w.wait("chain", c + 1)
                    inc(nc.vector.tensor_tensor(flat(state[1 - c]), flat(bank[6 + c]), flat(es[c]), ALU.add), "state")
                w.wait("mean", 1)
                w.wait("y", 1)
                inc(nc.vector.scalar_tensor_tensor(out=flat(yc), in0=flat(bank[0]), scalar=-1.0 / CH, in1=flat(ysb),
                                                   op0=ALU.mult, op1=ALU.add), "yc")
                w.wait("std", 1)
                nc.vector.reciprocal(flat(std), flat(std))
                dve.drain()
                nc.vector.tensor_tensor(flat(yc), flat(yc), flat(std), ALU.mult)
                dve.drain()
                nc.vector.tensor_tensor(yc[:, :, :], yc[:, :, :], cols_over(consts, "lnw", PAIRS, P), ALU.mult)
                dve.drain()
                nc.vector.tensor_tensor(yc[:, :, :], yc[:, :, :], cols_over(consts, "lnb", PAIRS, P), ALU.add)
                dve.drain()
                nc.vector.tensor_tensor(flat(yc), flat(yc), flat(bonus), ALU.add)
                dve.drain()
                inc(nc.vector.tensor_tensor(mix[:, 4:8, bass.ds(t * P, P)], yc[:, :, :], gate[:, :, :], ALU.mult),
                    "done")


def residual_stage(nc, name, weights, acts, src, dst, load=None):
    with Stage(nc, name) as st:
        w = [st.sb(f"w{i}", [P, KC, P]) for i in range(2)]
        ps = [st.psum(f"ps{i}", [P, 2, HALF]) for i in range(2)]
        w_ready = [st.sem(f"w_ready{i}") for i in range(2)]
        loaded, mm_done, added = st.sem("loaded"), st.sem("mm_done"), st.sem("added")
        block = st.block()

        @block.sync
        def _(sp):
            for i in range(2):
                sp.dma_start(w[i][:, :, :], weights[i]).then_inc(w_ready[i], 16)
            with sp.Fori(1, KC // 2) as g:
                for i in range(2):
                    sp.wait_ge(mm_done, g * 2 + (i - 1))
                    sp.dma_start(w[i][:, :, :], weights[bass.ds(g * 2 + i, 1)].rearrange(
                        "a p k c -> p (a k) c")).then_inc(w_ready[i], 16)

        @block.scalar
        def _(act):
            if load is not None:
                act.dma_start(src[:, :, :], load.rearrange("k p t -> p k t")).then_inc(loaded, 16)

        @block.tensor
        def _(pe):
            with pe.Fori(0, KC // 2) as g:
                for i in range(2):
                    pe.wait_ge(w_ready[i], g * 16 + 16)
                    pe.wait_ge(added, g * 2 + (i + 1))
                    for kc in range(KC):
                        for h in range(2):
                            last = nc.tensor.matmul(ps[i][:, h, :], w[i][:, kc, :],
                                                    acts[:, kc, h * HALF:(h + 1) * HALF],
                                                    start=(kc == 0), stop=(kc == KC - 1))
                    last.then_inc(mm_done, 1)

        @block.vector
        def _(dve):
            dve.nop().then_inc(added, 2)
            if load is not None:
                dve.wait_ge(loaded, 16)
            with dve.Fori(0, KC // 2) as g:
                for i in range(2):
                    dve.wait_ge(mm_done, g * 2 + (i + 1))
                    tile = bass.ds(g * 2 + i, 1)
                    nc.vector.tensor_tensor(dst[:, tile, :].rearrange("p a t -> p (a t)"),
                                            src[:, tile, :].rearrange("p a t -> p (a t)"), ps[i][:, :, :].rearrange("p a t -> p (a t)"),
                                            ALU.add).then_inc(added, 1)


def cross_attention_stage(nc, consts, acts, memn, oT, w_q, w_k, w_v):
    hd = D // XH
    scale = float(hd ** -0.5)
    fills = 6
    with Stage(nc, "xa") as st:
        wq, wk, wv = (st.sb(x, [P, KC, hd]) for x in ("wq", "wk", "wv"))
        q, k, v = st.sb("q", [P, 2, T]), st.sb("k", [P, 2, MEM]), st.sb("v", [P, 2, hd])
        pr = [st.sb(f"pr{i}", [P, 4, MEM]) for i in range(2)]
        prT = st.sb("prT", [P, 2, HALF])
        mx, rsum = st.sb("mx", [P, 2, 4]), st.sb("rsum", [P, 2, 4])
        x = [st.psum(f"x{i}", [P, 2, HALF]) for i in range(2)]
        pt = [st.psum(f"pt{i}", [P, 4, P]) for i in range(2)]
        po = [st.psum(f"po{i}", [P, HALF]) for i in range(2)]
        wq_ready, wk_ready, wv_ready = st.sem("wq_ready"), st.sem("wk_ready"), st.sem("wv_ready")
        x_full, x_taken = st.sem("x_full"), st.sem("x_taken")
        max_ready, probs_ready = st.sem("max_ready"), st.sem("probs_ready")
        pt_full, pt_taken, po_full, po_taken = (st.sem("pt_full"), st.sem("pt_taken"), st.sem("po_full"),
                                                st.sem("po_taken"))
        block = st.block()

        def flat(b):
            return b[:, :, :].rearrange("p a t -> p (a t)")

        @block.sync
        def _(sp):
            loads = ((wq, w_q, wq_ready, 2), (wk, w_k, wk_ready, 3), (wv, w_v, wv_ready, 4))
            for buf, src, ready, _n in loads:
                sp.dma_start(buf[:, :, :], src[0]).then_inc(ready, 16)
            with sp.Fori(1, XH) as h:
                for buf, src, ready, n in loads:
                    sp.wait_ge(x_full, h * fills + (n - fills))
                    sp.dma_start(buf[:, :, :], src[bass.ds(h, 1)].rearrange("a p k c -> p (a k) c")).then_inc(ready, 16)

        @block.tensor
        def _(pe):
            with pe.Fori(0, XH) as h:
                pe.wait_ge(wq_ready, h * 16 + 16)
                for a in range(2):
                    pe.wait_ge(x_taken, h * fills + (a + 1))
                    for kc in range(KC):
                        for s in range(2):
                            last = nc.tensor.matmul(x[a][:, s, :], wq[:, kc, a * P:(a + 1) * P],
                                                    acts[:, kc, s * HALF:(s + 1) * HALF],
                                                    start=(kc == 0), stop=(kc == KC - 1))
                    last.then_inc(x_full, 1)
                pe.wait_ge(wk_ready, h * 16 + 16)
                pe.wait_ge(x_taken, h * fills + 3)
                for a in range(2):
                    for kc in range(KC):
                        last = nc.tensor.matmul(x[0][:, 0, a * MEM:(a + 1) * MEM], wk[:, kc, a * P:(a + 1) * P],
                                                memn[:, kc, :], start=(kc == 0), stop=(kc == KC - 1))
                last.then_inc(x_full, 1)
                pe.wait_ge(wv_ready, h * 16 + 16)
                pe.wait_ge(x_taken, h * fills + 4)
                for m in range(2):
                    for kc in range(KC):
                        last = nc.tensor.matmul(x[1][:, 0, m * hd:(m + 1) * hd], memn[:, kc, m * P:(m + 1) * P],
                                                wv[:, kc, :], start=(kc == 0), stop=(kc == KC - 1))
                last.then_inc(x_full, 1)
                pe.wait_ge(x_taken, h * fills + 6)
                for s in range(2):
                    for i in range(4):
                        for a in range(2):
                            last = nc.tensor.matmul(flat(x[s])[:, i * MEM:(i + 1) * MEM],
                                                    q[:, a, (4 * s + i) * P:(4 * s + i + 1) * P], k[:, a, :],
                                                    start=(a == 0), stop=(a == 1))
                    last.then_inc(x_full, 1)
                for s in range(2):
                    pe.wait_ge(probs_ready, h * 2 + (s + 1))
                    for m in range(2):
                        pe.wait_ge(pt_taken, h * 4 + (2 * s + m + 1))
                        for i in range(4):
                            last = nc.tensor.transpose(pt[m][:, i, :], pr[s][:, i, m * P:(m + 1) * P],
                                                       consts["ident"][:, :])
                        last.then_inc(pt_full, 1)
                    pe.wait_ge(pt_taken, h * 4 + (2 * s + 4))
                    for a in range(2):
                        pe.wait_ge(po_taken, h * 4 + (2 * s + a + 1))
                        for m in range(2):
                            last = nc.tensor.matmul(po[a][:, :], v[:, m, a * P:(a + 1) * P], prT[:, m, :],
                                                    start=(m == 0), stop=(m == 1))
                        last.then_inc(po_full, 1)

        @block.scalar
        def _(act):
            act.nop().then_inc(x_taken, 2)
            act.nop().then_inc(pt_taken, 2)
            with act.Fori(0, XH) as h:
                for a in range(2):
                    act.wait_ge(x_full, h * fills + (a + 1))
                    nc.scalar.activation(q[:, a, :], flat(x[a]), ACT.Copy).then_inc(x_taken, 1)
                act.wait_ge(x_full, h * fills + 3)
                nc.scalar.activation(flat(k), x[0][:, 0, :], ACT.Copy).then_inc(x_taken, 1)
                act.wait_ge(x_full, h * fills + 4)
                act.wait_ge(po_taken, h * 4 + 2)
                nc.scalar.activation(flat(v), x[1][:, 0, :], ACT.Copy).then_inc(x_taken, 1)
                for s in range(2):
                    act.wait_ge(max_ready, h * 2 + (s + 1))
                    for i in range(4):
                        last = nc.scalar.activation(pr[s][:, i, :], flat(x[s])[:, i * MEM:(i + 1) * MEM], ACT.Exp,
                                                    bias=mx[:, s, i:i + 1], scale=scale, accum_out=rsum[:, s, i:i + 1])
                    last.then_inc(x_taken, 1)
                for s in range(2):
                    for m in range(2):
                        act.wait_ge(pt_full, h * 4 + (2 * s + m + 1))
                        act.wait_ge(po_taken, h * 4 + (2 * s + 2))
                        nc.scalar.activation(prT[:, m, :], flat(pt[m]), ACT.Copy).then_inc(pt_taken, 1)

        @block.vector
        def _(dve):
            dve.nop().then_inc(po_taken, 2)
            with dve.Fori(0, XH) as h:
                for s in range(2):
                    dve.drain()
                    dve.wait_ge(x_full, h * fills + (5 + s))
                    nc.vector.tensor_reduce(mx[:, s, :], flat(x[s]).rearrange("p (i m) -> p i m", m=MEM), AX.X, ALU.max)
                    dve.drain()
                    nc.vector.tensor_scalar(mx[:, s, :], mx[:, s, :], -scale, None, ALU.mult).then_inc(max_ready, 1)
                for s in range(2):
                    dve.wait_ge(x_taken, h * fills + (7 + s))
                    nc.vector.reciprocal(rsum[:, s, :], rsum[:, s, :])
                    dve.drain()
                    nc.vector.tensor_tensor(pr[s][:, :, :], pr[s][:, :, :],
                                            rsum[:, s, :].unsqueeze(2).broadcast_to([P, 4, MEM]),
                                            ALU.mult).then_inc(probs_ready, 1)
                for s in range(2):
                    for a in range(2):
                        dve.wait_ge(po_full, h * 4 + (2 * s + a + 1))
                        nc.vector.tensor_copy(oT[:, bass.ds(h * 2 + a, 1), s * HALF:(s + 1) * HALF].rearrange(
                            "p a t -> p (a t)"), po[a][:, :]).then_inc(po_taken, 1)


def expert_scores_stage(nc, consts, acts, w_query, keys_d, scores_d):
    n_tiles = 2 * PH
    with Stage(nc, "score") as st:
        w = [st.sb(f"w{i}", [P, KC, P]) for i in range(2)]
        keys = st.sb("keys", [P, n_tiles, NK])
        q = [st.sb(f"q{i}", [P, T]) for i in range(2)]
        s = [st.sb(f"s{i}", [P, NT, NK]) for i in range(2)]
        ps = [st.psum(f"ps{i}", [P, 2, HALF]) for i in range(2)]
        ss = [st.psum(f"ss{i}", [P, NT, NK]) for i in range(2)]
        w_ready = [st.sem(f"w_ready{i}") for i in range(2)]
        stored = [st.sem(f"stored{i}") for i in range(2)]
        by_head = scores_d.rearrange("(h t) p w k -> h p w t k", h=PH)
        keys_ready, q_mm, q_ready, s_mm, s_ready = (st.sem(x) for x in ("keys_ready", "q_mm", "q_ready", "s_mm",
                                                                       "s_ready"))
        block = st.block()

        @block.sync
        def _(sp):
            for i in range(2):
                sp.dma_start(w[i][:, :, :], w_query[i]).then_inc(w_ready[i], 16)
            sp.dma_start(keys[:, :, :], keys_d).then_inc(keys_ready, 16)
            with sp.Fori(1, n_tiles // 2) as g:
                for i in range(2):
                    sp.wait_ge(q_mm, g * 2 + (i - 1))
                    sp.dma_start(w[i][:, :, :], w_query[bass.ds(g * 2 + i, 1)].rearrange(
                        "a p k c -> p (a k) c")).then_inc(w_ready[i], 16)
                    sp.wait_ge(s_ready, g * 2 + (i + 1))
                    sp.dma_start(by_head[bass.ds(g - 1, 1), :, i].rearrange("h p t k -> (h p) t k"),
                                 s[i][:, :, :]).then_inc(stored[i], 16)
            for i in range(2):
                sp.wait_ge(s_ready, n_tiles + i + 1)
                sp.dma_start(by_head[PH - 1, :, i], s[i][:, :, :]).then_inc(stored[i], 16)
                sp.wait_ge(stored[i], 16 * (PH + 1))

        @block.tensor
        def _(pe):
            pe.wait_ge(keys_ready, 16)
            with pe.Fori(0, n_tiles // 2) as g:
                for i in range(2):
                    pe.wait_ge(w_ready[i], g * 16 + 16)
                    pe.wait_ge(q_ready, g * 2 + (i + 1))
                    for kc in range(KC):
                        for h in range(2):
                            last = nc.tensor.matmul(ps[i][:, h, :], w[i][:, kc, :],
                                                    acts[:, kc, h * HALF:(h + 1) * HALF],
                                                    start=(kc == 0), stop=(kc == KC - 1))
                    last.then_inc(q_mm, 1)
                    pe.wait_ge(q_ready, g * 2 + (i + 3))
                    pe.wait_ge(s_ready, g * 2 + (i + 1))
                    for t in range(NT):
                        last = nc.tensor.matmul(ss[i][:, t, :], q[i][:, t * P:(t + 1) * P],
                                                keys[:, bass.ds(g * 2 + i, 1), :].rearrange("p a k -> p (a k)"),
                                                start=True, stop=True)
                    last.then_inc(s_mm, 1)

        @block.scalar
        def _(act):
            act.nop().then_inc(q_ready, 2)
            with act.Fori(0, n_tiles // 2) as g:
                for i in range(2):
                    act.wait_ge(q_mm, g * 2 + (i + 1))
                    act.wait_ge(s_ready, g * 2 + (i + 1))
                    nc.scalar.activation(q[i][:, :], ps[i][:, :, :].rearrange("p a t -> p (a t)"),
                                         ACT.Copy).then_inc(q_ready, 1)

        @block.vector
        def _(dve):
            dve.nop().then_inc(s_ready, 2)
            for i in range(2):
                dve.nop().then_inc(stored[i], 16)
            with dve.Fori(0, n_tiles // 2) as g:
                for i in range(2):
                    dve.wait_ge(s_mm, g * 2 + (i + 1))
                    dve.wait_ge(stored[i], g * 16 + 16)
                    nc.vector.tensor_copy(s[i][:, :, :].rearrange("p a t -> p (a t)"),
                                          ss[i][:, :, :].rearrange("p a t -> p (a t)")).then_inc(s_ready, 1)

def split_stage(nc, src, high, low):
    with Stage(nc, "split") as st:
        rounded = st.sem("rounded")
        block = st.block()

        @block.scalar
        def _(act):
            for kc in range(KC):
                nc.scalar.activation(high[:, kc, :], src[:, kc, :], ACT.Copy).then_inc(rounded, 1)

        @block.vector
        def _(dve):
            for kc in range(KC):
                dve.wait_ge(rounded, kc + 1)
                nc.vector.tensor_tensor(low[:, kc, :], src[:, kc, :], high[:, kc, :].bitcast(F32), ALU.subtract)


def experts_in_stage(nc, consts, high, low, expert_u, scores_d, hidden_d, gates_d):
    LOW = -3.0e38
    heads = NT * PH
    with Stage(nc, "xin") as st:
        raw = [st.sb(f"raw{i}", [P, KC * P]) for i in range(2)]
        uh = [st.sb(f"uh{i}", [P, KC * P], F32R) for i in range(2)]
        ul = [st.sb(f"ul{i}", [P, KC * P], F32R) for i in range(2)]
        hid = [st.sb(f"hid{i}", [P, T]) for i in range(2)]
        ps = [st.psum(f"ps{i}", [P, 2, HALF]) for i in range(2)]
        sc, scw = st.sb("sc", [P, 2, NK]), st.sb("scw", [P, 2, NK])
        vals, ix, ixf = st.sb("vals", [P, 2, TOPK]), st.sb("ix", [P, 2, TOPK], U32), st.sb("ixf", [P, 2, TOPK])
        cand, candw, cv = st.sb("cand", [P, TOPK, TOPK]), st.sb("candw", [P, TOPK * TOPK]), st.sb("cv", [P, TOPK])
        ci, place, placef = st.sb("ci", [P, TOPK], U32), st.sb("place", [P, 2, TOPK], U32), st.sb("placef", [P, 2, TOPK])
        sel, e12, flat_e = st.sb("sel", [P, 2, TOPK, TOPK]), st.sb("e12", [P, 2, TOPK]), st.sb("flat_e", [P, TOPK])
        iota_i, iota = st.sb("iota_i", [P, TOPK], I32), st.sb("iota", [P, TOPK])
        tok_i, tok, wrap = st.sb("tok_i", [P, 1], I32), st.sb("tok", [P, 1]), st.sb("wrap", [P, 1])
        idx, gates = st.sb("idx", [P, TOPK], U32), st.sb("gates", [P, TOPK])
        gexp, nmax, gsum = st.sb("gexp", [P, TOPK]), st.sb("nmax", [P, 1]), st.sb("gsum", [P, 1])
        raw_ready = [st.sem(f"raw_ready{i}") for i in range(2)]
        stored = [st.sem(f"stored{i}") for i in range(2)]
        high_done, low_done, mm_done, gelu_done = (st.sem(x) for x in ("high_done", "low_done", "mm_done", "gelu_done"))
        sc_ready, sc_used, cv_ready, gate_exp = (st.sem(x) for x in ("sc_ready", "sc_used", "cv_ready", "gate_exp"))
        idx_ready, added, iota_ready = st.sem("idx_ready"), st.sem("added"), st.sem("iota_ready")
        block = st.block()
        gates_flat = gates_d.rearrange("j i t -> (j i t)").unsqueeze(1)

        @block.sync
        def _(sp):
            for i in range(2):
                sp.dma_start(raw[i][:, :], expert_u[i]).then_inc(raw_ready[i], 16)
            sp.dma_start(sc[:, :, :], scores_d[0]).then_inc(sc_ready, 16)
            with sp.Fori(1, NK // 2) as g:
                for i in range(2):
                    sp.wait_ge(low_done, g * 2 + (i - 1))
                    sp.dma_start(raw[i][:, :], expert_u[bass.ds(g * 2 + i, 1)].rearrange("a p n -> (a p) n")
                                 ).then_inc(raw_ready[i], 16)
                    if i == 0:
                        sp.wait_ge(sc_used, g)
                        sp.dma_start(sc[:, :, :], scores_d[bass.ds(g, 1)].rearrange("a p w k -> (a p) w k")
                                     ).then_inc(sc_ready, 16)
                    sp.wait_ge(gelu_done, g * 2 + (i + 1))
                    sp.dma_start(hidden_d[bass.ds(g * 2 + (i - 2), 1)].rearrange("a p t -> (a p) t"), hid[i][:, :]
                                 ).then_inc(stored[i], 16)
            for i in range(2):
                sp.wait_ge(gelu_done, NK + 1 + i)
                sp.dma_start(hidden_d[NK - 2 + i], hid[i][:, :]).then_inc(stored[i], 16)
                sp.wait_ge(stored[i], 16 * (NK // 2 + 1))

        @block.tensor
        def _(pe):
            with pe.Fori(0, NK // 2) as g:
                for i in range(2):
                    pe.wait_ge(low_done, g * 2 + (i + 1))
                    pe.wait_ge(gelu_done, g * 2 + (i + 1))
                    for kc in range(KC):
                        cols = slice(kc * P, kc * P + P)
                        for w, x in ((uh[i], high), (uh[i], low), (ul[i], high)):
                            for h in range(2):
                                last = nc.tensor.matmul(ps[i][:, h, :], w[:, cols], x[:, kc, h * HALF:(h + 1) * HALF],
                                                        start=(kc == 0 and w is uh[i] and x is high),
                                                        stop=(kc == KC - 1 and w is ul[i]))
                    last.then_inc(mm_done, 1)

        @block.scalar
        def _(act):
            def high_part(i, k):
                act.wait_ge(raw_ready[i], k)
                nc.scalar.activation(uh[i][:, :], raw[i][:, :], ACT.Copy).then_inc(high_done, 1)

            def gelu(i, done, free):
                act.wait_ge(mm_done, done)
                act.wait_ge(stored[i], free)
                nc.scalar.activation(hid[i][:, :], ps[i][:, :, :].rearrange("p a t -> p (a t)"),
                                     ACT.Gelu).then_inc(gelu_done, 1)

            def gate(k):
                act.wait_ge(cv_ready, k)
                nc.scalar.activation(gexp[:, :], cv[:, :], ACT.Exp, bias=nmax[:, :],
                                     accum_out=gsum[:, :]).then_inc(gate_exp, 1)

            high_part(0, 16)
            high_part(1, 16)
            gate(1)
            with act.Fori(1, NK // 2) as g:
                for i in range(2):
                    gelu(i, g * 2 + (i - 1), g * 16)
                    high_part(i, g * 16 + 16)
                gate(g + 1)
            for i in range(2):
                gelu(i, NK - 1 + i, 16 * (NK // 2))

        @block.gpsimd
        def _(pool):
            nc.gpsimd.iota(iota_i[:, :], [[1, TOPK]], base=0, channel_multiplier=0).then_inc(iota_ready, 1)
            nc.gpsimd.iota(tok_i[:, :], [[1, 1]], base=0, channel_multiplier=1).then_inc(iota_ready, 1)
            found = pool.alloc_register("found")
            with pool.Fori(0, heads) as n:
                pool.reg_mov(found, n + 1)
                pool.wait_ge(iota_ready, 1)
                pool.wait_ge(idx_ready, found)
                for k in range(TOPK):
                    if k:
                        pool.wait_ge(iota_ready, 1)
                    pool.indirect_dma_start(gates_flat, bass.IndirectOffsetOnAxis(ap=idx[:, k:k + 1], axis=0),
                                            gates[:, k:k + 1], None, compute_op=ALU.add).then_inc(added, 16)
            pool.wait_ge(added, 16 * TOPK * heads)

        @block.vector
        def _(dve):
            def low_part(i, k):
                dve.wait_ge(high_done, k)
                nc.vector.tensor_tensor(ul[i][:, :], raw[i][:, :], uh[i][:, :].bitcast(F32),
                                        ALU.subtract).then_inc(low_done, 1)

            def search(k, first=False):
                dve.drain()
                dve.wait_ge(sc_ready, k * 16)
                nc.vector.memset(wrap[:, :], 0.0)
                dve.drain()
                for w in range(2):
                    nc.vector.max(vals[:, w, 0:8], sc[:, w, :])
                dve.drain()
                for w in range(2):
                    nc.vector.max_index(ix[:, w, 0:8], vals[:, w, 0:8], sc[:, w, :])
                    last = nc.vector.match_replace(scw[:, w, :], vals[:, w, 0:8], sc[:, w, :], LOW)
                last.then_inc(sc_used, 1)
                dve.drain()
                for w in range(2):
                    nc.vector.max(vals[:, w, 8:16], scw[:, w, :])
                dve.drain()
                for w in range(2):
                    nc.vector.max_index(ix[:, w, 8:16], vals[:, w, 8:16], scw[:, w, :])
                nc.vector.tensor_tensor(cand[:, :, :], vals[:, 0, :].unsqueeze(2).broadcast_to([P, TOPK, TOPK]),
                                        vals[:, 1, :].unsqueeze(1).broadcast_to([P, TOPK, TOPK]), ALU.add)
                dve.drain()
                flat = cand[:, :, :].rearrange("p a b -> p (a b)")
                nc.vector.max(cv[:, 0:8], flat)
                nc.vector.tensor_copy(ixf[:, :, :], ix[:, :, :])
                dve.drain()
                nc.vector.tensor_scalar(nmax[:, :], cv[:, 0:1], -1.0, None, ALU.mult)
                nc.vector.max_index(ci[:, 0:8], cv[:, 0:8], flat)
                nc.vector.match_replace(candw[:, :], cv[:, 0:8], flat, LOW)
                dve.drain()
                nc.vector.max(cv[:, 8:16], candw[:, :]).then_inc(cv_ready, 1)
                dve.drain()
                nc.vector.max_index(ci[:, 8:16], cv[:, 8:16], candw[:, :])
                dve.drain()
                nc.vector.tensor_scalar(place[:, 0, :], ci[:, :], 4, None, ALU.logical_shift_right)
                nc.vector.tensor_scalar(place[:, 1, :], ci[:, :], 15, None, ALU.bitwise_and)
                dve.drain()
                nc.vector.tensor_copy(placef[:, :, :], place[:, :, :])
                dve.drain()
                nc.vector.tensor_tensor(sel[:, :, :, :], placef[:, :, :].unsqueeze(3).broadcast_to([P, 2, TOPK, TOPK]),
                                        iota[:, :].unsqueeze(1).unsqueeze(1).broadcast_to([P, 2, TOPK, TOPK]),
                                        ALU.is_equal)
                dve.drain()
                nc.vector.tensor_tensor(sel[:, :, :, :], sel[:, :, :, :],
                                        ixf[:, :, :].unsqueeze(2).broadcast_to([P, 2, TOPK, TOPK]), ALU.mult)
                dve.drain()
                nc.vector.tensor_reduce(e12[:, :, :], sel[:, :, :, :], AX.X, ALU.add)
                dve.drain()
                nc.vector.scalar_tensor_tensor(out=flat_e[:, :], in0=e12[:, 1, :], scalar=float(NK), in1=e12[:, 0, :],
                                               op0=ALU.mult, op1=ALU.add)
                dve.wait_ge(gate_exp, k)
                nc.vector.reciprocal(gsum[:, :], gsum[:, :])
                dve.drain()
                if not first:
                    dve.wait_ge(added, (k - 1) * (16 * TOPK))
                nc.vector.tensor_scalar(gates[:, :], gexp[:, :], gsum[:, :], None, ALU.mult)
                nc.vector.tensor_scalar(idx[:, :], flat_e[:, :], float(T), tok[:, :], ALU.mult,
                                        ALU.add).then_inc(idx_ready, 1)
                dve.drain()
                nc.vector.tensor_scalar(tok[:, :], tok[:, :], float(P), None, ALU.add)
                dve.drain()
                nc.vector.tensor_scalar(wrap[:, :], tok[:, :], float(T), -float(T), ALU.is_ge, ALU.mult)
                dve.drain()
                nc.vector.tensor_tensor(tok[:, :], tok[:, :], wrap[:, :], ALU.add)

            dve.wait_ge(iota_ready, 2)
            nc.vector.tensor_copy(iota[:, :], iota_i[:, :])
            nc.vector.tensor_copy(tok[:, :], tok_i[:, :])
            dve.nop().then_inc(gelu_done, 2)
            for i in range(2):
                dve.nop().then_inc(stored[i], 16)
            low_part(0, 1)
            low_part(1, 2)
            search(1, first=True)
            with dve.Fori(1, NK // 2) as g:
                low_part(0, g * 2 + 1)
                low_part(1, g * 2 + 2)
                search(g + 1)


def experts_out_stage(nc, hT, expert_v, hidden_d, gates_d):
    G = 4
    groups = NK // G
    with Stage(nc, "xout") as st:
        hid = [st.sb(f"hid{i}", [P, T]) for i in range(2)]
        gat = [st.sb(f"gat{i}", [P, T]) for i in range(2)]
        val = [st.sb(f"val{i}", [P, D]) for i in range(2)]
        ah, al, vh, vl = (st.sb(x, [P, 2 * G, T], F32R) for x in ("ah", "al", "vh", "vl"))
        ps = [st.psum(f"ps{i}", [P, 2, HALF]) for i in range(4)]
        in_ready = [st.sem(f"in_ready{i}") for i in range(2)]
        product, act_high, val_high, split_done = (st.sem(x) for x in ("product", "act_high", "val_high", "split_done"))
        group_done, pair_done, added = st.sem("group_done"), st.sem("pair_done"), st.sem("added")
        block = st.block()

        def each_group(eng, body):
            with eng.Fori(0, groups // 2 - 1) as gg:
                body(gg * 2, 0, True)
                body(gg * 2 + 1, 1, True)
            body(groups - 2, 0, True)
            body(groups - 1, 1, False)

        @block.sync
        def _(sp):
            def load(c, r, index):
                sp.dma_start(val[r][:, :], index(expert_v)).then_inc(in_ready[r], 16)
                sp.dma_start(hid[r][:, :], index(hidden_d)).then_inc(in_ready[r], 16)
                sp.dma_start(gat[r][:, :], index(gates_d)).then_inc(in_ready[r], 16)

            for c in range(2):
                load(c, c, lambda x: x[c])
            with sp.Fori(1, NK // 2) as cc:
                for r in range(2):
                    sp.wait_ge(split_done, cc * 2 + (r - 1))
                    load(cc * 2 + r, r, lambda x: x[bass.ds(cc * 2 + r, 1)].rearrange("a p t -> (a p) t"))

        @block.tensor
        def _(pe):
            def group(g, parity, more):
                pe.wait_ge(split_done, g * G + G)
                for f in range(KC):
                    out = ps[f % 4]
                    pe.wait_ge(added, g * KC + (f + 1))
                    for s in range(G):
                        n = parity * G + s
                        for w, x in ((vh, ah), (vh, al), (vl, ah)):
                            for h in range(2):
                                last = nc.tensor.matmul(out[:, h, :], w[:, n, f * P:(f + 1) * P],
                                                        x[:, n, h * HALF:(h + 1) * HALF],
                                                        start=(s == 0 and w is vh and x is ah),
                                                        stop=(s == G - 1 and w is vl))
                    last.then_inc(pair_done, 1)

            each_group(pe, group)

        @block.scalar
        def _(act):
            def highs(c, n):
                act.wait_ge(in_ready[n % 2], (c - n % 2) * 24 + 48)
                nc.scalar.activation(vh[:, n, :], val[n % 2][:, :], ACT.Copy).then_inc(val_high, 1)
                act.wait_ge(product, c + 1)
                nc.scalar.activation(ah[:, n, :], hid[n % 2][:, :], ACT.Copy).then_inc(act_high, 1)

            for s in range(G):
                highs(s, s)

            def group(g, parity, more):
                if not more:
                    return
                act.wait_ge(added, g * KC + 4)
                for s in range(G):
                    highs(g * G + (G + s), (1 - parity) * G + s)

            each_group(act, group)

        @block.vector
        def _(dve):
            def multiply(c, r):
                dve.wait_ge(in_ready[r], (c - r) * 24 + 48)
                nc.vector.tensor_tensor(hid[r][:, :], hid[r][:, :], gat[r][:, :], ALU.mult).then_inc(product, 1)

            def lows(c, n):
                dve.wait_ge(val_high, c + 1)
                nc.vector.tensor_tensor(vl[:, n, :], val[n % 2][:, :], vh[:, n, :].bitcast(F32), ALU.subtract)
                dve.wait_ge(act_high, c + 1)
                nc.vector.tensor_tensor(al[:, n, :], hid[n % 2][:, :], ah[:, n, :].bitcast(F32),
                                        ALU.subtract).then_inc(split_done, 1)

            dve.nop().then_inc(added, 4)
            for s in range(G):
                multiply(s, s % 2)
                dve.drain()
                lows(s, s)

            def group(g, parity, more):
                for f in range(KC):
                    if more and f % 2 == 0:
                        multiply(g * G + (G + f // 2), (f // 2) % 2)
                    dve.drain()
                    dve.wait_ge(pair_done, g * KC + (f + 1))
                    nc.vector.tensor_tensor(hT[:, f, :], hT[:, f, :], ps[f % 4][:, :, :].rearrange("p a t -> p (a t)"),
                                            ALU.add).then_inc(added, 1)
                    if more and f % 2 == 0:
                        lows(g * G + (G + f // 2), (1 - parity) * G + f // 2)

            each_group(dve, group)


def store_stage(nc, src, out):
    with Stage(nc, "store") as st:
        stored = st.sem("stored")
        block = st.block()

        @block.sync
        def _(sp):
            sp.dma_start(out.rearrange("(k p) t -> p k t", p=P), src[:, :, :]).then_inc(stored, 16)
            sp.wait_ge(stored, 16)


def build(nc, a, out):
    with ExitStack() as ctx:
        def sb(name, shape, dt=F32):
            return ctx.enter_context(nc.sbuf_tensor(name, shape, dt))

        consts = {"cols": sb("cols", [P, NCOLS]), "ones": sb("ones", [P, P]), "eps": sb("eps", [P, 2]),
                  "ident": sb("ident", [P, P]), "headones": sb("headones", [P, P]), "rot": sb("rot", [ROPE, P]),
                  "mask4": sb("mask4", [P, 4, P]), "level": sb("level", [P, 6, P]), "lower": sb("lower", [P, P]),
                  "upper0": sb("upper0", [P, P]), "scanmask": sb("scanmask", [P, 4 * P])}
        feats_d = nc.dram_tensor("feats_d", (NF, P, T), F32).ap()
        feats64_d = nc.dram_tensor("feats64_d", (3, 64, T), F32).ap()
        scores_d = nc.dram_tensor("scores_d", (NT * PH, P, 2, NK), F32).ap()
        hidden_d = nc.dram_tensor("hidden_d", (NK, P, T), F32).ap()
        gates_d = nc.dram_tensor("gates_d", (NK, P, T), F32).ap()
        build_constants(nc, consts, a["cols"])
        lower = sb("act_lower", [P, KC, T])
        with ExitStack() as front:
            xT = front.enter_context(nc.sbuf_tensor("xT", [P, KC, T], F32))
            norm_stage(nc, consts, "nmix", xT, "mix", lower, T, load=a["x"])
            project_in_stage(nc, consts, lower, a["w_in"], a["w_in64"], feats_d, feats64_d)
        with ExitStack() as mla:
            feats = mla.enter_context(nc.sbuf_tensor("feats", [P, 3, T], F32))
            cos = mla.enter_context(nc.sbuf_tensor("cos", [ROPE, T], F32))
            sin = mla.enter_context(nc.sbuf_tensor("sin", [ROPE, T], F32))
            krope = mla.enter_context(nc.sbuf_tensor("krope", [ROPE, T], F32))
            mla_prepare_stage(nc, consts, feats, feats_d, feats64_d, a["positions"], cos, sin, krope)
            mla_stage(nc, consts, feats, cos, sin, krope, lower, a["w_uq"], a["w_ukv"], gates_d)
        rwkv_stage(nc, consts, feats_d, feats64_d, a["rw_w_up"], a["rw_a_up"], a["rw_g_up"], lower)
        with ExitStack() as late:
            upper = late.enter_context(nc.sbuf_tensor("act_upper", [P, KC, T], F32))
            residual_stage(nc, "out", a["w_out"], lower, upper, upper, load=a["x"])
            with ExitStack() as cross:
                memn = cross.enter_context(nc.sbuf_tensor("memn", [P, KC, MEM], F32))
                oT = cross.enter_context(nc.sbuf_tensor("oT", [P, KC, T], F32))
                norm_stage(nc, consts, "nmem", memn, "mem", memn, MEM, load=a["mem"])
                norm_stage(nc, consts, "nxa", upper, "xa", lower, T)
                cross_attention_stage(nc, consts, lower, memn, oT, a["xa_wq"], a["xa_wk"], a["xa_wv"])
                residual_stage(nc, "xo", a["xa_wo"], oT, upper, lower)
            norm_stage(nc, consts, "nffn", lower, "ffn", upper, T)
            expert_scores_stage(nc, consts, upper, a["peer_wq"], a["peer_keys"], scores_d)
            with ExitStack() as deep:
                high = deep.enter_context(nc.sbuf_tensor("high", [P, KC, T], F32R))
                low = deep.enter_context(nc.sbuf_tensor("low", [P, KC, T], F32R))
                split_stage(nc, upper, high, low)
                experts_in_stage(nc, consts, high, low, a["expert_u"], scores_d, hidden_d, gates_d)
        experts_out_stage(nc, lower, a["expert_v"], hidden_d, gates_d)
        with ExitStack() as last:
            normed = last.enter_context(nc.sbuf_tensor("normed_out", [P, KC, T], F32))
            norm_stage(nc, consts, "nfin", lower, "fin", normed, T)
            store_stage(nc, normed, out)


def layout(inputs):
    def blocks(w, n):
        k = w.shape[0] // P
        return np.ascontiguousarray(w.reshape(k, P, w.shape[1] // n, n).transpose(2, 1, 0, 3))

    def vec(name, rows=P):
        return np.asarray(inputs[name]).reshape(-1, rows).T

    a = {k: np.asarray(v) for k, v in inputs.items()}
    w_in = a["w_in"][0]
    m = Q_LORA + KV_LORA
    r = m + ROPE
    out = {"x": np.ascontiguousarray(a["x"][0].T).reshape(KC, P, T)}
    out["positions"] = a["positions"]
    out["w_in"] = blocks(np.concatenate([w_in[:, 0:m], w_in[:, r:r + 3 * RW], w_in[:, r + 3 * RW + 128:]], 1), P)
    out["w_in64"] = blocks(np.concatenate([w_in[:, m:r], w_in[:, r + 3 * RW:r + 3 * RW + 128]], 1), 64)
    cols = np.zeros((P, NCOLS), np.float32)

    def put(name, part):
        cols[0:part.shape[0], COLS[name]:COLS[name] + part.shape[1]] = part

    for name, key in (("mix", "norm_mix_g"), ("xa", "norm_xa_g"), ("mem", "norm_mem_g"), ("ffn", "norm_ffn_g"),
                      ("w0", "rw_w0"), ("a0", "rw_a0"), ("kk", "rw_k_k"), ("ka", "rw_k_a"), ("rk", "rw_r_k"),
                      ("lnw", "rw_lnx_w"), ("lnb", "rw_lnx_b"), ("qg", "q_norm_g"), ("kvg", "kv_norm_g"),
                      ("fin", "final_norm_g")):
        put(name, vec(key))
    mu = a["shift_mu"][0]
    cols[:, COLS["mu"] + RT:COLS["mu"] + GT] = mu[0:3 * RW].reshape(-1, P).T
    cols[:, COLS["mu"] + GT] = mu[3 * RW + 128:]
    cols[0:64, COLS["mu64"] + WD] = mu[3 * RW:3 * RW + 64]
    cols[0:64, COLS["mu64"] + AD] = mu[3 * RW + 64:3 * RW + 128]
    half = np.float32(10000.0) ** (-np.arange(0, ROPE, 2, dtype=np.float32) / np.float32(ROPE))
    cols[0:ROPE, COLS["inv"]] = np.concatenate([half, half])
    out["cols"] = cols
    out["w_uq"] = blocks(a["w_uq"][0], P + ROPE)
    out["w_ukv"] = np.ascontiguousarray(a["w_ukv"][0].reshape(P, MLA_HEADS, 2 * P).transpose(1, 0, 2))
    for name in ("rw_w_up", "rw_a_up", "rw_g_up"):
        out[name] = a[name][0]
    out["w_out"], out["xa_wo"], out["peer_wq"] = (blocks(a[x][0], P) for x in ("w_out", "xa_wo", "peer_wq"))
    out["xa_wq"], out["xa_wk"], out["xa_wv"] = (blocks(a[x][0], D // XH) for x in ("xa_wq", "xa_wk", "xa_wv"))
    out["mem"] = np.ascontiguousarray(a["mem"][0].T).reshape(KC, P, MEM)
    out["peer_keys"] = np.ascontiguousarray(a["peer_keys"][0].reshape(2 * PH, NK, P).transpose(2, 0, 1))
    out["expert_u"] = np.ascontiguousarray(a["expert_u"][0].reshape(NK, NK, KC, P).transpose(1, 3, 2, 0)).reshape(
        NK, P, KC * P)
    out["expert_v"] = np.ascontiguousarray(a["expert_v"][0].reshape(NK, NK, D).transpose(1, 0, 2))
    return out


def kernel(**inputs):
    import concourse.bacc as bacc
    from concourse.bass_utils import run_bass_kernel_spmd

    nc = bacc.Bacc("TRN2", target_bir_lowering=False, num_devices=1)
    arrays, aps = {}, {}
    for name, arr in layout(inputs).items():
        arrays[f"in_{name}"] = arr
        aps[name] = nc.dram_tensor(f"in_{name}", arr.shape, mybir.dt.from_np(arr.dtype), kind="ExternalInput").ap()
    out = nc.dram_tensor("out_0", (T, D), F32, kind="ExternalOutput").ap()
    build(nc, aps, out)
    r = run_bass_kernel_spmd(nc, [arrays], core_ids=[0])
    return np.ascontiguousarray(r.results[0]["out_0"].T).reshape(1, T, D)
```

```python
from contextlib import ExitStack

import concourse.bass as bass
import numpy as np
from concourse import mybir

F32 = mybir.dt.float32
F32R = mybir.dt.float32r
I32 = mybir.dt.int32
U32 = mybir.dt.uint32
ALU = mybir.AluOpType
ACT = mybir.ActivationFunctionType
AX = mybir.AxisListType

P = 128
D = 1024
T = 1024
KC = D // P
NT = T // P
HALF = 512
EPS = 1e-6

MLA_HEADS = 4
ROPE = 64
Q_LORA = 256
KV_LORA = 128
RW = 512
PAIRS = 4
CH = 64
LNX_EPS = 64e-5
MEM = 256
XH = 4
PH = 8
NK = 128
TOPK = 16

CQ, CKV, RT, KT, VT, GT, KRWD, AD, NF = 0, 2, 3, 7, 11, 15, 16, 17, 18

COLS = {}
_at = 0
for _name, _n in (("mix", 8), ("xa", 8), ("mem", 8), ("ffn", 8), ("w0", 4), ("a0", 4), ("kk", 4), ("ka", 4),
                  ("rk", 4), ("lnw", 4), ("lnb", 4), ("qg", 2), ("kvg", 1), ("mu", NF),
                  ("inv", 1), ("fin", 8)):
    COLS[_name] = _at
    _at += _n
NCOLS = _at




class Stage:

    def __init__(self, nc, name):
        self.nc, self.name, self.stack, self.sems = nc, name, ExitStack(), []

    def __enter__(self):
        return self

    def __exit__(self, *e):
        done = self.stack.__exit__(*e)
        if e[0] is None:
            self.nc.clear_and_free_semaphores(self.sems)
            self.nc.all_engine_barrier()
        return done

    def sb(self, name, shape, dt=F32):
        return self.stack.enter_context(self.nc.sbuf_tensor(f"{self.name}_{name}", shape, dt))

    def psum(self, name, shape, dt=F32):
        return self.stack.enter_context(self.nc.psum_tensor(f"{self.name}_{name}", shape, dt))

    def sem(self, name):
        self.sems.append(self.nc.alloc_semaphore(f"{self.name}_{name}"))
        return self.sems[-1]

    def block(self):
        return self.stack.enter_context(self.nc.Block())


def col(consts, name, i=0, rows=P):
    c = COLS[name] + i
    return consts["cols"][0:rows, c:c + 1]


def cols_over(consts, name, n, width):
    c = COLS[name]
    return consts["cols"][:, c:c + n].unsqueeze(2).broadcast_to([P, n, width])


def build_constants(nc, consts, cols_d):
    with Stage(nc, "const") as st:
        loaded, made = st.sem("loaded"), st.sem("made")
        block = st.block()

        @block.sync
        def _(sp):
            sp.dma_start(consts["cols"][:, :], cols_d).then_inc(loaded, 16)
            sp.wait_ge(loaded, 16)

        @block.gpsimd
        def _(pool):
            nc.gpsimd.memset(consts["ones"][:, :], 1.0)
            nc.gpsimd.memset(consts["eps"][:, 0:1], EPS)
            nc.gpsimd.memset(consts["eps"][:, 1:2], LNX_EPS).then_inc(made, 1)
            nc.gpsimd.memset(consts["ident"][:, :], 0.0).then_inc(made, 1)
            pool.wait_ge(made, 2)
            nc.gpsimd.affine_select(out=consts["ident"][:, :], in_=consts["ident"][:, :], compare_op=ALU.not_equal,
                                    fill=1.0, base=0, pattern=[[-1, P]], channel_multiplier=1).then_inc(made, 1)
            bd = consts["headones"]
            nc.gpsimd.memset(bd[:, :], 1.0).then_inc(made, 1)
            pool.wait_ge(made, 4)
            nc.gpsimd.memset(bd[0:64, 64:128], 0.0).then_inc(made, 1)
            nc.gpsimd.memset(bd[64:128, 0:64], 0.0).then_inc(made, 1)
            rot = consts["rot"]
            nc.gpsimd.memset(rot[:, :], 0.0).then_inc(made, 1)
            pool.wait_ge(made, 7)
            nc.gpsimd.affine_select(out=rot[:, 0:32], in_=rot[:, 0:32], compare_op=ALU.not_equal, fill=-1.0,
                                    base=-32, pattern=[[-1, 32]], channel_multiplier=1)
            nc.gpsimd.affine_select(out=rot[:, 32:64], in_=rot[:, 32:64], compare_op=ALU.not_equal, fill=1.0,
                                    base=0, pattern=[[-1, 32]], channel_multiplier=1).then_inc(made, 1)
            m4 = consts["mask4"]
            nc.gpsimd.memset(m4[:, :, :], 1.0).then_inc(made, 1)
            lv = consts["level"]
            nc.gpsimd.memset(lv[:, :, :], 1.0).then_inc(made, 1)
            low = consts["lower"]
            nc.gpsimd.memset(low[:, :], 1.0).then_inc(made, 1)
            up0 = consts["upper0"]
            nc.gpsimd.memset(up0[:, :], 0.0).then_inc(made, 1)
            n = 12
            for i in range(4):
                pool.wait_ge(made, n)
                nc.gpsimd.affine_select(out=m4[:, i, :], in_=m4[:, i, :], compare_op=ALU.is_ge, fill=0.0,
                                        base=-1 if i % 2 == 0 else 0, pattern=[[1, P]],
                                        channel_multiplier=-1).then_inc(made, 1)
                n += 1
                pool.wait_ge(made, n)
                nc.gpsimd.memset(m4[0:64, i, 64:128], 0.0).then_inc(made, 1)
                n += 1
            nc.gpsimd.affine_select(out=low[:, :], in_=low[:, :], compare_op=ALU.is_ge, fill=0.0, base=-1,
                                    pattern=[[-1, P]], channel_multiplier=1).then_inc(made, 1)
            n += 1
            pool.wait_ge(made, n)
            nc.gpsimd.memset(low[64:128, 0:64], 0.0).then_inc(made, 1)
            n += 1
            pool.wait_ge(made, n)
            for l in range(6):
                b = 1 << l
                v = lv[:, l, :].rearrange("p (j y) -> p j y", y=2 * b)
                nc.gpsimd.memset(v[:, :, b:2 * b], 0.0).then_inc(made, 1)
                n += 1
                pool.wait_ge(made, n)
                nc.gpsimd.affine_select(out=v[:, :, 0:b], in_=v[:, :, 0:b], compare_op=ALU.is_ge, fill=0.0,
                                        base=-b, pattern=[[-2 * b, P // (2 * b)], [0, b]],
                                        channel_multiplier=1).then_inc(made, 1)
                n += 1
                pool.wait_ge(made, n)
                nc.gpsimd.affine_select(out=v[:, :, 0:b], in_=v[:, :, 0:b], compare_op=ALU.is_ge, fill=0.0,
                                        base=2 * b - 1, pattern=[[2 * b, P // (2 * b)], [0, b]],
                                        channel_multiplier=-1).then_inc(made, 1)
                n += 1
                pool.wait_ge(made, n)
            v = up0[:, :].rearrange("p (j y) -> p j y", y=2)[:, :, 1]
            nc.gpsimd.affine_select(out=v, in_=v, compare_op=ALU.not_equal, fill=1.0, base=0,
                                    pattern=[[-2, 64]], channel_multiplier=1).then_inc(made, 1)
            sm = consts["scanmask"]
            nc.gpsimd.memset(sm[:, :], 1.0).then_inc(made, 1)
            n += 2
            pool.wait_ge(made, n)
            nc.gpsimd.memset(sm[:, :].rearrange("p (c t) -> p c t", t=CH)[:, :, 0:1], 0.0).then_inc(made, 1)


def norm_stage(nc, consts, name, src, gain, dst, width, load=None):
    halves = [(a, min(HALF, width - a)) for a in range(0, width, HALF)]
    with Stage(nc, name) as st:
        sq = st.sb("sq", [P, 2, width])
        std = st.sb("std", [P, width])
        sums = [st.psum(f"sums{i}", [P, HALF]) for i in range(len(halves))]
        loaded, sq_ready, sq_used = st.sem("loaded"), st.sem("sq_ready"), st.sem("sq_used")
        std_ready, rstd_ready = st.sem("std_ready"), st.sem("rstd_ready")
        block = st.block()

        @block.sync
        def _(sp):
            if load is not None:
                for kc in range(KC):
                    sp.dma_start(src[:, kc, :], load[kc]).then_inc(loaded, 16)

        @block.scalar
        def _(act):
            for kc in range(KC):
                if load is not None:
                    act.wait_ge(loaded, 16 * KC)
                if kc >= 2:
                    act.wait_ge(sq_used, kc - 1)
                nc.scalar.activation(sq[:, kc % 2, :], src[:, kc, :], ACT.Square).then_inc(sq_ready, 1)
            act.wait_ge(sq_used, KC)
            for i, (a, w) in enumerate(halves):
                nc.scalar.activation(std[:, a:a + w], sums[i][:, 0:w], ACT.Sqrt, bias=consts["eps"][:, 0:1],
                                     scale=1.0 / D).then_inc(std_ready, 1)

        @block.tensor
        def _(pe):
            for kc in range(KC):
                pe.wait_ge(sq_ready, kc + 1)
                for i, (a, w) in enumerate(halves):
                    last = nc.tensor.matmul(sums[i][:, 0:w], consts["ones"][:, :], sq[:, kc % 2, a:a + w],
                                            start=(kc == 0), stop=(kc == KC - 1))
                last.then_inc(sq_used, 1)

        @block.vector
        def _(dve):
            if load is not None:
                dve.wait_ge(loaded, 16 * KC)
            dve.wait_ge(std_ready, len(halves))
            nc.vector.reciprocal(std[:, :], std[:, :]).then_inc(rstd_ready, 1)
            dve.wait_ge(rstd_ready, 1)
            for kc in range(KC):
                nc.vector.scalar_tensor_tensor(out=dst[:, kc, :], in0=src[:, kc, :], scalar=col(consts, gain, kc),
                                               in1=std[:, :], op0=ALU.mult, op1=ALU.mult)


class SplitInput:

    def __init__(self, nc, st, consts, src, gain=None, high=None, low=None, rstd=None):
        self.nc, self.consts, self.src, self.gain = nc, consts, src, gain
        self.high = st.sb("high", [P, KC, T], F32R) if high is None else high
        self.low = st.sb("low", [P, KC, T], F32R) if low is None else low
        self.high_ready, self.low_ready = st.sem("high_ready"), st.sem("low_ready")
        if gain:
            self.scaled, self.sq = st.sb("scaled", [P, 2, T]), st.sb("sq", [P, 2, T])
            self.rstd = st.sb("rstd", [P, T]) if rstd is None else rstd
            self.sums = st.psum("sums", [P, 2, HALF])
            self.scaled_ready, self.sq_ready, self.sq_summed = (st.sem(x) for x in ("scaled_ready", "sq_ready",
                                                                                   "sq_summed"))
            self.std_ready, self.rstd_ready = st.sem("std_ready"), st.sem("rstd_ready")

    def part(self, kc):
        return self.scaled[:, kc % 2, :] if self.gain else self.src[:, kc, :]

    def highs(self, act, loaded=None):
        for kc in range(KC):
            if self.gain:
                act.wait_ge(self.scaled_ready, kc + 1)
            elif loaded is not None and kc == 0:
                act.wait_ge(loaded, 16)
            self.nc.scalar.activation(self.high[:, kc, :], self.part(kc), ACT.Copy).then_inc(self.high_ready, 1)

    def std(self, act):
        act.wait_ge(self.sq_summed, KC)
        self.nc.scalar.activation(self.rstd[:, :], self.sums[:, :, :].rearrange("p a t -> p (a t)"), ACT.Sqrt,
                                  bias=self.consts["eps"][:, 0:1], scale=1.0 / D).then_inc(self.std_ready, 1)

    def squares(self, pool, loaded=None):
        for kc in range(KC):
            if loaded is not None:
                pool.wait_ge(loaded[kc], 16)
            if kc >= 2:
                pool.wait_ge(self.sq_summed, kc - 1)
            self.nc.gpsimd.tensor_tensor(self.sq[:, kc % 2, :], self.src[:, kc, :], self.src[:, kc, :],
                                         ALU.mult).then_inc(self.sq_ready, 1)

    def sum_squares(self, pe, kc):
        pe.wait_ge(self.sq_ready, kc + 1)
        for h in range(2):
            last = self.nc.tensor.matmul(self.sums[:, h, :], self.consts["ones"][:, :],
                                         self.sq[:, kc % 2, h * HALF:(h + 1) * HALF],
                                         start=(kc == 0), stop=(kc == KC - 1))
        last.then_inc(self.sq_summed, 1)

    def lows(self, dve, loaded=None):
        for kc in range(KC + 1 if self.gain else KC):
            if self.gain and kc < KC:
                if loaded is not None:
                    dve.wait_ge(loaded[kc], 16)
                if kc >= 2:
                    dve.wait_ge(self.high_ready, kc - 1)
                    dve.drain()
                self.nc.vector.tensor_scalar(self.scaled[:, kc % 2, :], self.src[:, kc, :],
                                             col(self.consts, self.gain, kc), None,
                                             ALU.mult).then_inc(self.scaled_ready, 1)
            k = kc - 1 if self.gain else kc
            if k >= 0:
                dve.wait_ge(self.high_ready, k + 1)
                if self.gain:
                    dve.wait_ge(self.scaled_ready, k + 1)
                self.nc.vector.tensor_tensor(self.low[:, k, :], self.part(k), self.high[:, k, :].bitcast(F32),
                                             ALU.subtract).then_inc(self.low_ready, 1)

    def invert(self, dve):
        dve.wait_ge(self.std_ready, 1)
        self.nc.vector.reciprocal(self.rstd[:, :], self.rstd[:, :]).then_inc(self.rstd_ready, 1)
        dve.wait_ge(self.rstd_ready, 1)


class Projection:

    def __init__(self, nc, st, weights, n_tiles, x):
        self.nc, self.weights, self.n, self.x = nc, weights, n_tiles, x
        self.raw = [st.sb(f"raw{i}", [P, KC * P]) for i in range(2)]
        self.wh = [st.sb(f"wh{i}", [P, KC * P], F32R) for i in range(2)]
        self.wl = [st.sb(f"wl{i}", [P, KC * P], F32R) for i in range(2)]
        self.ps = [st.psum(f"ps{i}", [P, 2, HALF]) for i in range(2)]
        self.w_ready = [st.sem(f"w_ready{i}") for i in range(2)]
        self.w_high, self.w_low, self.mm_done, self.taken = (st.sem(x) for x in ("w_high", "w_low", "mm_done",
                                                                                "taken"))

    def product(self, i):
        return self.ps[i][:, :, :].rearrange("p a t -> p (a t)")

    def first_loads(self, sp):
        for i in range(2):
            sp.dma_start(self.raw[i][:, :], self.weights[i]).then_inc(self.w_ready[i], 16)

    def loads(self, sp, store=None):
        with sp.Fori(1, self.n // 2) as g:
            for i in range(2):
                sp.wait_ge(self.w_low, g * 2 + (i - 1))
                sp.dma_start(self.raw[i][:, :], self.weights[bass.ds(g * 2 + i, 1)].rearrange("a p n -> (a p) n")
                             ).then_inc(self.w_ready[i], 16)
                if store:
                    store(i, g * 2 + (i - 2))

    def high(self, act, i, k):
        act.wait_ge(self.w_ready[i], k)
        self.nc.scalar.activation(self.wh[i][:, :], self.raw[i][:, :], ACT.Copy).then_inc(self.w_high, 1)

    def low(self, dve, i, tile):
        dve.wait_ge(self.w_high, tile + 1)
        self.nc.vector.tensor_tensor(self.wl[i][:, :], self.raw[i][:, :], self.wh[i][:, :].bitcast(F32),
                                     ALU.subtract).then_inc(self.w_low, 1)

    def first_highs(self, act):
        self.high(act, 0, 16)
        self.x.highs(act)
        self.high(act, 1, 16)
        if self.x.gain:
            self.x.std(act)

    def highs(self, act, after=None):
        with act.Fori(1, self.n // 2) as g:
            for i in range(2):
                act.wait_ge(self.mm_done, g * 2 + (i - 1))
                self.high(act, i, g * 16 + 16)
                if after:
                    after(i, g * 2 + i)

    def first_lows(self, dve, loaded=None):
        dve.nop().then_inc(self.taken, 2)
        self.low(dve, 0, 0)
        self.x.lows(dve, loaded)
        self.low(dve, 1, 1)
        if self.x.gain:
            self.x.invert(dve)

    def takes(self, dve, take):
        with dve.Fori(0, self.n // 2 - 1) as g:
            for i in range(2):
                dve.drain()
                dve.wait_ge(self.mm_done, g * 2 + (i + 1))
                take(i, g * 2 + i)
                self.low(dve, i, g * 2 + (i + 2))
        for i in range(2):
            dve.drain()
            dve.wait_ge(self.mm_done, self.n - 1 + i)
            take(i, self.n - 2 + i)

    def products(self, pe, after=None):
        def tile(i, first):
            for kc in range(KC):
                if first:
                    pe.wait_ge(self.x.low_ready, kc + 1)
                cols = slice(kc * P, kc * P + P)
                for w, x in ((self.wh[i], self.x.high), (self.wh[i], self.x.low), (self.wl[i], self.x.high)):
                    for h in range(2):
                        last = self.nc.tensor.matmul(self.ps[i][:, h, :], w[:, cols],
                                                     x[:, kc, h * HALF:(h + 1) * HALF],
                                                     start=(kc == 0 and w is self.wh[i] and x is self.x.high),
                                                     stop=(kc == KC - 1 and w is self.wl[i]))
                if first and self.x.gain:
                    self.x.sum_squares(pe, kc)
            last.then_inc(self.mm_done, 1)

        for i in range(2):
            pe.wait_ge(self.w_low, i + 1)
            tile(i, i == 0)
            if i and after:
                after(0, 0)
        with pe.Fori(1, self.n // 2) as g:
            for i in range(2):
                pe.wait_ge(self.w_low, g * 2 + (i + 1))
                pe.wait_ge(self.taken, g * 2 + (i + 1))
                tile(i, False)
                if after:
                    after(1 - i, g * 2 + (i - 1))


def project_in_stage(nc, consts, x_d, xT, weights, feats_d):
    with Stage(nc, "pin") as st:
        x = SplitInput(nc, st, consts, xT, "mix")
        proj = Projection(nc, st, weights, NF, x)
        raw = [st.sb(f"out{i}", [P, T + 1]) for i in range(2)]
        shifted = [st.sb(f"shifted{i}", [P, T]) for i in range(2)]
        diff, mu_tile = st.sb("diff", [P, T]), st.sb("mu", [P, 2])
        stored, loaded = [st.sem(f"stored{i}") for i in range(2)], [st.sem(f"loaded{kc}") for kc in range(KC)]
        shift_done = st.sem("shift_done")
        block = st.block()

        @block.sync
        def _(sp):
            proj.first_loads(sp)
            for kc in range(KC):
                sp.dma_start(xT[:, kc, :], x_d[kc]).then_inc(loaded[kc], 16)

            def store(i, tile):
                sp.wait_ge(shift_done, tile + 1)
                sp.dma_start(feats_d[bass.ds(tile, 1)].rearrange("a p t -> (a p) t"),
                             shifted[i][:, :]).then_inc(stored[i], 16)

            proj.loads(sp, store)
            for i in range(2):
                sp.wait_ge(shift_done, NF - 1 + i)
                sp.dma_start(feats_d[NF - 2 + i], shifted[i][:, :]).then_inc(stored[i], 16)
                sp.wait_ge(stored[i], 16 * (NF // 2 + 1))

        @block.gpsimd
        def _(pool):
            x.squares(pool, loaded)

        @block.tensor
        def _(pe):
            proj.products(pe)

        @block.scalar
        def _(act):
            proj.first_highs(act)
            proj.highs(act)

        @block.vector
        def _(dve):
            for i in range(2):
                nc.vector.memset(raw[i][:, 0:1], 0.0)
                nc.vector.memset(mu_tile[:, i:i + 1], 0.0).then_inc(stored[i], 16)
            proj.first_lows(dve, loaded)
            mu0 = COLS["mu"]

            def take(i, tile):
                nc.vector.tensor_tensor(raw[i][:, 1:T + 1], proj.product(i), x.rstd[:, :], ALU.mult
                                        ).then_inc(proj.taken, 1)
                at = bass.ds(tile + mu0, 1) if not isinstance(tile, int) else slice(tile + mu0, tile + mu0 + 1)
                nc.vector.tensor_copy(mu_tile[:, i:i + 1], consts["cols"][:, at])
                dve.drain()
                nc.vector.tensor_tensor(diff[:, :], raw[i][:, 0:T], raw[i][:, 1:T + 1], ALU.subtract)
                dve.drain()
                dve.wait_ge(stored[i], (tile - i) * 8 + 16)
                nc.vector.scalar_tensor_tensor(out=shifted[i][:, :], in0=diff[:, :], scalar=mu_tile[:, i:i + 1],
                                               in1=raw[i][:, 1:T + 1], op0=ALU.mult, op1=ALU.add
                                               ).then_inc(shift_done, 1)

            proj.takes(dve, take)


TWO_PI = 2.0 * np.pi
TWO_PI_A = 6.28125
TWO_PI_B = float(np.float32(round((TWO_PI - TWO_PI_A) * 2 ** 21) / 2 ** 21))
TWO_PI_C = float(TWO_PI - TWO_PI_A - TWO_PI_B)
ROUNDER = 12582912.0
PI_BELOW = 3.1415925


def mla_prepare_stage(nc, consts, feats, feats_d, positions, cos, sin, krope):
    with Stage(nc, "mprep") as st:
        sq = st.sb("sq", [P, 3, T])
        std = st.sb("std", [P, 2, T])
        pos_i = st.sb("pos_i", [ROPE, T], I32)
        ang = st.sb("ang", [ROPE, T])
        turns = st.sb("turns", [ROPE, T])
        krot = st.sb("krot", [ROPE, T])
        kr = st.sb("kr", [ROPE, T])
        sums = st.psum("sums", [P, 4, HALF])
        rot_ps = st.psum("rot_ps", [P, 2, HALF])
        loaded, sq_ready, sums_ready = st.sem("loaded"), st.sem("sq_ready"), st.sem("sums_ready")
        std_ready, rot_ready, angle_ready = st.sem("std_ready"), st.sem("rot_ready"), st.sem("angle_ready")
        trig_ready, pos_loaded = st.sem("trig_ready"), st.sem("pos_loaded")
        block = st.block()

        @block.sync
        def _(sp):
            sp.dma_start(pos_i[:, :], positions.broadcast_to([ROPE, T])).then_inc(pos_loaded, 16)
            sp.dma_start(feats[:, :, :], feats_d[0:3].rearrange("f p t -> p f t")).then_inc(loaded, 16)
            sp.dma_start(kr[:, :], feats_d[KRWD, 0:64]).then_inc(loaded, 16)

        @block.scalar
        def _(act):
            act.wait_ge(loaded, 32)
            for f in range(3):
                nc.scalar.activation(sq[:, f, :], feats[:, f, :], ACT.Square).then_inc(sq_ready, 1)
            act.wait_ge(sums_ready, 1)
            nc.scalar.activation(std[:, 0, :], sums[:, 0:2, :], ACT.Sqrt, bias=consts["eps"][:, 0:1],
                                 scale=1.0 / Q_LORA).then_inc(std_ready, 1)
            nc.scalar.activation(std[:, 1, :], sums[:, 2:4, :], ACT.Sqrt, bias=consts["eps"][:, 0:1],
                                 scale=1.0 / KV_LORA).then_inc(std_ready, 1)
            for i, out in enumerate((sin, cos)):
                act.wait_ge(angle_ready, i + 1)
                nc.scalar.activation(out[:, :], (krot if i == 0 else turns)[:, :], ACT.Sin).then_inc(trig_ready, 1)

        @block.tensor
        def _(pe):
            pe.wait_ge(loaded, 32)
            for h in range(2):
                nc.tensor.matmul(rot_ps[:, h, :], consts["rot"][:, :], kr[:, h * HALF:(h + 1) * HALF],
                                 start=True, stop=True).then_inc(rot_ready, 1)
            pe.wait_ge(sq_ready, 3)
            for f in range(3):
                for h in range(2):
                    last = nc.tensor.matmul(sums[:, (f // 2) * 2 + h, :], consts["ones"][:, :],
                                            sq[:, f, h * HALF:(h + 1) * HALF], start=(f != 1), stop=(f != 0))
            last.then_inc(sums_ready, 1)

        @block.vector
        def _(dve):
            def reduce_angle(out, quarter):
                nc.vector.tensor_scalar(out[:, :], ang[:, :], float(1.0 / TWO_PI), 0.25 * quarter, ALU.mult, ALU.add)
                dve.drain()
                nc.vector.tensor_scalar(cos[:, :], out[:, :], ROUNDER, -ROUNDER, ALU.add, ALU.add)
                dve.drain()
                nc.vector.scalar_tensor_tensor(out=out[:, :], in0=cos[:, :], scalar=-TWO_PI_A, in1=ang[:, :],
                                               op0=ALU.mult, op1=ALU.add)
                dve.drain()
                for part in (TWO_PI_B, TWO_PI_C):
                    nc.vector.scalar_tensor_tensor(out=out[:, :], in0=cos[:, :], scalar=-part, in1=out[:, :],
                                                   op0=ALU.mult, op1=ALU.add)
                    dve.drain()
                if quarter:
                    nc.vector.tensor_scalar(out[:, :], out[:, :], float(np.pi / 2), None, ALU.add)
                    dve.drain()
                nc.vector.tensor_scalar(out[:, :], out[:, :], PI_BELOW, -PI_BELOW, ALU.min,
                                        ALU.max).then_inc(angle_ready, 1)

            dve.wait_ge(pos_loaded, 16)
            nc.vector.tensor_copy(ang[:, :], pos_i[:, :])
            dve.drain()
            nc.vector.tensor_scalar(ang[:, :], ang[:, :], col(consts, "inv", 0, ROPE), None, ALU.mult)
            dve.drain()
            reduce_angle(krot, 0)
            dve.drain()
            reduce_angle(turns, 1)
            dve.wait_ge(std_ready, 2)
            nc.vector.reciprocal(std[:, :, :], std[:, :, :])
            dve.drain()
            for f, (gain, i) in enumerate((("qg", 0), ("qg", 1), ("kvg", 0))):
                nc.vector.scalar_tensor_tensor(out=feats[:, f, :], in0=feats[:, f, :], scalar=col(consts, gain, i),
                                               in1=std[:, f // 2, :], op0=ALU.mult, op1=ALU.mult)
            dve.wait_ge(trig_ready, 2)
            dve.wait_ge(rot_ready, 2)
            nc.vector.tensor_tensor(krot[:, :], rot_ps[0:ROPE, :, :].rearrange("p h t -> p (h t)"), sin[:, :], ALU.mult)
            nc.vector.tensor_tensor(krope[:, :], kr[:, :], cos[:, :], ALU.mult)
            dve.drain()
            nc.vector.tensor_tensor(krope[:, :], krope[:, :], krot[:, :], ALU.add)


def mla_stage(nc, consts, feats, cos, sin, krope, mix, w_q, w_kv, gates_d):
    scale = float((P + ROPE) ** -0.5)
    fills = 5 + NT
    takes = 4 + NT
    groups = [(i + 4) // 4 for i in range(NT)]
    before = [sum(groups[:i]) for i in range(NT + 1)]
    with Stage(nc, "mla") as st:
        wq = st.sb("wq", [P, 2, P + ROPE])
        wkv = st.sb("wkv", [P, 2 * P])
        qn, kn = st.sb("qn", [P, T]), st.sb("kn", [P, T])
        qraw, qr, qrot = st.sb("qraw", [ROPE, T]), st.sb("qr", [ROPE, T]), st.sb("qrot", [ROPE, T])
        v = st.sb("v", [P, NT, P])
        pr = [st.sb(f"pr{i}", [P, T]) for i in range(2)]
        prT = [st.sb(f"prT{i}", [P, NT, P]) for i in range(2)]
        mx, rsum = st.sb("mx", [P, 2]), st.sb("rsum", [P, 2])
        x = [st.psum(f"x{i}", [P, 2, HALF]) for i in range(2)]
        pt = [st.psum(f"pt{i}", [P, 4, P]) for i in range(2)]
        po = [st.psum(f"po{i}", [P, HALF]) for i in range(2)]
        w_ready, x_full, x_taken = st.sem("w_ready"), st.sem("x_full"), st.sem("x_taken")
        rope_done, max_ready, probs_ready = st.sem("rope_done"), st.sem("max_ready"), st.sem("probs_ready")
        pt_full, pt_taken, po_full, po_taken = (st.sem("pt_full"), st.sem("pt_taken"), st.sem("po_full"),
                                                st.sem("po_taken"))
        block = st.block()

        zeros, zeros_ready, cleared = st.sb("zeros", [P, T]), st.sem("zeros_ready"), st.sem("cleared")

        def keys(i):
            return (i + 1) * P

        @block.gpsimd
        def _(pool):
            nc.gpsimd.memset(zeros[:, :], 0.0).then_inc(zeros_ready, 1)
            pool.wait_ge(zeros_ready, 1)
            with pool.Fori(0, NK) as j:
                pool.dma_start(gates_d[bass.ds(j, 1)].rearrange("a p t -> (a p) t"), zeros[:, :]).then_inc(cleared, 16)
            pool.wait_ge(cleared, 16 * NK)

        @block.sync
        def _(sp):
            sp.dma_start(wq[:, :, :], w_q[0]).then_inc(w_ready, 16)
            sp.dma_start(wkv[:, :], w_kv[0]).then_inc(w_ready, 16)
            with sp.Fori(1, MLA_HEADS) as h:
                sp.wait_ge(x_full, h * fills + (5 - fills))
                sp.dma_start(wq[:, :, :], w_q[bass.ds(h, 1)].rearrange("a p k c -> p (a k) c")).then_inc(w_ready, 16)
                sp.dma_start(wkv[:, :], w_kv[bass.ds(h, 1)].rearrange("a p c -> p (a c)")).then_inc(w_ready, 16)

        @block.tensor
        def _(pe):
            def scores(h, i):
                pe.wait_ge(x_taken, h * takes + (1 + (3 if i == 0 else 3 + i)))
                dst = x[(i + 1) % 2]
                for a in range(0, keys(i), HALF):
                    w = min(HALF, keys(i) - a)
                    nc.tensor.matmul(dst[:, a // HALF, 0:w], qn[:, i * P:(i + 1) * P], kn[:, a:a + w],
                                     start=True, stop=False)
                    last = nc.tensor.matmul(dst[:, a // HALF, 0:w], qr[:, i * P:(i + 1) * P], krope[:, a:a + w],
                                            start=False, stop=True)
                last.then_inc(x_full, 1)

            def transposes(h, i):
                pe.wait_ge(probs_ready, h * NT + (i + 1))
                for g in range(groups[i]):
                    n = before[i] + g
                    pe.wait_ge(pt_taken, h * before[NT] + (n + 1))
                    for j in range(4 * g, min(4 * g + 4, i + 1)):
                        last = nc.tensor.transpose(pt[n % 2][:, j % 4, :], pr[i % 2][:, j * P:(j + 1) * P],
                                                   consts["ident"][:, :])
                    last.then_inc(pt_full, 1)

            def weigh(h, i):
                pe.wait_ge(pt_taken, h * before[NT] + (before[i + 1] + 2))
                pe.wait_ge(po_taken, h * NT + (i + 1))
                for j in range(i + 1):
                    last = nc.tensor.matmul(po[i % 2][:, 0:P], v[:, j, :], prT[i % 2][:, j, :],
                                            start=(j == 0), stop=(j == i))
                last.then_inc(po_full, 1)

            with pe.Fori(0, MLA_HEADS) as h:
                pe.wait_ge(w_ready, h * 32 + 32)
                pe.wait_ge(x_taken, h * takes + 1)
                for kc in range(2):
                    for a in range(2):
                        last = nc.tensor.matmul(x[0][0:ROPE, a, :], wq[:, kc, P:P + ROPE],
                                                feats[:, CQ + kc, a * HALF:(a + 1) * HALF],
                                                start=(kc == 0), stop=(kc == 1))
                last.then_inc(x_full, 1)
                for kc in range(2):
                    for a in range(2):
                        last = nc.tensor.matmul(x[1][:, a, :], wq[:, kc, 0:P],
                                                feats[:, CQ + kc, a * HALF:(a + 1) * HALF],
                                                start=(kc == 0), stop=(kc == 1))
                last.then_inc(x_full, 1)
                pe.wait_ge(x_taken, h * takes + 2)
                for a in range(2):
                    last = nc.tensor.matmul(x[0][:, a, :], consts["rot"][:, :], qraw[:, a * HALF:(a + 1) * HALF],
                                            start=True, stop=True)
                last.then_inc(x_full, 1)
                pe.wait_ge(x_taken, h * takes + 3)
                for a in range(2):
                    last = nc.tensor.matmul(x[1][:, a, :], wkv[:, 0:P], feats[:, CKV, a * HALF:(a + 1) * HALF],
                                            start=True, stop=True)
                last.then_inc(x_full, 1)
                pe.wait_ge(rope_done, h + 2)
                for i in range(NT):
                    last = nc.tensor.matmul(x[0][:, i // 4, (i % 4) * P:(i % 4 + 1) * P],
                                            feats[:, CKV, i * P:(i + 1) * P], wkv[:, P:2 * P], start=True, stop=True)
                last.then_inc(x_full, 1)
                scores(h, 0)
                for i in range(NT):
                    if i + 1 < NT:
                        scores(h, i + 1)
                    transposes(h, i)
                    weigh(h, i)

        @block.scalar
        def _(act):
            def exps(h, i):
                act.wait_ge(max_ready, h * NT + (i + 1))
                nc.scalar.activation(pr[i % 2][:, 0:keys(i)],
                                     x[(i + 1) % 2][:, :, :].rearrange("p a b -> p (a b)")[:, 0:keys(i)], ACT.Exp,
                                     bias=mx[:, i % 2:i % 2 + 1], scale=scale,
                                     accum_out=rsum[:, i % 2:i % 2 + 1]).then_inc(x_taken, 1)

            nc.scalar.activation(rsum[:, 0:1], consts["ones"][:, 0:1], ACT.Copy).then_inc(x_taken, 1)
            nc.scalar.activation(rsum[:, 1:2], consts["ones"][:, 0:1], ACT.Copy).then_inc(pt_taken, 2)
            with act.Fori(0, MLA_HEADS) as h:
                act.wait_ge(x_full, h * fills + 1)
                act.wait_ge(rope_done, h + 1)
                nc.scalar.activation(qraw[:, :], x[0][0:ROPE, :, :].rearrange("p a b -> p (a b)"),
                                     ACT.Copy).then_inc(x_taken, 1)
                act.wait_ge(x_full, h * fills + 2)
                nc.scalar.activation(qn[:, :], x[1][:, :, :].rearrange("p a b -> p (a b)"),
                                     ACT.Copy).then_inc(x_taken, 1)
                act.wait_ge(x_full, h * fills + 4)
                nc.scalar.activation(kn[:, :], x[1][:, :, :].rearrange("p a b -> p (a b)"),
                                     ACT.Copy).then_inc(x_taken, 1)
                act.wait_ge(x_full, h * fills + 5)
                act.wait_ge(po_taken, h * NT + 2)
                nc.scalar.activation(v[:, :, :].rearrange("p a b -> p (a b)"),
                                     x[0][:, :, :].rearrange("p a b -> p (a b)"), ACT.Copy).then_inc(x_taken, 1)
                exps(h, 0)
                for i in range(NT):
                    if i + 1 < NT:
                        exps(h, i + 1)
                    for g in range(groups[i]):
                        n = before[i] + g
                        if i >= 2 and g == 0:
                            act.wait_ge(po_full, h * NT + (i - 1))
                        act.wait_ge(pt_full, h * before[NT] + (n + 1))
                        m = min(4, i + 1 - 4 * g)
                        nc.scalar.activation(prT[i % 2][:, 4 * g:4 * g + m, :], pt[n % 2][:, 0:m, :],
                                             ACT.Copy).then_inc(pt_taken, 1)

        @block.vector
        def _(dve):
            def maxima(h, i):
                dve.wait_ge(x_full, h * fills + (6 + i))
                s = x[(i + 1) % 2][:, :, :].rearrange("p a b -> p (a b)")
                nc.vector.memset(s[0:64, keys(i) - 64:keys(i)], -1e30)
                dve.drain()
                nc.vector.tensor_reduce(mx[:, i % 2:i % 2 + 1], s[:, 0:keys(i)], AX.X, ALU.max)
                dve.drain()
                nc.vector.tensor_scalar(mx[:, i % 2:i % 2 + 1], mx[:, i % 2:i % 2 + 1], -scale, None,
                                        ALU.mult).then_inc(max_ready, 1)

            def normalise(h, i):
                dve.wait_ge(x_taken, h * takes + (1 + 4 + i + 1))
                nc.vector.reciprocal(rsum[:, i % 2:i % 2 + 1], rsum[:, i % 2:i % 2 + 1])
                dve.drain()
                nc.vector.tensor_scalar(pr[i % 2][:, 0:keys(i)], pr[i % 2][:, 0:keys(i)], rsum[:, i % 2:i % 2 + 1],
                                        None, ALU.mult).then_inc(probs_ready, 1)

            def output(h, i):
                dve.wait_ge(po_full, h * NT + (i + 1))
                nc.vector.tensor_copy(mix[:, bass.ds(h, 1), i * P:(i + 1) * P].rearrange("p a t -> p (a t)"),
                                      po[i % 2][:, 0:P]).then_inc(po_taken, 1)

            nc.vector.memset(mx[:, 0:1], 0.0).then_inc(rope_done, 1)
            nc.vector.memset(mx[:, 1:2], 0.0).then_inc(po_taken, 2)
            dve.drain()
            with dve.Fori(0, MLA_HEADS) as h:
                dve.wait_ge(x_taken, h * takes + 2)
                nc.vector.tensor_tensor(qr[:, :], qraw[:, :], cos[:, :], ALU.mult)
                dve.wait_ge(x_full, h * fills + 3)
                nc.vector.tensor_tensor(qrot[:, :], x[0][0:ROPE, :, :].rearrange("p a b -> p (a b)"), sin[:, :],
                                        ALU.mult)
                dve.drain()
                nc.vector.tensor_tensor(qr[:, :], qr[:, :], qrot[:, :], ALU.add).then_inc(rope_done, 1)
                maxima(h, 0)
                for i in range(NT):
                    if i + 1 < NT:
                        maxima(h, i + 1)
                    normalise(h, i)
                    if i >= 1:
                        output(h, i - 1)
                output(h, NT - 1)


def rwkv_stage(nc, consts, feats_d, w_up_d, a_up_d, g_up_d, mix):
    decay = float(np.exp(-0.5))
    W = PAIRS * P
    with Stage(nc, "rwkv") as st:
        w_up, a_up, g_up = st.sb("w_up", [64, RW]), st.sb("a_up", [64, RW]), st.sb("g_up", [P, RW])
        rkv = st.sb("rkv", [P, 12, P])
        gd = st.sb("gd", [P, P])
        wad = st.sb("wad", [64, 2, P])

        def tile4(name, n=1):
            return st.sb(name, [P, PAIRS * n, P])

        sgw, al, gate, cum, prev, rem = (tile4(x) for x in ("sgw", "al", "gate", "cum", "prev", "rem"))
        w_t, w_inv, w_prev, w_rem = (tile4(x) for x in ("w_t", "w_inv", "w_prev", "w_rem"))
        kkr, sqk, nrm, kap, b, ta, k2 = (tile4(x) for x in ("kkr", "sqk", "nrm", "kap", "b", "ta", "k2"))
        ktrt = st.sb("ktrt", [P, PAIRS, 2, P])
        kh, bh, krm, brm, rk, bonus = (tile4(x) for x in ("kh", "bh", "krm", "brm", "rk", "bonus"))
        rhsU = st.sb("rhsU", [P, 2 * PAIRS, P])
        kr_t, br_t, v_t = (tile4(x) for x in ("kr_t", "br_t", "v_t"))
        gm = st.sb("gm", [P, 2 * PAIRS, 4, P])
        lb = [tile4(f"lb{e}") for e in range(2)]
        xi = [tile4(f"xi{e}") for e in range(2)]
        yi = [tile4(f"yi{e}") for e in range(2)]
        tmp = [tile4(f"tmp{e}") for e in range(2)]
        ll = st.sb("ll", [P, 2, 5, PAIRS, P])
        pe_s = [tile4(f"pe_s{e}") for e in range(2)]
        nu = st.sb("nu", [P, 2, 2 * PAIRS, 64])
        at, diag, es = ([tile4(f"{x}{c}") for c in range(2)] for x in ("at", "diag", "es"))
        q1 = tile4("q1")
        state = [tile4(f"state{c}") for c in range(2)]
        ysb, yc, sqy, std = (tile4(x) for x in ("ysb", "yc", "sqy", "std"))
        bank = [st.psum(f"bank{i}", [P, PAIRS, P]) for i in range(8)]

        per_tile = {}

        def sem(name, n):
            per_tile[name] = (st.sem(name), n)
            return name

        for name, n in (("loaded", 64), ("pre", 3), ("biased", 2), ("sig", 2), ("gated", 1), ("cums", 1), ("kk", 1),
                        ("sqk", 1), ("norms", 1), ("sqrt", 1), ("k2", 1), ("exps", 4), ("ktrt", 1), ("khbh", 1),
                        ("rem", 1), ("rk", 2), ("bonus_mm", 1), ("bonus", 1), ("trans", 4), ("trans_taken", 4),
                        ("gram", 8), ("masked", 8), ("lb_mm", 2), ("lb", 2), ("ux", 1), ("ux_taken", 1),
                        ("level", 10), ("inv", 12), ("p_mm", 10), ("p_taken", 10), ("z_mm", 10), ("u_mm", 2),
                        ("nu", 2), ("at_mm", 2), ("e_mm", 2), ("diag", 2), ("at", 2), ("es", 2), ("q_mm", 1),
                        ("q1", 1), ("chain", 2), ("state", 2), ("y_mm", 1), ("y", 1), ("mean", 1), ("yc", 1),
                        ("sqy", 1), ("var", 1), ("std", 1), ("done", 1)):
            sem(name, n)
        w_loaded, mixed = st.sem("w_loaded"), st.sem("mixed")
        block = st.block()

        def inc(ins, name, n=1):
            return ins.then_inc(per_tile[name][0], n)

        def flat(x):
            return x[:, :, :].rearrange("p a b -> p (a b)")

        def over_heads(c):
            return c.unsqueeze(1).broadcast_to([P, PAIRS, P])

        class Tile:
            def __init__(self, eng, t):
                self.eng, self.t = eng, t

            def wait(self, name, k):
                s, n = per_tile[name]
                self.eng.wait_ge(s, self.t * n + k)

            def begin(self):
                self.eng.wait_ge(per_tile["done"][0], self.t + 1)

        @block.sync
        def _(sp):
            sp.dma_start(w_up[:, :], w_up_d).then_inc(w_loaded, 16)
            sp.dma_start(a_up[:, :], a_up_d).then_inc(w_loaded, 16)
            sp.dma_start(g_up[:, :], g_up_d).then_inc(w_loaded, 16)
            with sp.Fori(0, NT) as t:
                Tile(sp, t).begin()
                tok = bass.ds(t * P, P)
                inc(sp.dma_start(rkv[:, :, :], feats_d[RT:GT, :, tok].rearrange("f p t -> p f t")), "loaded", 16)
                inc(sp.dma_start(gd[:, :], feats_d[GT, :, tok]), "loaded", 16)
                inc(sp.dma_start(wad[:, 0, :], feats_d[KRWD, 64:P, tok]), "loaded", 16)
                inc(sp.dma_start(wad[:, 1, :], feats_d[AD, 0:64, tok]), "loaded", 16)

        @block.tensor
        def _(pe):
            pe.wait_ge(w_loaded, 48)
            with pe.Fori(0, NT) as t:
                w = Tile(pe, t)
                w.begin()

                w.wait("gated", 1)
                for f in range(PAIRS):
                    last = nc.tensor.matmul(bank[0][:, f, :], w_up[:, f * P:(f + 1) * P], wad[:, 0, :],
                                            start=True, stop=True)
                inc(last, "pre")
                for f in range(PAIRS):
                    last = nc.tensor.matmul(bank[1][:, f, :], a_up[:, f * P:(f + 1) * P], wad[:, 1, :],
                                            start=True, stop=True)
                inc(last, "pre")
                for f in range(PAIRS):
                    last = nc.tensor.matmul(bank[2][:, f, :], g_up[:, f * P:(f + 1) * P], gd[:, :],
                                            start=True, stop=True)
                inc(last, "pre")
                w.wait("biased", 2)
                w.wait("sqk", 1)
                inc(nc.tensor.matmul(flat(bank[0]), consts["headones"][:, :], flat(sqk), start=True, stop=True),
                    "norms")
                w.wait("rk", 2)
                inc(nc.tensor.matmul(flat(bank[1]), consts["headones"][:, :], flat(rk), start=True, stop=True),
                    "bonus_mm")
                for n, (src, after) in enumerate(((lambda f: ktrt[:, f, 0, :], "ktrt"), (lambda f: krm[:, f, :], "rem"),
                                                  (lambda f: brm[:, f, :], "rem"),
                                                  (lambda f: rkv[:, 8 + f, :], "rem"))):
                    w.wait(after, 1)
                    if n >= 2:
                        w.wait("trans_taken", n - 1)
                    for f in range(PAIRS):
                        last = nc.tensor.transpose(bank[6 + n % 2][:, f, :], src(f), consts["ident"][:, :])
                    inc(last, "trans")
                w.wait("khbh", 1)
                for h in range(2 * PAIRS):
                    f, rows = h // 2, slice(64 * (h % 2), 64 * (h % 2) + 64)
                    if h >= 2:
                        w.wait("masked", h - 1)
                    nc.tensor.matmul(bank[4 + h % 2][:, 0:2, :], kh[rows, f, :], ktrt[rows, f, :, :],
                                     start=True, stop=True)
                    inc(nc.tensor.matmul(bank[4 + h % 2][:, 2:4, :], bh[rows, f, :], ktrt[rows, f, :, :],
                                         start=True, stop=True), "gram")
                for e in range(2):
                    rows = slice(64 * e, 64 * e + 64)
                    w.wait("trans_taken", 3 + e)
                    for f in range(PAIRS):
                        last = nc.tensor.matmul(bank[6 + e][:, f, :], ktrt[rows, f, 0, :], bh[rows, f, :],
                                                start=True, stop=True)
                    inc(last, "lb_mm")
                w.wait("masked", 8)
                for h in range(2 * PAIRS):
                    last = nc.tensor.matmul(bank[3][:, h // 2, 64 * (h % 2):64 * (h % 2) + 64], gm[:, h, 0, :],
                                            flat(v_t)[:, h * 64:(h + 1) * 64], start=True, stop=True)
                inc(last, "ux")
                w.wait("norms", 1)
                w.wait("sqrt", 1)
                w.wait("bonus", 1)
                for l in range(1, 6):
                    for e in range(2):
                        w.wait("level", 2 * (l - 1) + e + 1)
                        w.wait("inv", 2 * (l - 1) + e + 1)
                        for f in range(PAIRS):
                            last = nc.tensor.matmul(bank[e][:, f, :], ll[:, e, l - 1, f, :], xi[e][:, f, :],
                                                    start=True, stop=True)
                        inc(last, "p_mm")
                    if l == 1:
                        w.wait("ux_taken", 1)
                    for e in range(2):
                        w.wait("p_taken", 2 * (l - 1) + e + 1)
                        for f in range(PAIRS):
                            last = nc.tensor.matmul(bank[2 + e][:, f, :], yi[e][:, f, :], pe_s[e][:, f, :],
                                                    start=True, stop=True)
                            if l < 5:
                                last = nc.tensor.matmul(bank[4 + e][:, f, :], pe_s[e][:, f, :], yi[e][:, f, :],
                                                        start=True, stop=True)
                        inc(last, "z_mm")
                for e in range(2):
                    w.wait("inv", 10 + e + 1)
                    for f in range(PAIRS):
                        last = nc.tensor.matmul(bank[e][:, f, :], xi[e][:, f, :], rhsU[:, 2 * f + e, :],
                                                start=True, stop=True)
                    inc(last, "u_mm")
                w.wait("nu", 2)
                for c in range(2):
                    rows = slice(64 * c, 64 * c + 64)
                    for f in range(PAIRS):
                        last = nc.tensor.matmul(bank[c][:, f, :], nu[rows, 0, 2 * f:2 * f + 2, :].rearrange("p h c -> p (h c)"),
                                                br_t[rows, f, :], start=True, stop=True)
                    inc(last, "at_mm")
                    for f in range(PAIRS):
                        nc.tensor.matmul(bank[2 + c][:, f, :], kr_t[rows, f, :], v_t[rows, f, :],
                                         start=True, stop=False)
                        last = nc.tensor.matmul(bank[2 + c][:, f, :], br_t[rows, f, :],
                                                nu[rows, 1, 2 * f:2 * f + 2, :].rearrange("p h c -> p (h c)"), start=False, stop=True)
                    inc(last, "e_mm")
                for h in range(2 * PAIRS):
                    f, rows = h // 2, slice(64 * (h % 2), 64 * (h % 2) + 64)
                    last = nc.tensor.matmul(bank[4][rows, f, :], nu[:, 0, h, :], gm[:, h, 3, :], start=True, stop=True)
                inc(last, "q_mm")
                for h in range(2 * PAIRS):
                    f, rows = h // 2, slice(64 * (h % 2), 64 * (h % 2) + 64)
                    nc.tensor.matmul(bank[5][rows, f, :], flat(v_t)[:, h * 64:(h + 1) * 64], gm[:, h, 1, :],
                                     start=(h < 2), stop=False, skip_group_check=True)
                    nc.tensor.matmul(bank[5][rows, f, :], nu[:, 1, h, :], gm[:, h, 3, :],
                                     start=False, stop=False, skip_group_check=True)
                w.wait("q1", 1)
                for c in range(2):
                    if c == 0:
                        pe.wait_ge(per_tile["state"][0], t * 2 + 1)
                    else:
                        w.wait("state", 2)
                    for f in range(PAIRS):
                        last = nc.tensor.matmul(bank[5][:, f, c * CH:(c + 1) * CH], state[c][:, f, :],
                                                q1[:, f, c * CH:(c + 1) * CH], start=False, stop=(c == 1),
                                                skip_group_check=True)
                    if c == 1:
                        inc(last, "y_mm")
                    w.wait("at", c + 1)
                    for f in range(PAIRS):
                        last = nc.tensor.matmul(bank[6 + c][:, f, :], at[c][:, f, :], state[c][:, f, :],
                                                start=True, stop=True)
                    inc(last, "chain")
                w.wait("y", 1)
                inc(nc.tensor.matmul(flat(bank[0]), consts["headones"][:, :], flat(ysb), start=True, stop=True), "mean")
                w.wait("sqy", 1)
                inc(nc.tensor.matmul(flat(bank[1]), consts["headones"][:, :], flat(sqy), start=True, stop=True), "var")

        @block.scalar
        def _(act):
            with act.Fori(0, NT) as t:
                w = Tile(act, t)
                w.begin()
                w.wait("loaded", 64)
                nc.scalar.activation(wad[:, 0, :], wad[:, 0, :], ACT.Tanh)
                inc(nc.scalar.activation(gd[:, :], gd[:, :], ACT.Sigmoid), "gated")
                w.wait("biased", 1)
                inc(nc.scalar.activation(flat(sgw), flat(sgw), ACT.Sigmoid), "sig")
                w.wait("biased", 2)
                inc(nc.scalar.activation(flat(al), flat(al), ACT.Sigmoid), "sig")
                w.wait("pre", 3)
                nc.scalar.activation(flat(gate), flat(bank[2]), ACT.Copy)
                w.wait("kk", 1)
                inc(nc.scalar.activation(flat(sqk), flat(kkr), ACT.Square), "sqk")
                w.wait("norms", 1)
                inc(nc.scalar.activation(flat(nrm), flat(bank[0]), ACT.Sqrt), "sqrt")
                w.wait("cums", 1)
                for out, x, sign in ((w_prev, prev, -1.0), (w_t, cum, -1.0), (w_inv, cum, 1.0), (w_rem, rem, -1.0)):
                    inc(nc.scalar.activation(flat(out), flat(x), ACT.Exp, scale=sign * decay), "exps")
                for n, dst in enumerate((rhsU[:, :, 0:64], kr_t, br_t, v_t)):
                    w.wait("trans", n + 1)
                    src = bank[6 + n % 2]
                    if n == 0:
                        last = nc.scalar.activation(dst, flat(src).rearrange("p (h c) -> p h c", c=64), ACT.Copy)
                    else:
                        last = nc.scalar.activation(flat(dst), flat(src), ACT.Copy)
                    inc(last, "trans_taken")
                w.wait("ux", 1)
                inc(nc.scalar.activation(rhsU[:, :, 64:128], flat(bank[3]).rearrange("p (h c) -> p h c", c=64),
                                         ACT.Copy), "ux_taken")
                for l in range(1, 6):
                    for e in range(2):
                        w.wait("p_mm", 2 * (l - 1) + e + 1)
                        if l >= 2:
                            w.wait("z_mm", 2 * (l - 2) + e + 1)
                        inc(nc.scalar.activation(flat(pe_s[e]), flat(bank[e]), ACT.Copy), "p_taken")
                for e in range(2):
                    w.wait("u_mm", e + 1)
                    inc(nc.scalar.activation(nu[:, :, :, :].rearrange("p w (f e) c -> p e f w c", e=2)[:, e],
                                             bank[e][:, :, :].rearrange("p f (w c) -> p f w c", w=2), ACT.Copy, scale=-1.0), "nu")
                w.wait("y_mm", 1)
                inc(nc.scalar.activation(flat(ysb), flat(bank[5]), ACT.Copy), "y")
                w.wait("yc", 1)
                inc(nc.scalar.activation(flat(sqy), flat(yc), ACT.Square), "sqy")
                w.wait("var", 1)
                inc(nc.scalar.activation(flat(std), flat(bank[1]), ACT.Sqrt, bias=consts["eps"][:, 1:2],
                                         scale=1.0 / CH), "std")

        @block.gpsimd
        def _(pool):
            with pool.Fori(0, NT) as t:
                w = Tile(pool, t)
                w.begin()
                w.wait("loaded", 64)
                inc(nc.gpsimd.tensor_tensor(kkr[:, :, :], rkv[:, 4:8, :], cols_over(consts, "kk", PAIRS, P), ALU.mult),
                    "kk")
                w.wait("k2", 1)
                inc(nc.gpsimd.tensor_tensor(rk[:, :, :], rkv[:, 0:4, :], k2[:, :, :], ALU.mult), "rk")
                w.wait("rk", 1)
                inc(nc.gpsimd.tensor_tensor(rk[:, :, :], rk[:, :, :], cols_over(consts, "rk", PAIRS, P), ALU.mult),
                    "rk")
                w.wait("exps", 4)
                for c in range(2):
                    end = w_t[:, :, c * CH + CH - 1:c * CH + CH].broadcast_to([P, PAIRS, P])
                    inc(nc.gpsimd.tensor_tensor(diag[c][:, :, :], over_heads(consts["ident"][:, :]), end, ALU.mult),
                        "diag")
                for l in range(1, 6):
                    for e in range(2):
                        if l == 1:
                            w.wait("lb", e + 1)
                        inc(nc.gpsimd.tensor_tensor(ll[:, e, l - 1, :, :], lb[e][:, :, :],
                                                    over_heads(consts["level"][:, l, :]), ALU.mult), "level")

        @block.vector
        def _(dve):
            inc(nc.vector.memset(flat(state[0]), 0.0), "state")
            inc(nc.vector.memset(flat(state[1]), 0.0), "done")
            with dve.Fori(0, NT) as t:
                w = Tile(dve, t)
                w.wait("pre", 1)
                nc.vector.tensor_tensor(sgw[:, :, :], bank[0][:, :, :], cols_over(consts, "w0", PAIRS, P),
                                        ALU.add).then_inc(per_tile["biased"][0], 1)
                w.wait("pre", 2)
                inc(nc.vector.tensor_tensor(al[:, :, :], bank[1][:, :, :], cols_over(consts, "a0", PAIRS, P), ALU.add),
                    "biased")
                w.wait("sig", 1)
                nc.vector.tensor_tensor_scan(flat(cum), consts["scanmask"][:, :], flat(sgw), 0.0, ALU.mult, ALU.add)
                dve.drain()
                nc.vector.tensor_tensor(flat(prev), flat(cum), flat(sgw), ALU.subtract)
                chunks = flat(cum).rearrange("p (c t) -> p c t", t=CH)
                inc(nc.vector.tensor_tensor(flat(rem).rearrange("p (c t) -> p c t", t=CH),
                                            chunks[:, :, CH - 1:CH].broadcast_to([P, 2 * PAIRS, CH]), chunks,
                                            ALU.subtract), "cums")
                w.wait("sig", 2)
                nc.vector.scalar_tensor_tensor(out=ta[:, :, :], in0=al[:, :, :], scalar=-1.0,
                                               in1=cols_over(consts, "ka", PAIRS, P), op0=ALU.add, op1=ALU.mult)
                dve.drain()
                inc(nc.vector.scalar_tensor_tensor(out=k2[:, :, :], in0=ta[:, :, :], scalar=1.0, in1=rkv[:, 4:8, :],
                                                   op0=ALU.add, op1=ALU.mult), "k2")
                w.wait("sqrt", 1)
                nc.vector.tensor_scalar(flat(nrm), flat(nrm), 1e-12, None, ALU.max)
                dve.drain()
                nc.vector.reciprocal(flat(nrm), flat(nrm))
                dve.drain()
                nc.vector.tensor_tensor(flat(kap), flat(kkr), flat(nrm), ALU.mult)
                dve.drain()
                nc.vector.tensor_tensor(flat(b), flat(kap), flat(al), ALU.mult)
                w.wait("exps", 2)
                nc.vector.tensor_tensor(ktrt[:, :, 0, :], kap[:, :, :], w_prev[:, :, :], ALU.mult)
                inc(nc.vector.tensor_tensor(ktrt[:, :, 1, :], rkv[:, 0:4, :], w_t[:, :, :], ALU.mult), "ktrt")
                dve.drain()
                w.wait("exps", 4)
                nc.vector.tensor_tensor(flat(kh), flat(k2), flat(w_inv), ALU.mult)
                inc(nc.vector.tensor_tensor(flat(bh), flat(b), flat(w_inv), ALU.mult), "khbh")
                nc.vector.tensor_tensor(flat(krm), flat(k2), flat(w_rem), ALU.mult)
                inc(nc.vector.tensor_tensor(flat(brm), flat(b), flat(w_rem), ALU.mult), "rem")
                w.wait("bonus_mm", 1)
                inc(nc.vector.tensor_tensor(bonus[:, :, :], bank[1][:, :, :], rkv[:, 8:12, :], ALU.mult), "bonus")
                for h in range(2 * PAIRS):
                    w.wait("gram", h + 1)
                    inc(nc.vector.tensor_tensor(gm[:, h, :, :], bank[4 + h % 2][:, :, :], consts["mask4"][:, :, :],
                                                ALU.mult), "masked")
                for e in range(2):
                    w.wait("lb_mm", e + 1)
                    inc(nc.vector.tensor_tensor(lb[e][:, :, :], bank[6 + e][:, :, :], over_heads(consts["lower"][:, :]),
                                                ALU.mult), "lb")
                dve.drain()
                gv = gm[:, :, :, :].rearrange("p (f e) w c -> p f e w c", e=2)
                for e in range(2):
                    nc.vector.tensor_tensor(tmp[0][:, :, :], gv[:, :, e, 2, :], over_heads(consts["upper0"][:, :]),
                                            ALU.mult)
                    nc.vector.tensor_tensor(tmp[1][:, :, :], lb[e][:, :, :], over_heads(consts["level"][:, 0, :]),
                                            ALU.mult)
                    dve.drain()
                    nc.vector.scalar_tensor_tensor(out=xi[e][:, :, :], in0=tmp[0][:, :, :], scalar=-1.0,
                                                   in1=over_heads(consts["ident"][:, :]), op0=ALU.mult, op1=ALU.add)
                    inc(nc.vector.scalar_tensor_tensor(out=yi[e][:, :, :], in0=tmp[1][:, :, :], scalar=-1.0,
                                                       in1=over_heads(consts["ident"][:, :]), op0=ALU.mult,
                                                       op1=ALU.add), "inv")
                    dve.drain()
                for l in range(1, 6):
                    for e in range(2):
                        w.wait("z_mm", 2 * (l - 1) + e + 1)
                        last = nc.vector.tensor_tensor(flat(xi[e]), flat(xi[e]), flat(bank[2 + e]), ALU.subtract)
                        if l < 5:
                            last = nc.vector.tensor_tensor(flat(yi[e]), flat(yi[e]), flat(bank[4 + e]), ALU.subtract)
                        inc(last, "inv")
                    dve.drain()
                for c in range(2):
                    w.wait("at_mm", c + 1)
                    nc.vector.tensor_tensor(at[c][:, :, :], bank[c][:, :, :], over_heads(consts["headones"][:, :]),
                                            ALU.mult)
                    w.wait("e_mm", c + 1)
                    nc.vector.tensor_tensor(es[c][:, :, :], bank[2 + c][:, :, :], over_heads(consts["headones"][:, :]),
                                            ALU.mult)
                    dve.drain()
                    w.wait("diag", c + 1)
                    inc(nc.vector.tensor_tensor(flat(at[c]), flat(at[c]), flat(diag[c]), ALU.add), "at")
                w.wait("q_mm", 1)
                inc(nc.vector.tensor_tensor(q1[:, :, :], bank[4][:, :, :], ktrt[:, :, 1, :], ALU.add), "q1")
                for c in range(2):
                    w.wait("chain", c + 1)
                    inc(nc.vector.tensor_tensor(flat(state[1 - c]), flat(bank[6 + c]), flat(es[c]), ALU.add), "state")
                w.wait("mean", 1)
                w.wait("y", 1)
                inc(nc.vector.scalar_tensor_tensor(out=flat(yc), in0=flat(bank[0]), scalar=-1.0 / CH, in1=flat(ysb),
                                                   op0=ALU.mult, op1=ALU.add), "yc")
                w.wait("std", 1)
                nc.vector.reciprocal(flat(std), flat(std))
                dve.drain()
                nc.vector.tensor_tensor(flat(yc), flat(yc), flat(std), ALU.mult)
                dve.drain()
                nc.vector.tensor_tensor(yc[:, :, :], yc[:, :, :], cols_over(consts, "lnw", PAIRS, P), ALU.mult)
                dve.drain()
                nc.vector.tensor_tensor(yc[:, :, :], yc[:, :, :], cols_over(consts, "lnb", PAIRS, P), ALU.add)
                dve.drain()
                nc.vector.tensor_tensor(flat(yc), flat(yc), flat(bonus), ALU.add)
                dve.drain()
                inc(nc.vector.tensor_tensor(mix[:, 4:8, bass.ds(t * P, P)], yc[:, :, :], gate[:, :, :], ALU.mult),
                    "done")


def residual_stage(nc, consts, name, weights, acts, src, dst, load=None):
    with Stage(nc, name) as st:
        x = SplitInput(nc, st, consts, acts)
        proj = Projection(nc, st, weights, KC, x)
        loaded = st.sem("loaded")
        block = st.block()

        @block.sync
        def _(sp):
            proj.first_loads(sp)
            if load is not None:
                sp.dma_start(src[:, :, :], load.rearrange("k p t -> p k t")).then_inc(loaded, 16)
            proj.loads(sp)

        @block.tensor
        def _(pe):
            proj.products(pe)

        @block.scalar
        def _(act):
            proj.first_highs(act)
            proj.highs(act)

        @block.vector
        def _(dve):
            proj.first_lows(dve)
            if load is not None:
                dve.wait_ge(loaded, 16)

            def take(i, tile):
                at = bass.ds(tile, 1) if not isinstance(tile, int) else slice(tile, tile + 1)
                nc.vector.tensor_tensor(dst[:, at, :].rearrange("p a t -> p (a t)"),
                                        src[:, at, :].rearrange("p a t -> p (a t)"), proj.product(i),
                                        ALU.add).then_inc(proj.taken, 1)

            proj.takes(dve, take)


def queries_stage(nc, consts, h, weights, q):
    with Stage(nc, "xq") as st:
        x = SplitInput(nc, st, consts, h, "xa")
        proj = Projection(nc, st, weights, KC, x)
        block = st.block()

        @block.sync
        def _(sp):
            proj.first_loads(sp)
            proj.loads(sp)

        @block.gpsimd
        def _(pool):
            x.squares(pool)

        @block.tensor
        def _(pe):
            proj.products(pe)

        @block.scalar
        def _(act):
            proj.first_highs(act)
            proj.highs(act)

        @block.vector
        def _(dve):
            proj.first_lows(dve)

            def take(i, tile):
                at = bass.ds(tile, 1) if not isinstance(tile, int) else slice(tile, tile + 1)
                nc.vector.tensor_tensor(q[:, at, :].rearrange("p a t -> p (a t)"), proj.product(i), x.rstd[:, :],
                                        ALU.mult).then_inc(proj.taken, 1)

            proj.takes(dve, take)


def memory_stage(nc, memn, w_k, w_v, k, v):
    hd = D // XH
    with Stage(nc, "kv") as st:
        wk = [st.sb(f"wk{i}", [P, KC, hd]) for i in range(XH)]
        wv = [st.sb(f"wv{i}", [P, KC, hd]) for i in range(XH)]
        ps = [st.psum(f"ps{i}", [P, HALF]) for i in range(4)]
        w_ready, mm_done = st.sem("w_ready"), st.sem("mm_done")
        block = st.block()

        @block.sync
        def _(sp):
            for h in range(XH):
                sp.dma_start(wk[h][:, :, :], w_k[h]).then_inc(w_ready, 16)
                sp.wait_ge(w_ready, 32 * h + 16)
                sp.dma_start(wv[h][:, :, :], w_v[h]).then_inc(w_ready, 16)
                sp.wait_ge(w_ready, 32 * h + 32)

        taken = st.sem("taken")

        @block.tensor
        def _(pe):
            for h in range(XH):
                for kind in range(2):
                    n = 2 * h + kind
                    pe.wait_ge(w_ready, 16 * (n + 1))
                    if n >= 4:
                        pe.wait_ge(taken, n - 3)
                    for a in range(2):
                        part = slice(a * P, (a + 1) * P)
                        for kc in range(KC):
                            lhs, rhs = ((wk[h][:, kc, part], memn[:, kc, :]) if kind == 0 else
                                        (memn[:, kc, part], wv[h][:, kc, :]))
                            last = nc.tensor.matmul(ps[n % 4][:, a * MEM:(a + 1) * MEM], lhs, rhs,
                                                    start=(kc == 0), stop=(kc == KC - 1))
                    last.then_inc(mm_done, 1)

        @block.scalar
        def _(act):
            for h in range(XH):
                for kind, dst in enumerate((k, v)):
                    n = 2 * h + kind
                    act.wait_ge(mm_done, n + 1)
                    nc.scalar.activation(dst[:, h, :], ps[n % 4][:, :], ACT.Copy).then_inc(taken, 1)


def cross_attention_stage(nc, consts, qo, k, v):
    hd = D // XH
    scale = float(hd ** -0.5)
    with Stage(nc, "xa") as st:
        q, vh = st.sb("q", [P, 2, T]), st.sb("vh", [P, 2, hd])
        pr = [st.sb(f"pr{i}", [P, 4, MEM]) for i in range(2)]
        prT = st.sb("prT", [P, 2, HALF])
        mx, rsum = st.sb("mx", [P, 2, 4]), st.sb("rsum", [P, 2, 4])
        x = [st.psum(f"x{i}", [P, 4 * MEM]) for i in range(2)]
        pt = [st.psum(f"pt{i}", [P, 4, P]) for i in range(2)]
        po = [st.psum(f"po{i}", [P, HALF]) for i in range(2)]
        q_in, v_in, s_full, max_ready = st.sem("q_in"), st.sem("v_in"), st.sem("s_full"), st.sem("max_ready")
        exp_done, probs_ready = st.sem("exp_done"), st.sem("probs_ready")
        pt_full, pt_taken, po_full, po_taken = (st.sem("pt_full"), st.sem("pt_taken"), st.sem("po_full"),
                                                st.sem("po_taken"))
        block = st.block()

        def at(i, n=1):
            return slice(i, i + n) if isinstance(i, int) else bass.ds(i, n)

        def each_head(eng, body):
            with eng.Fori(0, XH - 1) as h:
                body(h, True)
            body(XH - 1, False)

        @block.gpsimd
        def _(pool):
            nc.gpsimd.tensor_copy(q[:, :, :], qo[:, 0:2, :]).then_inc(q_in, 1)
            nc.gpsimd.tensor_copy(vh[:, :, :].rearrange("p m c -> p (m c)"), v[:, 0, :]).then_inc(v_in, 1)
            with pool.Fori(0, XH - 1) as h:
                pool.wait_ge(s_full, h * 2 + 2)
                nc.gpsimd.tensor_copy(q[:, :, :], qo[:, at(h * 2 + 2, 2), :]).then_inc(q_in, 1)
                pool.wait_ge(po_full, h * 4 + 4)
                nc.gpsimd.tensor_copy(vh[:, :, :].rearrange("p m c -> p (m c)"),
                                      v[:, at(h + 1), :].rearrange("p a c -> p (a c)")).then_inc(v_in, 1)

        @block.tensor
        def _(pe):
            def scores(h, s):
                if s == 0:
                    pe.wait_ge(q_in, h + 1)
                pe.wait_ge(exp_done, h * 2 + (s + 1))
                for i in range(4):
                    for a in range(2):
                        last = nc.tensor.matmul(x[s][:, i * MEM:(i + 1) * MEM],
                                                q[:, a, (4 * s + i) * P:(4 * s + i + 1) * P],
                                                k[:, at(h), a * MEM:(a + 1) * MEM].rearrange("p a m -> p (a m)"),
                                                start=(a == 0), stop=(a == 1))
                last.then_inc(s_full, 1)

            def values(h, s):
                pe.wait_ge(probs_ready, h * 2 + (s + 1))
                for m in range(2):
                    pe.wait_ge(pt_taken, h * 4 + (2 * s + m + 1))
                    for i in range(4):
                        last = nc.tensor.transpose(pt[m][:, i, :], pr[s][:, i, m * P:(m + 1) * P],
                                                   consts["ident"][:, :])
                    last.then_inc(pt_full, 1)
                if s == 0:
                    pe.wait_ge(v_in, h + 1)
                pe.wait_ge(pt_taken, h * 4 + (2 * s + 4))
                for a in range(2):
                    pe.wait_ge(po_taken, h * 4 + (2 * s + a + 1))
                    for m in range(2):
                        last = nc.tensor.matmul(po[a][:, :], vh[:, m, a * P:(a + 1) * P], prT[:, m, :],
                                                start=(m == 0), stop=(m == 1))
                    last.then_inc(po_full, 1)

            def head(h, more):
                scores(h, 1)
                values(h, 0)
                if more:
                    scores(h + 1, 0)
                values(h, 1)

            scores(0, 0)
            each_head(pe, head)

        @block.scalar
        def _(act):
            def exps(h, s):
                act.wait_ge(max_ready, h * 2 + (s + 1))
                for i in range(4):
                    last = nc.scalar.activation(pr[s][:, i, :], x[s][:, i * MEM:(i + 1) * MEM], ACT.Exp,
                                                bias=mx[:, s, i:i + 1], scale=scale, accum_out=rsum[:, s, i:i + 1])
                last.then_inc(exp_done, 1)

            def transposed(h, s):
                for m in range(2):
                    act.wait_ge(pt_full, h * 4 + (2 * s + m + 1))
                    act.wait_ge(po_taken, h * 4 + (2 * s + 2))
                    nc.scalar.activation(prT[:, m, :], pt[m][:, :, :].rearrange("p a b -> p (a b)"),
                                         ACT.Copy).then_inc(pt_taken, 1)

            def head(h, more):
                transposed(h, 0)
                exps(h, 1)
                transposed(h, 1)
                if more:
                    exps(h + 1, 0)

            act.nop().then_inc(exp_done, 2)
            act.nop().then_inc(pt_taken, 2)
            exps(0, 0)
            each_head(act, head)

        @block.vector
        def _(dve):
            def maxima(h, s):
                dve.drain()
                dve.wait_ge(s_full, h * 2 + (s + 1))
                nc.vector.tensor_reduce(mx[:, s, :], x[s][:, :].rearrange("p (i m) -> p i m", m=MEM), AX.X, ALU.max)
                dve.drain()
                nc.vector.tensor_scalar(mx[:, s, :], mx[:, s, :], -scale, None, ALU.mult).then_inc(max_ready, 1)

            def normalize(h, s):
                dve.wait_ge(exp_done, h * 2 + (s + 3))
                nc.vector.reciprocal(rsum[:, s, :], rsum[:, s, :])
                dve.drain()
                nc.vector.tensor_tensor(pr[s][:, :, :], pr[s][:, :, :],
                                        rsum[:, s, :].unsqueeze(2).broadcast_to([P, 4, MEM]),
                                        ALU.mult).then_inc(probs_ready, 1)

            def outputs(h, s):
                for a in range(2):
                    dve.wait_ge(po_full, h * 4 + (2 * s + a + 1))
                    nc.vector.tensor_copy(qo[:, at(h * 2 + a), s * HALF:(s + 1) * HALF].rearrange(
                        "p a t -> p (a t)"), po[a][:, :]).then_inc(po_taken, 1)

            def head(h, more):
                normalize(h, 0)
                maxima(h, 1)
                outputs(h, 0)
                normalize(h, 1)
                if more:
                    maxima(h + 1, 0)
                outputs(h, 1)

            dve.nop().then_inc(po_taken, 2)
            maxima(0, 0)
            each_head(dve, head)


def expert_scores_stage(nc, consts, h, w_query, keys_d, scores_d, high, low, rstd):
    n_tiles = 2 * PH
    with Stage(nc, "score") as st:
        x = SplitInput(nc, st, consts, h, "ffn", high, low, rstd)
        proj = Projection(nc, st, w_query, n_tiles, x)
        keys = st.sb("keys", [P, n_tiles, NK])
        q = [st.sb(f"q{i}", [P, T]) for i in range(2)]
        s = [st.sb(f"s{i}", [P, NT, NK]) for i in range(2)]
        ss = st.psum("ss", [P, NT, NK])
        stored = [st.sem(f"stored{i}") for i in range(2)]
        by_head = scores_d.rearrange("(h t) p w k -> h p w t k", h=PH)
        keys_ready, s_mm, s_ready = st.sem("keys_ready"), st.sem("s_mm"), st.sem("s_ready")
        block = st.block()

        @block.sync
        def _(sp):
            proj.first_loads(sp)
            sp.dma_start(keys[:, :, :], keys_d).then_inc(keys_ready, 16)
            with sp.Fori(1, n_tiles // 2) as g:
                for i in range(2):
                    sp.wait_ge(proj.w_low, g * 2 + (i - 1))
                    sp.dma_start(proj.raw[i][:, :], w_query[bass.ds(g * 2 + i, 1)].rearrange("a p n -> (a p) n")
                                 ).then_inc(proj.w_ready[i], 16)
                    sp.wait_ge(s_ready, g * 2 + i)
                    sp.dma_start(by_head[bass.ds(g - 1, 1), :, i].rearrange("h p t k -> (h p) t k"),
                                 s[i][:, :, :]).then_inc(stored[i], 16)
            for i in range(2):
                sp.wait_ge(s_ready, n_tiles + i)
                sp.dma_start(by_head[PH - 1, :, i], s[i][:, :, :]).then_inc(stored[i], 16)
                sp.wait_ge(stored[i], 16 * (PH + 1))

        @block.gpsimd
        def _(pool):
            x.squares(pool)

        @block.tensor
        def _(pe):
            def scores(i, tile):
                if isinstance(tile, int) and tile == 0:
                    pe.wait_ge(keys_ready, 16)
                pe.wait_ge(proj.taken, tile + 3)
                pe.wait_ge(s_ready, tile + 1)
                at = slice(tile, tile + 1) if isinstance(tile, int) else bass.ds(tile, 1)
                for t in range(NT):
                    last = nc.tensor.matmul(ss[:, t, :], q[i][:, t * P:(t + 1) * P],
                                            keys[:, at, :].rearrange("p a k -> p (a k)"), start=True, stop=True)
                last.then_inc(s_mm, 1)

            pe.nop().then_inc(s_mm, 2)
            proj.products(pe, scores)
            scores(1, n_tiles - 1)

        @block.scalar
        def _(act):
            def scores(i, tile):
                act.wait_ge(s_mm, tile + 3)
                act.wait_ge(stored[i], (tile - i) * 8 + 16)
                nc.scalar.activation(s[i][:, :, :], ss[:, :, :], ACT.Copy).then_inc(s_ready, 1)

            act.nop().then_inc(s_ready, 1)
            for i in range(2):
                act.nop().then_inc(stored[i], 16)
            proj.first_highs(act)
            proj.highs(act, lambda i, tile: scores(i, tile - 2))
            scores(0, n_tiles - 2)
            scores(1, n_tiles - 1)

        @block.vector
        def _(dve):
            proj.first_lows(dve)

            def take(i, tile):
                dve.wait_ge(s_mm, tile + 1)
                nc.vector.tensor_tensor(q[i][:, :], proj.product(i), x.rstd[:, :], ALU.mult).then_inc(proj.taken, 1)

            proj.takes(dve, take)


def experts_in_stage(nc, consts, high, low, rstd, expert_u, scores_d, hidden_d, gates_d):
    LOW = -3.0e38
    heads = NT * PH
    with Stage(nc, "xin") as st:
        raw = [st.sb(f"raw{i}", [P, KC * P]) for i in range(2)]
        uh = [st.sb(f"uh{i}", [P, KC * P], F32R) for i in range(2)]
        ul = [st.sb(f"ul{i}", [P, KC * P], F32R) for i in range(2)]
        hid = [st.sb(f"hid{i}", [P, T]) for i in range(2)]
        ps = [st.psum(f"ps{i}", [P, 2, HALF]) for i in range(2)]
        pre = [st.sb(f"pre{i}", [P, T]) for i in range(2)]
        pre_ready = st.sem("pre_ready")
        sc, scw = st.sb("sc", [P, 2, NK]), st.sb("scw", [P, 2, NK])
        vals, ix, ixf = st.sb("vals", [P, 2, TOPK]), st.sb("ix", [P, 2, TOPK], U32), st.sb("ixf", [P, 2, TOPK])
        cand, candw, cv = st.sb("cand", [P, TOPK, TOPK]), st.sb("candw", [P, TOPK * TOPK]), st.sb("cv", [P, TOPK])
        ci, place, placef = st.sb("ci", [P, TOPK], U32), st.sb("place", [P, 2, TOPK], U32), st.sb("placef", [P, 2, TOPK])
        sel, e12, flat_e = st.sb("sel", [P, 2, TOPK, TOPK]), st.sb("e12", [P, 2, TOPK]), st.sb("flat_e", [P, TOPK])
        iota_i, iota = st.sb("iota_i", [P, TOPK], I32), st.sb("iota", [P, TOPK])
        tok_i, tok, wrap = st.sb("tok_i", [P, 1], I32), st.sb("tok", [P, 1]), st.sb("wrap", [P, 1])
        idx, gates = st.sb("idx", [P, TOPK], U32), st.sb("gates", [P, TOPK])
        gexp, nmax, gsum = st.sb("gexp", [P, TOPK]), st.sb("nmax", [P, 1]), st.sb("gsum", [P, 1])
        raw_ready = [st.sem(f"raw_ready{i}") for i in range(2)]
        stored = [st.sem(f"stored{i}") for i in range(2)]
        high_done, low_done, mm_done, gelu_done = (st.sem(x) for x in ("high_done", "low_done", "mm_done", "gelu_done"))
        sc_ready, sc_used, cv_ready, gate_exp = (st.sem(x) for x in ("sc_ready", "sc_used", "cv_ready", "gate_exp"))
        idx_ready, added, iota_ready = st.sem("idx_ready"), st.sem("added"), st.sem("iota_ready")
        block = st.block()
        gates_flat = gates_d.rearrange("j i t -> (j i t)").unsqueeze(1)

        @block.sync
        def _(sp):
            for i in range(2):
                sp.dma_start(raw[i][:, :], expert_u[i]).then_inc(raw_ready[i], 16)
            sp.dma_start(sc[:, :, :], scores_d[0]).then_inc(sc_ready, 16)
            with sp.Fori(1, NK // 2) as g:
                for i in range(2):
                    sp.wait_ge(low_done, g * 2 + (i - 1))
                    sp.dma_start(raw[i][:, :], expert_u[bass.ds(g * 2 + i, 1)].rearrange("a p n -> (a p) n")
                                 ).then_inc(raw_ready[i], 16)
                    if i == 0:
                        sp.wait_ge(sc_used, g)
                        sp.dma_start(sc[:, :, :], scores_d[bass.ds(g, 1)].rearrange("a p w k -> (a p) w k")
                                     ).then_inc(sc_ready, 16)
                    sp.wait_ge(gelu_done, g * 2 + (i + 1))
                    sp.dma_start(hidden_d[bass.ds(g * 2 + (i - 2), 1)].rearrange("a p t -> (a p) t"), hid[i][:, :]
                                 ).then_inc(stored[i], 16)
            for i in range(2):
                sp.wait_ge(gelu_done, NK + 1 + i)
                sp.dma_start(hidden_d[NK - 2 + i], hid[i][:, :]).then_inc(stored[i], 16)
                sp.wait_ge(stored[i], 16 * (NK // 2 + 1))

        @block.tensor
        def _(pe):
            with pe.Fori(0, NK // 2) as g:
                for i in range(2):
                    pe.wait_ge(low_done, g * 2 + (i + 1))
                    pe.wait_ge(pre_ready, g * 2 + (i + 1))
                    for kc in range(KC):
                        cols = slice(kc * P, kc * P + P)
                        for w, x in ((uh[i], high), (uh[i], low), (ul[i], high)):
                            for h in range(2):
                                last = nc.tensor.matmul(ps[i][:, h, :], w[:, cols], x[:, kc, h * HALF:(h + 1) * HALF],
                                                        start=(kc == 0 and w is uh[i] and x is high),
                                                        stop=(kc == KC - 1 and w is ul[i]))
                    last.then_inc(mm_done, 1)

        @block.scalar
        def _(act):
            def high_part(i, k):
                act.wait_ge(raw_ready[i], k)
                nc.scalar.activation(uh[i][:, :], raw[i][:, :], ACT.Copy).then_inc(high_done, 1)

            def gelu(i, done, free):
                act.wait_ge(pre_ready, done + 2)
                act.wait_ge(stored[i], free)
                nc.scalar.activation(hid[i][:, :], pre[i][:, :], ACT.Gelu).then_inc(gelu_done, 1)

            def gate(k):
                act.wait_ge(cv_ready, k)
                nc.scalar.activation(gexp[:, :], cv[:, :], ACT.Exp, bias=nmax[:, :],
                                     accum_out=gsum[:, :]).then_inc(gate_exp, 1)

            high_part(0, 16)
            high_part(1, 16)
            gate(1)
            with act.Fori(1, NK // 2) as g:
                for i in range(2):
                    act.wait_ge(mm_done, g * 2 + (i - 1))
                    high_part(i, g * 16 + 16)
                    gelu(i, g * 2 + (i - 1), g * 16)
                gate(g + 1)
            for i in range(2):
                gelu(i, NK - 1 + i, 16 * (NK // 2))

        @block.gpsimd
        def _(pool):
            nc.gpsimd.iota(iota_i[:, :], [[1, TOPK]], base=0, channel_multiplier=0).then_inc(iota_ready, 1)
            nc.gpsimd.iota(tok_i[:, :], [[1, 1]], base=0, channel_multiplier=1).then_inc(iota_ready, 1)
            found = pool.alloc_register("found")
            with pool.Fori(0, heads) as n:
                pool.reg_mov(found, n + 1)
                pool.wait_ge(iota_ready, 1)
                pool.wait_ge(idx_ready, found)
                for k in range(TOPK):
                    if k:
                        pool.wait_ge(iota_ready, 1)
                    pool.indirect_dma_start(gates_flat, bass.IndirectOffsetOnAxis(ap=idx[:, k:k + 1], axis=0),
                                            gates[:, k:k + 1], None, compute_op=ALU.add).then_inc(added, 16)
            pool.wait_ge(added, 16 * TOPK * heads)

        @block.vector
        def _(dve):
            def low_part(i, k):
                dve.wait_ge(high_done, k)
                nc.vector.tensor_tensor(ul[i][:, :], raw[i][:, :], uh[i][:, :].bitcast(F32),
                                        ALU.subtract).then_inc(low_done, 1)

            def scale_product(i, done):
                dve.wait_ge(mm_done, done)
                dve.wait_ge(gelu_done, done)
                nc.vector.tensor_tensor(pre[i][:, :], ps[i][:, :, :].rearrange("p a t -> p (a t)"), rstd[:, :],
                                        ALU.mult).then_inc(pre_ready, 1)

            def best_keys(k):
                dve.drain()
                dve.wait_ge(sc_ready, k * 16)
                nc.vector.memset(wrap[:, :], 0.0)
                dve.drain()
                for w in range(2):
                    nc.vector.max(vals[:, w, 0:8], sc[:, w, :])
                dve.drain()
                for w in range(2):
                    nc.vector.max_index(ix[:, w, 0:8], vals[:, w, 0:8], sc[:, w, :])
                    last = nc.vector.match_replace(scw[:, w, :], vals[:, w, 0:8], sc[:, w, :], LOW)
                last.then_inc(sc_used, 1)
                dve.drain()
                for w in range(2):
                    nc.vector.max(vals[:, w, 8:16], scw[:, w, :])
                dve.drain()
                for w in range(2):
                    nc.vector.max_index(ix[:, w, 8:16], vals[:, w, 8:16], scw[:, w, :])
                nc.vector.tensor_tensor(cand[:, :, :], vals[:, 0, :].unsqueeze(2).broadcast_to([P, TOPK, TOPK]),
                                        vals[:, 1, :].unsqueeze(1).broadcast_to([P, TOPK, TOPK]), ALU.add)

            def best_pairs(k, first=False):
                dve.drain()
                flat = cand[:, :, :].rearrange("p a b -> p (a b)")
                nc.vector.max(cv[:, 0:8], flat)
                nc.vector.tensor_copy(ixf[:, :, :], ix[:, :, :])
                dve.drain()
                nc.vector.tensor_scalar(nmax[:, :], cv[:, 0:1], -1.0, None, ALU.mult)
                nc.vector.max_index(ci[:, 0:8], cv[:, 0:8], flat)
                nc.vector.match_replace(candw[:, :], cv[:, 0:8], flat, LOW)
                dve.drain()
                nc.vector.max(cv[:, 8:16], candw[:, :]).then_inc(cv_ready, 1)
                dve.drain()
                nc.vector.max_index(ci[:, 8:16], cv[:, 8:16], candw[:, :])
                dve.drain()
                nc.vector.tensor_scalar(place[:, 0, :], ci[:, :], 4, None, ALU.logical_shift_right)
                nc.vector.tensor_scalar(place[:, 1, :], ci[:, :], 15, None, ALU.bitwise_and)
                dve.drain()
                nc.vector.tensor_copy(placef[:, :, :], place[:, :, :])
                dve.drain()
                nc.vector.tensor_tensor(sel[:, :, :, :], placef[:, :, :].unsqueeze(3).broadcast_to([P, 2, TOPK, TOPK]),
                                        iota[:, :].unsqueeze(1).unsqueeze(1).broadcast_to([P, 2, TOPK, TOPK]),
                                        ALU.is_equal)
                dve.drain()
                nc.vector.tensor_tensor(sel[:, :, :, :], sel[:, :, :, :],
                                        ixf[:, :, :].unsqueeze(2).broadcast_to([P, 2, TOPK, TOPK]), ALU.mult)
                dve.drain()
                nc.vector.tensor_reduce(e12[:, :, :], sel[:, :, :, :], AX.X, ALU.add)
                dve.drain()
                nc.vector.scalar_tensor_tensor(out=flat_e[:, :], in0=e12[:, 1, :], scalar=float(NK), in1=e12[:, 0, :],
                                               op0=ALU.mult, op1=ALU.add)
                dve.wait_ge(gate_exp, k)
                nc.vector.reciprocal(gsum[:, :], gsum[:, :])
                dve.drain()
                if not first:
                    dve.wait_ge(added, (k - 1) * (16 * TOPK))
                nc.vector.tensor_scalar(gates[:, :], gexp[:, :], gsum[:, :], None, ALU.mult)
                nc.vector.tensor_scalar(idx[:, :], flat_e[:, :], float(T), tok[:, :], ALU.mult,
                                        ALU.add).then_inc(idx_ready, 1)
                dve.drain()
                nc.vector.tensor_scalar(tok[:, :], tok[:, :], float(P), None, ALU.add)
                dve.drain()
                nc.vector.tensor_scalar(wrap[:, :], tok[:, :], float(T), -float(T), ALU.is_ge, ALU.mult)
                dve.drain()
                nc.vector.tensor_tensor(tok[:, :], tok[:, :], wrap[:, :], ALU.add)

            dve.wait_ge(iota_ready, 2)
            nc.vector.tensor_copy(iota[:, :], iota_i[:, :])
            nc.vector.tensor_copy(tok[:, :], tok_i[:, :])
            dve.nop().then_inc(gelu_done, 2)
            dve.nop().then_inc(pre_ready, 2)
            for i in range(2):
                dve.nop().then_inc(stored[i], 16)
            low_part(0, 1)
            low_part(1, 2)
            best_keys(1)
            best_pairs(1, first=True)
            with dve.Fori(1, NK // 2) as g:
                scale_product(0, g * 2 - 1)
                low_part(0, g * 2 + 1)
                best_keys(g + 1)
                scale_product(1, g * 2)
                low_part(1, g * 2 + 2)
                best_pairs(g + 1)
            scale_product(0, NK - 1)
            scale_product(1, NK)


def experts_out_stage(nc, hT, expert_v, hidden_d, gates_d):
    G = 4
    groups = NK // G
    with Stage(nc, "xout") as st:
        hid = [st.sb(f"hid{i}", [P, T]) for i in range(2)]
        gat = [st.sb(f"gat{i}", [P, T]) for i in range(2)]
        val = [st.sb(f"val{i}", [P, D]) for i in range(2)]
        ah, al, vh, vl = (st.sb(x, [P, 2 * G, T], F32R) for x in ("ah", "al", "vh", "vl"))
        ps = [st.psum(f"ps{i}", [P, 2, HALF]) for i in range(4)]
        in_ready = [st.sem(f"in_ready{i}") for i in range(2)]
        product, act_high, val_high, split_done = (st.sem(x) for x in ("product", "act_high", "val_high", "split_done"))
        group_done, pair_done, added = st.sem("group_done"), st.sem("pair_done"), st.sem("added")
        block = st.block()

        def each_group(eng, body):
            with eng.Fori(0, groups // 2 - 1) as gg:
                body(gg * 2, 0, True)
                body(gg * 2 + 1, 1, True)
            body(groups - 2, 0, True)
            body(groups - 1, 1, False)

        @block.sync
        def _(sp):
            def load(c, r, index):
                sp.dma_start(val[r][:, :], index(expert_v)).then_inc(in_ready[r], 16)
                sp.dma_start(hid[r][:, :], index(hidden_d)).then_inc(in_ready[r], 16)
                sp.dma_start(gat[r][:, :], index(gates_d)).then_inc(in_ready[r], 16)

            for c in range(2):
                load(c, c, lambda x: x[c])
            with sp.Fori(1, NK // 2) as cc:
                for r in range(2):
                    sp.wait_ge(split_done, cc * 2 + (r - 1))
                    load(cc * 2 + r, r, lambda x: x[bass.ds(cc * 2 + r, 1)].rearrange("a p t -> (a p) t"))

        @block.tensor
        def _(pe):
            def group(g, parity, more):
                pe.wait_ge(split_done, g * G + G)
                for f in range(KC):
                    out = ps[f % 4]
                    pe.wait_ge(added, g * KC + (f + 1))
                    for s in range(G):
                        n = parity * G + s
                        for w, x in ((vh, ah), (vh, al), (vl, ah)):
                            for h in range(2):
                                last = nc.tensor.matmul(out[:, h, :], w[:, n, f * P:(f + 1) * P],
                                                        x[:, n, h * HALF:(h + 1) * HALF],
                                                        start=(s == 0 and w is vh and x is ah),
                                                        stop=(s == G - 1 and w is vl))
                    last.then_inc(pair_done, 1)

            each_group(pe, group)

        @block.scalar
        def _(act):
            def highs(c, n):
                act.wait_ge(in_ready[n % 2], (c - n % 2) * 24 + 48)
                nc.scalar.activation(vh[:, n, :], val[n % 2][:, :], ACT.Copy).then_inc(val_high, 1)
                act.wait_ge(product, c + 1)
                nc.scalar.activation(ah[:, n, :], hid[n % 2][:, :], ACT.Copy).then_inc(act_high, 1)

            for s in range(G):
                highs(s, s)

            def group(g, parity, more):
                if not more:
                    return
                act.wait_ge(added, g * KC + 4)
                for s in range(G):
                    highs(g * G + (G + s), (1 - parity) * G + s)

            each_group(act, group)

        @block.vector
        def _(dve):
            def multiply(c, r):
                dve.wait_ge(in_ready[r], (c - r) * 24 + 48)
                nc.vector.tensor_tensor(hid[r][:, :], hid[r][:, :], gat[r][:, :], ALU.mult).then_inc(product, 1)

            def lows(c, n):
                dve.wait_ge(val_high, c + 1)
                nc.vector.tensor_tensor(vl[:, n, :], val[n % 2][:, :], vh[:, n, :].bitcast(F32), ALU.subtract)
                dve.wait_ge(act_high, c + 1)
                nc.vector.tensor_tensor(al[:, n, :], hid[n % 2][:, :], ah[:, n, :].bitcast(F32),
                                        ALU.subtract).then_inc(split_done, 1)

            dve.nop().then_inc(added, 4)
            for s in range(G):
                multiply(s, s % 2)
                dve.drain()
                lows(s, s)

            def group(g, parity, more):
                for f in range(KC):
                    if more and f % 2 == 0:
                        multiply(g * G + (G + f // 2), (f // 2) % 2)
                    dve.drain()
                    dve.wait_ge(pair_done, g * KC + (f + 1))
                    nc.vector.tensor_tensor(hT[:, f, :], hT[:, f, :], ps[f % 4][:, :, :].rearrange("p a t -> p (a t)"),
                                            ALU.add).then_inc(added, 1)
                    if more and f % 2 == 0:
                        lows(g * G + (G + f // 2), (1 - parity) * G + f // 2)

            each_group(dve, group)


def store_stage(nc, src, out):
    with Stage(nc, "store") as st:
        stored = st.sem("stored")
        block = st.block()

        @block.sync
        def _(sp):
            sp.dma_start(out.rearrange("(k p) t -> p k t", p=P), src[:, :, :]).then_inc(stored, 16)
            sp.wait_ge(stored, 16)


def build(nc, a, out):
    with ExitStack() as ctx:
        def sb(name, shape, dt=F32):
            return ctx.enter_context(nc.sbuf_tensor(name, shape, dt))

        consts = {"cols": sb("cols", [P, NCOLS]), "ones": sb("ones", [P, P]), "eps": sb("eps", [P, 2]),
                  "ident": sb("ident", [P, P]), "headones": sb("headones", [P, P]), "rot": sb("rot", [ROPE, P]),
                  "mask4": sb("mask4", [P, 4, P]), "level": sb("level", [P, 6, P]), "lower": sb("lower", [P, P]),
                  "upper0": sb("upper0", [P, P]), "scanmask": sb("scanmask", [P, 4 * P])}
        feats_d = nc.dram_tensor("feats_d", (NF, P, T), F32).ap()
        scores_d = nc.dram_tensor("scores_d", (NT * PH, P, 2, NK), F32).ap()
        hidden_d = nc.dram_tensor("hidden_d", (NK, P, T), F32).ap()
        gates_d = nc.dram_tensor("gates_d", (NK, P, T), F32).ap()
        build_constants(nc, consts, a["cols"])
        lower = sb("act_lower", [P, KC, T])
        project_in_stage(nc, consts, a["x"], lower, a["w_in"], feats_d)
        with ExitStack() as mla:
            feats = mla.enter_context(nc.sbuf_tensor("feats", [P, 3, T], F32))
            cos = mla.enter_context(nc.sbuf_tensor("cos", [ROPE, T], F32))
            sin = mla.enter_context(nc.sbuf_tensor("sin", [ROPE, T], F32))
            krope = mla.enter_context(nc.sbuf_tensor("krope", [ROPE, T], F32))
            mla_prepare_stage(nc, consts, feats, feats_d, a["positions"], cos, sin, krope)
            mla_stage(nc, consts, feats, cos, sin, krope, lower, a["w_uq"], a["w_ukv"], gates_d)
        rwkv_stage(nc, consts, feats_d, a["rw_w_up"], a["rw_a_up"], a["rw_g_up"], lower)
        with ExitStack() as late:
            upper = late.enter_context(nc.sbuf_tensor("act_upper", [P, KC, T], F32))
            k = late.enter_context(nc.sbuf_tensor("k", [P, XH, 2 * MEM], F32))
            v = late.enter_context(nc.sbuf_tensor("v", [P, XH, 2 * MEM], F32))
            residual_stage(nc, consts, "out", a["w_out"], lower, upper, upper, load=a["x"])
            with ExitStack() as memory:
                memn = memory.enter_context(nc.sbuf_tensor("memn", [P, KC, MEM], F32))
                norm_stage(nc, consts, "nmem", memn, "mem", memn, MEM, load=a["mem"])
                memory_stage(nc, memn, a["xa_wk"], a["xa_wv"], k, v)
            queries_stage(nc, consts, upper, a["xa_wq"], lower)
            cross_attention_stage(nc, consts, lower, k, v)
            residual_stage(nc, consts, "xo", a["xa_wo"], lower, upper, lower)
        with ExitStack() as deep:
            high = deep.enter_context(nc.sbuf_tensor("high", [P, KC, T], F32R))
            low = deep.enter_context(nc.sbuf_tensor("low", [P, KC, T], F32R))
            rstd = deep.enter_context(nc.sbuf_tensor("rstd", [P, T], F32))
            expert_scores_stage(nc, consts, lower, a["peer_wq"], a["peer_keys"], scores_d, high, low, rstd)
            experts_in_stage(nc, consts, high, low, rstd, a["expert_u"], scores_d, hidden_d, gates_d)
        experts_out_stage(nc, lower, a["expert_v"], hidden_d, gates_d)
        with ExitStack() as last:
            normed = last.enter_context(nc.sbuf_tensor("normed_out", [P, KC, T], F32))
            norm_stage(nc, consts, "nfin", lower, "fin", normed, T)
            store_stage(nc, normed, out)


def layout(inputs):
    def blocks(w, n):
        k = w.shape[0] // P
        return np.ascontiguousarray(w.reshape(k, P, w.shape[1] // n, n).transpose(2, 1, 0, 3))

    def tiles(w):
        return blocks(w, P).reshape(-1, P, KC * P)

    def vec(name, rows=P):
        return np.asarray(inputs[name]).reshape(-1, rows).T

    a = {k: np.asarray(v) for k, v in inputs.items()}
    w_in = a["w_in"][0]
    m = Q_LORA + KV_LORA
    r = m + ROPE
    out = {"x": np.ascontiguousarray(a["x"][0].T).reshape(KC, P, T)}
    out["positions"] = a["positions"]
    out["w_in"] = tiles(np.concatenate([w_in[:, 0:m], w_in[:, r:r + 3 * RW], w_in[:, r + 3 * RW + 128:],
                                        w_in[:, m:r], w_in[:, r + 3 * RW:r + 3 * RW + 128],
                                        np.zeros((D, 64), np.float32)], 1))
    cols = np.zeros((P, NCOLS), np.float32)

    def put(name, part):
        cols[0:part.shape[0], COLS[name]:COLS[name] + part.shape[1]] = part

    for name, key in (("mix", "norm_mix_g"), ("xa", "norm_xa_g"), ("mem", "norm_mem_g"), ("ffn", "norm_ffn_g"),
                      ("w0", "rw_w0"), ("a0", "rw_a0"), ("kk", "rw_k_k"), ("ka", "rw_k_a"), ("rk", "rw_r_k"),
                      ("lnw", "rw_lnx_w"), ("lnb", "rw_lnx_b"), ("qg", "q_norm_g"), ("kvg", "kv_norm_g"),
                      ("fin", "final_norm_g")):
        put(name, vec(key))
    mu = a["shift_mu"][0]
    cols[:, COLS["mu"] + RT:COLS["mu"] + GT] = mu[0:3 * RW].reshape(-1, P).T
    cols[:, COLS["mu"] + GT] = mu[3 * RW + 128:]
    cols[64:, COLS["mu"] + KRWD] = mu[3 * RW:3 * RW + 64]
    cols[0:64, COLS["mu"] + AD] = mu[3 * RW + 64:3 * RW + 128]
    half = np.float32(10000.0) ** (-np.arange(0, ROPE, 2, dtype=np.float32) / np.float32(ROPE))
    cols[0:ROPE, COLS["inv"]] = np.concatenate([half, half])
    out["cols"] = cols
    out["w_uq"] = blocks(a["w_uq"][0], P + ROPE)
    out["w_ukv"] = np.ascontiguousarray(a["w_ukv"][0].reshape(P, MLA_HEADS, 2 * P).transpose(1, 0, 2))
    for name in ("rw_w_up", "rw_a_up", "rw_g_up"):
        out[name] = a[name][0]
    for name in ("w_out", "xa_wq", "xa_wo", "peer_wq"):
        out[name] = tiles(a[name][0])
    out["xa_wk"], out["xa_wv"] = (blocks(a[x][0], D // XH) for x in ("xa_wk", "xa_wv"))
    out["mem"] = np.ascontiguousarray(a["mem"][0].T).reshape(KC, P, MEM)
    out["peer_keys"] = np.ascontiguousarray(a["peer_keys"][0].reshape(2 * PH, NK, P).transpose(2, 0, 1))
    out["expert_u"] = np.ascontiguousarray(a["expert_u"][0].reshape(NK, NK, KC, P).transpose(1, 3, 2, 0)).reshape(
        NK, P, KC * P)
    out["expert_v"] = np.ascontiguousarray(a["expert_v"][0].reshape(NK, NK, D).transpose(1, 0, 2))
    return out


def kernel(**inputs):
    import concourse.bacc as bacc
    from concourse.bass_utils import run_bass_kernel_spmd

    nc = bacc.Bacc("TRN2", target_bir_lowering=False, num_devices=1)
    arrays, aps = {}, {}
    for name, arr in layout(inputs).items():
        arrays[f"in_{name}"] = arr
        aps[name] = nc.dram_tensor(f"in_{name}", arr.shape, mybir.dt.from_np(arr.dtype), kind="ExternalInput").ap()
    out = nc.dram_tensor("out_0", (T, D), F32, kind="ExternalOutput").ap()
    build(nc, aps, out)
    r = run_bass_kernel_spmd(nc, [arrays], core_ids=[0])
    return np.ascontiguousarray(r.results[0]["out_0"].T).reshape(1, T, D)
```

```python
from contextlib import ExitStack

import concourse.bass as bass
import numpy as np
from concourse import mybir

F32 = mybir.dt.float32
F32R = mybir.dt.float32r
I32 = mybir.dt.int32
U32 = mybir.dt.uint32
ALU = mybir.AluOpType
ACT = mybir.ActivationFunctionType
AX = mybir.AxisListType

P = 128
D = 1024
T = 1024
KC = D // P
NT = T // P
HALF = 512
EPS = 1e-6

MLA_HEADS = 4
ROPE = 64
Q_LORA = 256
KV_LORA = 128
RW = 512
PAIRS = 4
CH = 64
LNX_EPS = 64e-5
MEM = 256
XH = 4
PH = 8
NK = 128
TOPK = 16

CQ, CKV, RT, KT, VT, GT, KRWD, AD, NF = 0, 2, 3, 7, 11, 15, 16, 17, 18

COLS = {}
_at = 0
for _name, _n in (("mix", 8), ("xa", 8), ("mem", 8), ("ffn", 8), ("w0", 4), ("a0", 4), ("kk", 4), ("ka", 4),
                  ("rk", 4), ("lnw", 4), ("lnb", 4), ("qg", 2), ("kvg", 1), ("mu", NF),
                  ("inv", 1), ("fin", 8)):
    COLS[_name] = _at
    _at += _n
NCOLS = _at




class Stage:

    def __init__(self, nc, name):
        self.nc, self.name, self.stack, self.sems = nc, name, ExitStack(), []

    def __enter__(self):
        return self

    def __exit__(self, *e):
        done = self.stack.__exit__(*e)
        if e[0] is None:
            self.nc.clear_and_free_semaphores(self.sems)
            self.nc.all_engine_barrier()
        return done

    def sb(self, name, shape, dt=F32):
        return self.stack.enter_context(self.nc.sbuf_tensor(f"{self.name}_{name}", shape, dt))

    def psum(self, name, shape, dt=F32):
        return self.stack.enter_context(self.nc.psum_tensor(f"{self.name}_{name}", shape, dt))

    def sem(self, name):
        self.sems.append(self.nc.alloc_semaphore(f"{self.name}_{name}"))
        return self.sems[-1]

    def block(self):
        return self.stack.enter_context(self.nc.Block())


def col(consts, name, i=0, rows=P):
    c = COLS[name] + i
    return consts["cols"][0:rows, c:c + 1]


def cols_over(consts, name, n, width):
    c = COLS[name]
    return consts["cols"][:, c:c + n].unsqueeze(2).broadcast_to([P, n, width])


def build_constants(nc, consts, cols_d):
    with Stage(nc, "const") as st:
        loaded, made = st.sem("loaded"), st.sem("made")
        block = st.block()

        @block.sync
        def _(sp):
            sp.dma_start(consts["cols"][:, :], cols_d).then_inc(loaded, 16)
            sp.wait_ge(loaded, 16)

        @block.gpsimd
        def _(pool):
            nc.gpsimd.memset(consts["ones"][:, :], 1.0)
            nc.gpsimd.memset(consts["eps"][:, 0:1], EPS)
            nc.gpsimd.memset(consts["eps"][:, 1:2], LNX_EPS).then_inc(made, 1)
            nc.gpsimd.memset(consts["ident"][:, :], 0.0).then_inc(made, 1)
            pool.wait_ge(made, 2)
            nc.gpsimd.affine_select(out=consts["ident"][:, :], in_=consts["ident"][:, :], compare_op=ALU.not_equal,
                                    fill=1.0, base=0, pattern=[[-1, P]], channel_multiplier=1).then_inc(made, 1)
            bd = consts["headones"]
            nc.gpsimd.memset(bd[:, :], 1.0).then_inc(made, 1)
            pool.wait_ge(made, 4)
            nc.gpsimd.memset(bd[0:64, 64:128], 0.0).then_inc(made, 1)
            nc.gpsimd.memset(bd[64:128, 0:64], 0.0).then_inc(made, 1)
            rot = consts["rot"]
            nc.gpsimd.memset(rot[:, :], 0.0).then_inc(made, 1)
            pool.wait_ge(made, 7)
            nc.gpsimd.affine_select(out=rot[:, 0:32], in_=rot[:, 0:32], compare_op=ALU.not_equal, fill=-1.0,
                                    base=-32, pattern=[[-1, 32]], channel_multiplier=1)
            nc.gpsimd.affine_select(out=rot[:, 32:64], in_=rot[:, 32:64], compare_op=ALU.not_equal, fill=1.0,
                                    base=0, pattern=[[-1, 32]], channel_multiplier=1).then_inc(made, 1)
            m4 = consts["mask4"]
            nc.gpsimd.memset(m4[:, 0:2, :], 1.0)
            nc.gpsimd.memset(m4[:, 3, :], 1.0).then_inc(made, 1)
            lv = consts["level"]
            nc.gpsimd.memset(lv[:, :, :], 1.0).then_inc(made, 1)
            low = consts["lower"]
            nc.gpsimd.memset(low[:, :], 1.0).then_inc(made, 1)
            nc.gpsimd.memset(m4[:, 2, :], 0.0).then_inc(made, 1)
            n = 12
            for i in (0, 1, 3):
                pool.wait_ge(made, n)
                nc.gpsimd.affine_select(out=m4[:, i, :], in_=m4[:, i, :], compare_op=ALU.is_ge, fill=0.0,
                                        base=-1 if i % 2 == 0 else 0, pattern=[[1, P]],
                                        channel_multiplier=-1).then_inc(made, 1)
                n += 1
                pool.wait_ge(made, n)
                nc.gpsimd.memset(m4[0:64, i, 64:128], 0.0).then_inc(made, 1)
                n += 1
            nc.gpsimd.affine_select(out=low[:, :], in_=low[:, :], compare_op=ALU.is_ge, fill=0.0, base=-1,
                                    pattern=[[-1, P]], channel_multiplier=1).then_inc(made, 1)
            n += 1
            pool.wait_ge(made, n)
            nc.gpsimd.memset(low[64:128, 0:64], 0.0).then_inc(made, 1)
            n += 1
            pool.wait_ge(made, n)
            for l in range(6):
                b = 1 << l
                v = lv[:, l, :].rearrange("p (j y) -> p j y", y=2 * b)
                nc.gpsimd.memset(v[:, :, b:2 * b], 0.0).then_inc(made, 1)
                n += 1
                pool.wait_ge(made, n)
                nc.gpsimd.affine_select(out=v[:, :, 0:b], in_=v[:, :, 0:b], compare_op=ALU.is_ge, fill=0.0,
                                        base=-b, pattern=[[-2 * b, P // (2 * b)], [0, b]],
                                        channel_multiplier=1).then_inc(made, 1)
                n += 1
                pool.wait_ge(made, n)
                nc.gpsimd.affine_select(out=v[:, :, 0:b], in_=v[:, :, 0:b], compare_op=ALU.is_ge, fill=0.0,
                                        base=2 * b - 1, pattern=[[2 * b, P // (2 * b)], [0, b]],
                                        channel_multiplier=-1).then_inc(made, 1)
                n += 1
                pool.wait_ge(made, n)
            v = m4[:, 2, :].rearrange("p (j y) -> p j y", y=2)[:, :, 1]
            nc.gpsimd.affine_select(out=v, in_=v, compare_op=ALU.not_equal, fill=-1.0, base=0,
                                    pattern=[[-2, 64]], channel_multiplier=1).then_inc(made, 1)
            sm = consts["scanmask"]
            nc.gpsimd.memset(sm[:, :], 1.0).then_inc(made, 1)
            n += 2
            pool.wait_ge(made, n)
            nc.gpsimd.memset(sm[:, :].rearrange("p (c t) -> p c t", t=CH)[:, :, 0:1], 0.0).then_inc(made, 1)


def norm_stage(nc, consts, name, src, gain, dst, width, load=None):
    halves = [(a, min(HALF, width - a)) for a in range(0, width, HALF)]
    with Stage(nc, name) as st:
        sq = st.sb("sq", [P, 2, width])
        std = st.sb("std", [P, width])
        sums = [st.psum(f"sums{i}", [P, HALF]) for i in range(len(halves))]
        loaded, sq_ready, sq_used = st.sem("loaded"), st.sem("sq_ready"), st.sem("sq_used")
        std_ready, rstd_ready = st.sem("std_ready"), st.sem("rstd_ready")
        block = st.block()

        @block.sync
        def _(sp):
            if load is not None:
                for kc in range(KC):
                    sp.dma_start(src[:, kc, :], load[kc]).then_inc(loaded, 16)

        @block.scalar
        def _(act):
            for kc in range(KC):
                if load is not None:
                    act.wait_ge(loaded, 16 * KC)
                if kc >= 2:
                    act.wait_ge(sq_used, kc - 1)
                nc.scalar.activation(sq[:, kc % 2, :], src[:, kc, :], ACT.Square).then_inc(sq_ready, 1)
            act.wait_ge(sq_used, KC)
            for i, (a, w) in enumerate(halves):
                nc.scalar.activation(std[:, a:a + w], sums[i][:, 0:w], ACT.Sqrt, bias=consts["eps"][:, 0:1],
                                     scale=1.0 / D).then_inc(std_ready, 1)

        @block.tensor
        def _(pe):
            for kc in range(KC):
                pe.wait_ge(sq_ready, kc + 1)
                for i, (a, w) in enumerate(halves):
                    last = nc.tensor.matmul(sums[i][:, 0:w], consts["ones"][:, :], sq[:, kc % 2, a:a + w],
                                            start=(kc == 0), stop=(kc == KC - 1))
                last.then_inc(sq_used, 1)

        @block.vector
        def _(dve):
            if load is not None:
                dve.wait_ge(loaded, 16 * KC)
            dve.wait_ge(std_ready, len(halves))
            nc.vector.reciprocal(std[:, :], std[:, :]).then_inc(rstd_ready, 1)
            dve.wait_ge(rstd_ready, 1)
            for kc in range(KC):
                nc.vector.scalar_tensor_tensor(out=dst[:, kc, :], in0=src[:, kc, :], scalar=col(consts, gain, kc),
                                               in1=std[:, :], op0=ALU.mult, op1=ALU.mult)


class SplitInput:

    def __init__(self, nc, st, consts, src, gain=None, high=None, low=None, rstd=None):
        self.nc, self.consts, self.src, self.gain = nc, consts, src, gain
        self.high = st.sb("high", [P, KC, T], F32R) if high is None else high
        self.low = st.sb("low", [P, KC, T], F32R) if low is None else low
        self.high_ready, self.low_ready = st.sem("high_ready"), st.sem("low_ready")
        if gain:
            self.scaled, self.sq = st.sb("scaled", [P, 2, T]), st.sb("sq", [P, 2, T])
            self.acc = st.sb("acc", [P, 2, T])
            self.rstd = st.sb("rstd", [P, T]) if rstd is None else rstd
            self.sums = st.psum("sums", [P, 2, HALF])
            self.scaled_ready, self.sq_ready, self.sq_summed = (st.sem(x) for x in ("scaled_ready", "sq_ready",
                                                                                   "sq_summed"))
            self.sq_added = st.sem("sq_added")
            self.std_ready, self.rstd_ready = st.sem("std_ready"), st.sem("rstd_ready")

    def part(self, kc):
        return self.scaled[:, kc % 2, :] if self.gain else self.src[:, kc, :]

    def highs(self, act, loaded=None):
        for kc in range(KC):
            if self.gain:
                act.wait_ge(self.scaled_ready, kc + 1)
            elif loaded is not None and kc == 0:
                act.wait_ge(loaded, 16)
            self.nc.scalar.activation(self.high[:, kc, :], self.part(kc), ACT.Copy).then_inc(self.high_ready, 1)
            if self.gain:
                if kc >= 2:
                    act.wait_ge(self.sq_added, kc // 2)
                self.nc.scalar.activation(self.sq[:, kc % 2, :], self.src[:, kc, :],
                                          ACT.Square).then_inc(self.sq_ready, 1)

    def std(self, act):
        act.wait_ge(self.sq_summed, KC // 2)
        self.nc.scalar.activation(self.rstd[:, :], self.sums[:, :, :].rearrange("p a t -> p (a t)"), ACT.Sqrt,
                                  bias=self.consts["eps"][:, 0:1], scale=1.0 / D).then_inc(self.std_ready, 1)

    def add_squares(self, pool):
        for m in range(KC // 2):
            pool.wait_ge(self.sq_ready, 2 * m + 2)
            if m >= 2:
                pool.wait_ge(self.sq_summed, m - 1)
            self.nc.gpsimd.tensor_tensor(self.acc[:, m % 2, :], self.sq[:, 0, :], self.sq[:, 1, :],
                                         ALU.add).then_inc(self.sq_added, 1)

    def sum_squares(self, pe, m):
        pe.wait_ge(self.sq_added, m + 1)
        for h in range(2):
            last = self.nc.tensor.matmul(self.sums[:, h, :], self.consts["ones"][:, :],
                                         self.acc[:, m % 2, h * HALF:(h + 1) * HALF],
                                         start=(m == 0), stop=(m == KC // 2 - 1))
        last.then_inc(self.sq_summed, 1)

    def lows(self, dve, loaded=None):
        for kc in range(KC + 1 if self.gain else KC):
            if self.gain and kc < KC:
                if loaded is not None:
                    dve.wait_ge(loaded[kc], 16)
                if kc >= 2:
                    dve.wait_ge(self.high_ready, kc - 1)
                    dve.drain()
                self.nc.vector.tensor_scalar(self.scaled[:, kc % 2, :], self.src[:, kc, :],
                                             col(self.consts, self.gain, kc), None,
                                             ALU.mult).then_inc(self.scaled_ready, 1)
            k = kc - 1 if self.gain else kc
            if k >= 0:
                dve.wait_ge(self.high_ready, k + 1)
                if self.gain:
                    dve.wait_ge(self.scaled_ready, k + 1)
                self.nc.vector.tensor_tensor(self.low[:, k, :], self.part(k), self.high[:, k, :].bitcast(F32),
                                             ALU.subtract).then_inc(self.low_ready, 1)

    def invert(self, dve):
        dve.wait_ge(self.std_ready, 1)
        self.nc.vector.reciprocal(self.rstd[:, :], self.rstd[:, :]).then_inc(self.rstd_ready, 1)
        dve.wait_ge(self.rstd_ready, 1)


class Projection:

    def __init__(self, nc, st, weights, n_tiles, x):
        self.nc, self.weights, self.n, self.x = nc, weights, n_tiles, x
        self.raw = [st.sb(f"raw{i}", [P, KC * P]) for i in range(2)]
        self.wh = [st.sb(f"wh{i}", [P, KC * P], F32R) for i in range(2)]
        self.wl = [st.sb(f"wl{i}", [P, KC * P], F32R) for i in range(2)]
        self.ps = [st.psum(f"ps{i}", [P, 2, HALF]) for i in range(2)]
        self.w_ready = [st.sem(f"w_ready{i}") for i in range(2)]
        self.w_high, self.w_low, self.mm_done, self.taken = (st.sem(x) for x in ("w_high", "w_low", "mm_done",
                                                                                "taken"))

    def product(self, i):
        return self.ps[i][:, :, :].rearrange("p a t -> p (a t)")

    def first_loads(self, sp):
        for i in range(2):
            sp.dma_start(self.raw[i][:, :], self.weights[i]).then_inc(self.w_ready[i], 16)

    def loads(self, sp, store=None):
        with sp.Fori(1, self.n // 2) as g:
            for i in range(2):
                sp.wait_ge(self.w_low, g * 2 + (i - 1))
                sp.dma_start(self.raw[i][:, :], self.weights[bass.ds(g * 2 + i, 1)].rearrange("a p n -> (a p) n")
                             ).then_inc(self.w_ready[i], 16)
                if store:
                    store(i, g * 2 + (i - 2))

    def high(self, act, i, k):
        act.wait_ge(self.w_ready[i], k)
        self.nc.scalar.activation(self.wh[i][:, :], self.raw[i][:, :], ACT.Copy).then_inc(self.w_high, 1)

    def low(self, dve, i, tile):
        dve.wait_ge(self.w_high, tile + 1)
        self.nc.vector.tensor_tensor(self.wl[i][:, :], self.raw[i][:, :], self.wh[i][:, :].bitcast(F32),
                                     ALU.subtract).then_inc(self.w_low, 1)

    def first_highs(self, act):
        self.high(act, 0, 16)
        self.x.highs(act)
        self.high(act, 1, 16)
        if self.x.gain:
            self.x.std(act)

    def highs(self, act, after=None):
        with act.Fori(1, self.n // 2) as g:
            for i in range(2):
                act.wait_ge(self.mm_done, g * 2 + (i - 1))
                self.high(act, i, g * 16 + 16)
                if after:
                    after(i, g * 2 + i)

    def first_lows(self, dve, loaded=None):
        dve.nop().then_inc(self.taken, 2)
        self.low(dve, 0, 0)
        self.x.lows(dve, loaded)
        self.low(dve, 1, 1)
        if self.x.gain:
            self.x.invert(dve)

    def takes(self, dve, take):
        with dve.Fori(0, self.n // 2 - 1) as g:
            for i in range(2):
                dve.drain()
                dve.wait_ge(self.mm_done, g * 2 + (i + 1))
                take(i, g * 2 + i)
                self.low(dve, i, g * 2 + (i + 2))
        for i in range(2):
            dve.drain()
            dve.wait_ge(self.mm_done, self.n - 1 + i)
            take(i, self.n - 2 + i)

    def products(self, pe, after=None):
        def tile(i, first=False, second=False):
            for kc in range(KC):
                if first:
                    pe.wait_ge(self.x.low_ready, kc + 1)
                cols = slice(kc * P, kc * P + P)
                for w, x in ((self.wh[i], self.x.high), (self.wh[i], self.x.low), (self.wl[i], self.x.high)):
                    for h in range(2):
                        last = self.nc.tensor.matmul(self.ps[i][:, h, :], w[:, cols],
                                                     x[:, kc, h * HALF:(h + 1) * HALF],
                                                     start=(kc == 0 and w is self.wh[i] and x is self.x.high),
                                                     stop=(kc == KC - 1 and w is self.wl[i]))
                if first and self.x.gain and kc in (3, 5, 7):
                    self.x.sum_squares(pe, (kc - 3) // 2)
                if second and self.x.gain and kc == 1:
                    self.x.sum_squares(pe, 3)
            last.then_inc(self.mm_done, 1)

        for i in range(2):
            pe.wait_ge(self.w_low, i + 1)
            tile(i, i == 0, i == 1)
            if i and after:
                after(0, 0)
        with pe.Fori(1, self.n // 2) as g:
            for i in range(2):
                pe.wait_ge(self.w_low, g * 2 + (i + 1))
                pe.wait_ge(self.taken, g * 2 + (i + 1))
                tile(i)
                if after:
                    after(1 - i, g * 2 + (i - 1))


def project_in_stage(nc, consts, x_d, xT, weights, feats_d):
    with Stage(nc, "pin") as st:
        x = SplitInput(nc, st, consts, xT, "mix")
        proj = Projection(nc, st, weights, NF, x)
        raw = [st.sb(f"out{i}", [P, T + 1]) for i in range(2)]
        shifted = [st.sb(f"shifted{i}", [P, T]) for i in range(2)]
        diff, mu_tile = st.sb("diff", [P, T]), st.sb("mu", [P, 2])
        stored, loaded = [st.sem(f"stored{i}") for i in range(2)], [st.sem(f"loaded{kc}") for kc in range(KC)]
        shift_done = st.sem("shift_done")
        block = st.block()

        @block.sync
        def _(sp):
            proj.first_loads(sp)
            for kc in range(KC):
                sp.dma_start(xT[:, kc, :], x_d[kc]).then_inc(loaded[kc], 16)

            def store(i, tile):
                sp.wait_ge(shift_done, tile + 1)
                sp.dma_start(feats_d[bass.ds(tile, 1)].rearrange("a p t -> (a p) t"),
                             shifted[i][:, :]).then_inc(stored[i], 16)

            proj.loads(sp, store)
            for i in range(2):
                sp.wait_ge(shift_done, NF - 1 + i)
                sp.dma_start(feats_d[NF - 2 + i], shifted[i][:, :]).then_inc(stored[i], 16)
                sp.wait_ge(stored[i], 16 * (NF // 2 + 1))

        @block.gpsimd
        def _(pool):
            x.add_squares(pool)

        @block.tensor
        def _(pe):
            proj.products(pe)

        @block.scalar
        def _(act):
            proj.first_highs(act)
            proj.highs(act)

        @block.vector
        def _(dve):
            for i in range(2):
                nc.vector.memset(raw[i][:, 0:1], 0.0)
                nc.vector.memset(mu_tile[:, i:i + 1], 0.0).then_inc(stored[i], 16)
            proj.first_lows(dve, loaded)
            mu0 = COLS["mu"]

            def take(i, tile):
                nc.vector.tensor_tensor(raw[i][:, 1:T + 1], proj.product(i), x.rstd[:, :], ALU.mult
                                        ).then_inc(proj.taken, 1)
                at = bass.ds(tile + mu0, 1) if not isinstance(tile, int) else slice(tile + mu0, tile + mu0 + 1)
                nc.vector.tensor_copy(mu_tile[:, i:i + 1], consts["cols"][:, at])
                dve.drain()
                nc.vector.tensor_tensor(diff[:, :], raw[i][:, 0:T], raw[i][:, 1:T + 1], ALU.subtract)
                dve.drain()
                dve.wait_ge(stored[i], (tile - i) * 8 + 16)
                nc.vector.scalar_tensor_tensor(out=shifted[i][:, :], in0=diff[:, :], scalar=mu_tile[:, i:i + 1],
                                               in1=raw[i][:, 1:T + 1], op0=ALU.mult, op1=ALU.add
                                               ).then_inc(shift_done, 1)

            proj.takes(dve, take)


TWO_PI = 2.0 * np.pi
TWO_PI_A = 6.28125
TWO_PI_B = float(np.float32(round((TWO_PI - TWO_PI_A) * 2 ** 21) / 2 ** 21))
TWO_PI_C = float(TWO_PI - TWO_PI_A - TWO_PI_B)
ROUNDER = 12582912.0
PI_BELOW = 3.1415925


def mla_prepare_stage(nc, consts, feats, feats_d, positions, cos, sin, krope):
    with Stage(nc, "mprep") as st:
        sq = st.sb("sq", [P, 3, T])
        std = st.sb("std", [P, 2, T])
        pos_i = st.sb("pos_i", [ROPE, T], I32)
        ang = st.sb("ang", [ROPE, T])
        turns = st.sb("turns", [ROPE, T])
        krot = st.sb("krot", [ROPE, T])
        kr = st.sb("kr", [ROPE, T])
        sums = st.psum("sums", [P, 4, HALF])
        rot_ps = st.psum("rot_ps", [P, 2, HALF])
        loaded, sq_ready, sums_ready = st.sem("loaded"), st.sem("sq_ready"), st.sem("sums_ready")
        std_ready, rot_ready, angle_ready = st.sem("std_ready"), st.sem("rot_ready"), st.sem("angle_ready")
        trig_ready, pos_loaded = st.sem("trig_ready"), st.sem("pos_loaded")
        block = st.block()

        @block.sync
        def _(sp):
            sp.dma_start(pos_i[:, :], positions.broadcast_to([ROPE, T])).then_inc(pos_loaded, 16)
            sp.dma_start(feats[:, :, :], feats_d[0:3].rearrange("f p t -> p f t")).then_inc(loaded, 16)
            sp.dma_start(kr[:, :], feats_d[KRWD, 0:64]).then_inc(loaded, 16)

        @block.scalar
        def _(act):
            act.wait_ge(loaded, 32)
            for f in range(3):
                nc.scalar.activation(sq[:, f, :], feats[:, f, :], ACT.Square).then_inc(sq_ready, 1)
            act.wait_ge(sums_ready, 1)
            nc.scalar.activation(std[:, 0, :], sums[:, 0:2, :], ACT.Sqrt, bias=consts["eps"][:, 0:1],
                                 scale=1.0 / Q_LORA).then_inc(std_ready, 1)
            nc.scalar.activation(std[:, 1, :], sums[:, 2:4, :], ACT.Sqrt, bias=consts["eps"][:, 0:1],
                                 scale=1.0 / KV_LORA).then_inc(std_ready, 1)
            for i, out in enumerate((sin, cos)):
                act.wait_ge(angle_ready, i + 1)
                nc.scalar.activation(out[:, :], (krot if i == 0 else turns)[:, :], ACT.Sin).then_inc(trig_ready, 1)

        @block.tensor
        def _(pe):
            pe.wait_ge(loaded, 32)
            for h in range(2):
                nc.tensor.matmul(rot_ps[:, h, :], consts["rot"][:, :], kr[:, h * HALF:(h + 1) * HALF],
                                 start=True, stop=True).then_inc(rot_ready, 1)
            pe.wait_ge(sq_ready, 3)
            for f in range(3):
                for h in range(2):
                    last = nc.tensor.matmul(sums[:, (f // 2) * 2 + h, :], consts["ones"][:, :],
                                            sq[:, f, h * HALF:(h + 1) * HALF], start=(f != 1), stop=(f != 0))
            last.then_inc(sums_ready, 1)

        @block.vector
        def _(dve):
            def reduce_angle(out, quarter):
                nc.vector.tensor_scalar(out[:, :], ang[:, :], float(1.0 / TWO_PI), 0.25 * quarter, ALU.mult, ALU.add)
                dve.drain()
                nc.vector.tensor_scalar(cos[:, :], out[:, :], ROUNDER, -ROUNDER, ALU.add, ALU.add)
                dve.drain()
                nc.vector.scalar_tensor_tensor(out=out[:, :], in0=cos[:, :], scalar=-TWO_PI_A, in1=ang[:, :],
                                               op0=ALU.mult, op1=ALU.add)
                dve.drain()
                for part in (TWO_PI_B, TWO_PI_C):
                    nc.vector.scalar_tensor_tensor(out=out[:, :], in0=cos[:, :], scalar=-part, in1=out[:, :],
                                                   op0=ALU.mult, op1=ALU.add)
                    dve.drain()
                if quarter:
                    nc.vector.tensor_scalar(out[:, :], out[:, :], float(np.pi / 2), None, ALU.add)
                    dve.drain()
                nc.vector.tensor_scalar(out[:, :], out[:, :], PI_BELOW, -PI_BELOW, ALU.min,
                                        ALU.max).then_inc(angle_ready, 1)

            dve.wait_ge(pos_loaded, 16)
            nc.vector.tensor_copy(ang[:, :], pos_i[:, :])
            dve.drain()
            nc.vector.tensor_scalar(ang[:, :], ang[:, :], col(consts, "inv", 0, ROPE), None, ALU.mult)
            dve.drain()
            reduce_angle(krot, 0)
            dve.drain()
            reduce_angle(turns, 1)
            dve.wait_ge(std_ready, 2)
            nc.vector.reciprocal(std[:, :, :], std[:, :, :])
            dve.drain()
            for f, (gain, i) in enumerate((("qg", 0), ("qg", 1), ("kvg", 0))):
                nc.vector.scalar_tensor_tensor(out=feats[:, f, :], in0=feats[:, f, :], scalar=col(consts, gain, i),
                                               in1=std[:, f // 2, :], op0=ALU.mult, op1=ALU.mult)
            dve.wait_ge(trig_ready, 2)
            dve.wait_ge(rot_ready, 2)
            nc.vector.tensor_tensor(krot[:, :], rot_ps[0:ROPE, :, :].rearrange("p h t -> p (h t)"), sin[:, :], ALU.mult)
            nc.vector.tensor_tensor(krope[:, :], kr[:, :], cos[:, :], ALU.mult)
            dve.drain()
            nc.vector.tensor_tensor(krope[:, :], krope[:, :], krot[:, :], ALU.add)


def mla_stage(nc, consts, feats, cos, sin, krope, mix, w_q, w_kv, gates_d):
    scale = float((P + ROPE) ** -0.5)
    fills = 5 + NT
    takes = 4 + NT
    groups = [(i + 4) // 4 for i in range(NT)]
    before = [sum(groups[:i]) for i in range(NT + 1)]
    with Stage(nc, "mla") as st:
        wq = st.sb("wq", [P, 2, P + ROPE])
        wkv = st.sb("wkv", [P, 2 * P])
        qn, kn = st.sb("qn", [P, T]), st.sb("kn", [P, T])
        qraw, qr, qrot = st.sb("qraw", [ROPE, T]), st.sb("qr", [ROPE, T]), st.sb("qrot", [ROPE, T])
        v = st.sb("v", [P, NT, P])
        pr = [st.sb(f"pr{i}", [P, T]) for i in range(2)]
        prT = [st.sb(f"prT{i}", [P, NT, P]) for i in range(2)]
        mx, rsum = st.sb("mx", [P, 2]), st.sb("rsum", [P, 2])
        x = [st.psum(f"x{i}", [P, 2, HALF]) for i in range(2)]
        pt = [st.psum(f"pt{i}", [P, 4, P]) for i in range(2)]
        po = [st.psum(f"po{i}", [P, HALF]) for i in range(2)]
        w_ready, x_full, x_taken = st.sem("w_ready"), st.sem("x_full"), st.sem("x_taken")
        rope_done, max_ready, probs_ready = st.sem("rope_done"), st.sem("max_ready"), st.sem("probs_ready")
        pt_full, pt_taken, po_full, po_taken = (st.sem("pt_full"), st.sem("pt_taken"), st.sem("po_full"),
                                                st.sem("po_taken"))
        block = st.block()

        zeros, zeros_ready, cleared = st.sb("zeros", [P, T]), st.sem("zeros_ready"), st.sem("cleared")

        def keys(i):
            return (i + 1) * P

        @block.gpsimd
        def _(pool):
            nc.gpsimd.memset(zeros[:, :], 0.0).then_inc(zeros_ready, 1)
            pool.wait_ge(zeros_ready, 1)
            with pool.Fori(0, NK) as j:
                pool.dma_start(gates_d[bass.ds(j, 1)].rearrange("a p t -> (a p) t"), zeros[:, :]).then_inc(cleared, 16)
            pool.wait_ge(cleared, 16 * NK)

        @block.sync
        def _(sp):
            sp.dma_start(wq[:, :, :], w_q[0]).then_inc(w_ready, 16)
            sp.dma_start(wkv[:, :], w_kv[0]).then_inc(w_ready, 16)
            with sp.Fori(1, MLA_HEADS) as h:
                sp.wait_ge(x_full, h * fills + (5 - fills))
                sp.dma_start(wq[:, :, :], w_q[bass.ds(h, 1)].rearrange("a p k c -> p (a k) c")).then_inc(w_ready, 16)
                sp.dma_start(wkv[:, :], w_kv[bass.ds(h, 1)].rearrange("a p c -> p (a c)")).then_inc(w_ready, 16)

        @block.tensor
        def _(pe):
            def scores(h, i):
                pe.wait_ge(x_taken, h * takes + (1 + (3 if i == 0 else 3 + i)))
                dst = x[(i + 1) % 2]
                for a in range(0, keys(i), HALF):
                    w = min(HALF, keys(i) - a)
                    nc.tensor.matmul(dst[:, a // HALF, 0:w], qn[:, i * P:(i + 1) * P], kn[:, a:a + w],
                                     start=True, stop=False)
                    last = nc.tensor.matmul(dst[:, a // HALF, 0:w], qr[:, i * P:(i + 1) * P], krope[:, a:a + w],
                                            start=False, stop=True)
                last.then_inc(x_full, 1)

            def transposes(h, i):
                pe.wait_ge(probs_ready, h * NT + (i + 1))
                for g in range(groups[i]):
                    n = before[i] + g
                    pe.wait_ge(pt_taken, h * before[NT] + (n + 1))
                    for j in range(4 * g, min(4 * g + 4, i + 1)):
                        last = nc.tensor.transpose(pt[n % 2][:, j % 4, :], pr[i % 2][:, j * P:(j + 1) * P],
                                                   consts["ident"][:, :])
                    last.then_inc(pt_full, 1)

            def weigh(h, i):
                pe.wait_ge(pt_taken, h * before[NT] + (before[i + 1] + 2))
                pe.wait_ge(po_taken, h * NT + (i + 1))
                for j in range(i + 1):
                    last = nc.tensor.matmul(po[i % 2][:, 0:P], v[:, j, :], prT[i % 2][:, j, :],
                                            start=(j == 0), stop=(j == i))
                last.then_inc(po_full, 1)

            with pe.Fori(0, MLA_HEADS) as h:
                pe.wait_ge(w_ready, h * 32 + 32)
                pe.wait_ge(x_taken, h * takes + 1)
                for kc in range(2):
                    for a in range(2):
                        last = nc.tensor.matmul(x[0][0:ROPE, a, :], wq[:, kc, P:P + ROPE],
                                                feats[:, CQ + kc, a * HALF:(a + 1) * HALF],
                                                start=(kc == 0), stop=(kc == 1))
                last.then_inc(x_full, 1)
                for kc in range(2):
                    for a in range(2):
                        last = nc.tensor.matmul(x[1][:, a, :], wq[:, kc, 0:P],
                                                feats[:, CQ + kc, a * HALF:(a + 1) * HALF],
                                                start=(kc == 0), stop=(kc == 1))
                last.then_inc(x_full, 1)
                pe.wait_ge(x_taken, h * takes + 2)
                for a in range(2):
                    last = nc.tensor.matmul(x[0][:, a, :], consts["rot"][:, :], qraw[:, a * HALF:(a + 1) * HALF],
                                            start=True, stop=True)
                last.then_inc(x_full, 1)
                pe.wait_ge(x_taken, h * takes + 3)
                for a in range(2):
                    last = nc.tensor.matmul(x[1][:, a, :], wkv[:, 0:P], feats[:, CKV, a * HALF:(a + 1) * HALF],
                                            start=True, stop=True)
                last.then_inc(x_full, 1)
                pe.wait_ge(rope_done, h + 2)
                for i in range(NT):
                    last = nc.tensor.matmul(x[0][:, i // 4, (i % 4) * P:(i % 4 + 1) * P],
                                            feats[:, CKV, i * P:(i + 1) * P], wkv[:, P:2 * P], start=True, stop=True)
                last.then_inc(x_full, 1)
                scores(h, 0)
                for i in range(NT):
                    if i + 1 < NT:
                        scores(h, i + 1)
                    transposes(h, i)
                    weigh(h, i)

        @block.scalar
        def _(act):
            def exps(h, i):
                act.wait_ge(max_ready, h * NT + (i + 1))
                nc.scalar.activation(pr[i % 2][:, 0:keys(i)],
                                     x[(i + 1) % 2][:, :, :].rearrange("p a b -> p (a b)")[:, 0:keys(i)], ACT.Exp,
                                     bias=mx[:, i % 2:i % 2 + 1], scale=scale,
                                     accum_out=rsum[:, i % 2:i % 2 + 1]).then_inc(x_taken, 1)

            nc.scalar.activation(rsum[:, 0:1], consts["ones"][:, 0:1], ACT.Copy).then_inc(x_taken, 1)
            nc.scalar.activation(rsum[:, 1:2], consts["ones"][:, 0:1], ACT.Copy).then_inc(pt_taken, 2)
            with act.Fori(0, MLA_HEADS) as h:
                act.wait_ge(x_full, h * fills + 1)
                act.wait_ge(rope_done, h + 1)
                nc.scalar.activation(qraw[:, :], x[0][0:ROPE, :, :].rearrange("p a b -> p (a b)"),
                                     ACT.Copy).then_inc(x_taken, 1)
                act.wait_ge(x_full, h * fills + 2)
                nc.scalar.activation(qn[:, :], x[1][:, :, :].rearrange("p a b -> p (a b)"),
                                     ACT.Copy).then_inc(x_taken, 1)
                act.wait_ge(x_full, h * fills + 4)
                nc.scalar.activation(kn[:, :], x[1][:, :, :].rearrange("p a b -> p (a b)"),
                                     ACT.Copy).then_inc(x_taken, 1)
                act.wait_ge(x_full, h * fills + 5)
                act.wait_ge(po_taken, h * NT + 2)
                nc.scalar.activation(v[:, :, :].rearrange("p a b -> p (a b)"),
                                     x[0][:, :, :].rearrange("p a b -> p (a b)"), ACT.Copy).then_inc(x_taken, 1)
                exps(h, 0)
                for i in range(NT):
                    for g in range(groups[i]):
                        n = before[i] + g
                        if i >= 2 and g == 0:
                            act.wait_ge(po_full, h * NT + (i - 1))
                        act.wait_ge(pt_full, h * before[NT] + (n + 1))
                        m = min(4, i + 1 - 4 * g)
                        nc.scalar.activation(prT[i % 2][:, 4 * g:4 * g + m, :], pt[n % 2][:, 0:m, :],
                                             ACT.Copy).then_inc(pt_taken, 1)
                    if i + 1 < NT:
                        exps(h, i + 1)

        @block.vector
        def _(dve):
            def maxima(h, i):
                dve.wait_ge(x_full, h * fills + (6 + i))
                s = x[(i + 1) % 2][:, :, :].rearrange("p a b -> p (a b)")
                nc.vector.memset(s[0:64, keys(i) - 64:keys(i)], -1e30)
                dve.drain()
                nc.vector.tensor_reduce(mx[:, i % 2:i % 2 + 1], s[:, 0:keys(i)], AX.X, ALU.max)
                dve.drain()
                nc.vector.tensor_scalar(mx[:, i % 2:i % 2 + 1], mx[:, i % 2:i % 2 + 1], -scale, None,
                                        ALU.mult).then_inc(max_ready, 1)

            def normalise(h, i):
                dve.wait_ge(x_taken, h * takes + (1 + 4 + i + 1))
                nc.vector.reciprocal(rsum[:, i % 2:i % 2 + 1], rsum[:, i % 2:i % 2 + 1])
                dve.drain()
                nc.vector.tensor_scalar(pr[i % 2][:, 0:keys(i)], pr[i % 2][:, 0:keys(i)], rsum[:, i % 2:i % 2 + 1],
                                        None, ALU.mult).then_inc(probs_ready, 1)

            def output(h, i):
                dve.wait_ge(po_full, h * NT + (i + 1))
                nc.vector.tensor_copy(mix[:, bass.ds(h, 1), i * P:(i + 1) * P].rearrange("p a t -> p (a t)"),
                                      po[i % 2][:, 0:P]).then_inc(po_taken, 1)

            nc.vector.memset(mx[:, 0:1], 0.0).then_inc(rope_done, 1)
            nc.vector.memset(mx[:, 1:2], 0.0).then_inc(po_taken, 2)
            dve.drain()
            with dve.Fori(0, MLA_HEADS) as h:
                dve.wait_ge(x_taken, h * takes + 2)
                nc.vector.tensor_tensor(qr[:, :], qraw[:, :], cos[:, :], ALU.mult)
                dve.wait_ge(x_full, h * fills + 3)
                nc.vector.tensor_tensor(qrot[:, :], x[0][0:ROPE, :, :].rearrange("p a b -> p (a b)"), sin[:, :],
                                        ALU.mult)
                dve.drain()
                nc.vector.tensor_tensor(qr[:, :], qr[:, :], qrot[:, :], ALU.add).then_inc(rope_done, 1)
                maxima(h, 0)
                for i in range(NT):
                    normalise(h, i)
                    if i + 1 < NT:
                        maxima(h, i + 1)
                    if i >= 1:
                        output(h, i - 1)
                output(h, NT - 1)


def rwkv_stage(nc, consts, feats_d, w_up_d, a_up_d, g_up_d, mix):
    decay = float(np.exp(-0.5))
    W = PAIRS * P
    with Stage(nc, "rwkv") as st:
        w_up, a_up, g_up = st.sb("w_up", [64, RW]), st.sb("a_up", [64, RW]), st.sb("g_up", [P, RW])
        rkv = st.sb("rkv", [P, 12, P])
        gd = st.sb("gd", [P, P])
        wad = st.sb("wad", [64, 2, P])

        def tile4(name, n=1):
            return st.sb(name, [P, PAIRS * n, P])

        sgw, al, gate, cum, prev, rem = (tile4(x) for x in ("sgw", "al", "gate", "cum", "prev", "rem"))
        w_t, w_inv, w_prev, w_rem = (tile4(x) for x in ("w_t", "w_inv", "w_prev", "w_rem"))
        kkr, sqk, nrm, kap, b, ta, k2 = (tile4(x) for x in ("kkr", "sqk", "nrm", "kap", "b", "ta", "k2"))
        ktrt = st.sb("ktrt", [P, PAIRS, 2, P])
        kh, bh, krm, brm, rk, bonus = (tile4(x) for x in ("kh", "bh", "krm", "brm", "rk", "bonus"))
        rhsU = st.sb("rhsU", [P, 2 * PAIRS, P])
        kr_t, br_t, v_t = (tile4(x) for x in ("kr_t", "br_t", "v_t"))
        gm = st.sb("gm", [P, 2 * PAIRS, 4, P])
        lb = [tile4(f"lb{e}") for e in range(2)]
        xi = [tile4(f"xi{e}") for e in range(2)]
        yi = [tile4(f"yi{e}") for e in range(2)]
        tmp = [tile4(f"tmp{e}") for e in range(2)]
        ll = st.sb("ll", [P, 2, 5, PAIRS, P])
        pe_s = [tile4(f"pe_s{e}") for e in range(2)]
        nu = st.sb("nu", [P, 2, 2 * PAIRS, 64])
        at, diag, es = ([tile4(f"{x}{c}") for c in range(2)] for x in ("at", "diag", "es"))
        q1 = tile4("q1")
        state = [tile4(f"state{c}") for c in range(2)]
        ysb, yc, sqy, std = (tile4(x) for x in ("ysb", "yc", "sqy", "std"))
        bank = [st.psum(f"bank{i}", [P, PAIRS, P]) for i in range(8)]

        rt_keep = tile4("rt_keep")
        per_tile = {}

        def sem(name, n):
            per_tile[name] = (st.sem(name), n)
            return name

        for name, n in (("loaded", 64), ("pre", 2), ("biased", 2), ("gated", 1), ("sig", 2), ("cums", 1), ("kk", 1),
                        ("sqk", 1), ("norms", 1), ("sqrt", 1), ("k2", 1), ("exps", 4), ("ktrt", 1), ("khbh", 1),
                        ("rem", 1), ("rk", 2), ("kept", 1), ("gate_mm", 1), ("gate", 1), ("bonus_mm", 1), ("bonus", 1),
                        ("trans", 4), ("trans_taken", 4), ("gram", 8), ("masked", 8), ("lb_mm", 2), ("lb", 2),
                        ("ux", 1), ("ux_taken", 1), ("level", 10), ("inv", 12), ("inv_t", 10), ("p_mm", 10), ("p_taken", 10),
                        ("z_mm", 10), ("u_mm", 2), ("nu", 2), ("at_mm", 2), ("e_mm", 2), ("diag", 2), ("at", 2),
                        ("q_mm", 1), ("q1", 1), ("chain", 2), ("state", 2), ("y_mm", 1), ("y", 1), ("mean", 1),
                        ("yc", 1), ("sqy", 1), ("var", 1), ("std", 1), ("rstd", 2), ("normed", 4), ("done", 1)):
            sem(name, n)
        w_loaded = st.sem("w_loaded")
        block = st.block()

        def inc(ins, name, n=1):
            return ins.then_inc(per_tile[name][0], n)

        def flat(x):
            return x[:, :, :].rearrange("p a b -> p (a b)")

        def over_heads(c):
            return c.unsqueeze(1).broadcast_to([P, PAIRS, P])

        class Tile:
            def __init__(self, eng, t, ahead=0):
                self.eng, self.t, self.ahead = eng, t, ahead

            def wait(self, name, k):
                s, n = per_tile[name]
                self.eng.wait_ge(s, self.t * n + (self.ahead * n + k))

            def tokens(self):
                if isinstance(self.t, int):
                    return slice((self.t + self.ahead) * P, (self.t + self.ahead + 1) * P)
                return bass.ds(self.t * P + self.ahead * P, P)

        def each_tile(eng, prepare, matrices, solve):
            first = Tile(eng, 0)
            for step in range(7):
                prepare(first, step, None)
            matrices(first, None)
            with eng.Fori(0, NT - 1) as t:
                this, following = Tile(eng, t), Tile(eng, t, 1)
                solve(this, lambda step: prepare(following, step, this))
                matrices(following, this)
            solve(Tile(eng, NT - 1), lambda step: None)

        @block.sync
        def _(sp):
            def load(tok):
                inc(sp.dma_start(rkv[:, :, :], feats_d[RT:GT, :, tok].rearrange("f p t -> p f t")), "loaded", 16)
                inc(sp.dma_start(gd[:, :], feats_d[GT, :, tok]), "loaded", 16)
                inc(sp.dma_start(wad[:, 0, :], feats_d[KRWD, 64:P, tok]), "loaded", 16)
                inc(sp.dma_start(wad[:, 1, :], feats_d[AD, 0:64, tok]), "loaded", 16)

            sp.dma_start(w_up[:, :], w_up_d).then_inc(w_loaded, 16)
            sp.dma_start(a_up[:, :], a_up_d).then_inc(w_loaded, 16)
            sp.dma_start(g_up[:, :], g_up_d).then_inc(w_loaded, 16)
            load(slice(0, P))
            with sp.Fori(0, NT - 1) as t:
                start = sp.snap(t * P + P)
                Tile(sp, t).wait("bonus", 1)
                load(bass.ds(start, P))

        @block.tensor
        def _(pe):
            def prepare(w, step, before):
                if step == 1:
                    w.wait("gated", 1)
                    if before:
                        before.wait("lb", 2)
                    for f in range(PAIRS):
                        last = nc.tensor.matmul(bank[6][:, f, :], w_up[:, f * P:(f + 1) * P], wad[:, 0, :],
                                                start=True, stop=True)
                    inc(last, "pre")
                    for f in range(PAIRS):
                        last = nc.tensor.matmul(bank[7][:, f, :], a_up[:, f * P:(f + 1) * P], wad[:, 1, :],
                                                start=True, stop=True)
                    inc(last, "pre")
                if step == 3:
                    w.wait("biased", 1)
                    w.wait("sqk", 1)
                    inc(nc.tensor.matmul(flat(bank[6]), consts["headones"][:, :], flat(sqk), start=True, stop=True),
                        "norms")

            def matrices(w, before):
                w.wait("sqrt", 1)
                w.wait("biased", 2)
                for n, (src, after) in enumerate(((lambda f: ktrt[:, f, 0, :], "ktrt"), (lambda f: krm[:, f, :], "rem"),
                                                  (lambda f: brm[:, f, :], "rem"),
                                                  (lambda f: rkv[:, 8 + f, :], "rem"))):
                    w.wait(after, 1)
                    if n < 2 and before:
                        before.wait("state", n + 2)
                    if n >= 2:
                        w.wait("trans_taken", n - 1)
                    for f in range(PAIRS):
                        last = nc.tensor.transpose(bank[6 + n % 2][:, f, :], src(f), consts["ident"][:, :])
                    inc(last, "trans")
                    if n == 0 and before:
                        before.wait("y", 1)
                        inc(nc.tensor.matmul(flat(bank[0]), consts["headones"][:, :], flat(ysb), start=True,
                                             stop=True), "mean")
                if before:
                    before.wait("sqy", 1)
                    inc(nc.tensor.matmul(flat(bank[1]), consts["headones"][:, :], flat(sqy), start=True, stop=True),
                        "var")
                w.wait("khbh", 1)
                for h in range(2 * PAIRS):
                    f, rows = h // 2, slice(64 * (h % 2), 64 * (h % 2) + 64)
                    if h >= 2:
                        w.wait("masked", h - 1)
                    nc.tensor.matmul(bank[4 + h % 2][:, 0:2, :], kh[rows, f, :], ktrt[rows, f, :, :],
                                     start=True, stop=True)
                    inc(nc.tensor.matmul(bank[4 + h % 2][:, 2:4, :], bh[rows, f, :], ktrt[rows, f, :, :],
                                         start=True, stop=True), "gram")
                for e in range(2):
                    rows = slice(64 * e, 64 * e + 64)
                    w.wait("trans_taken", 3 + e)
                    for f in range(PAIRS):
                        last = nc.tensor.matmul(bank[6 + e][:, f, :], ktrt[rows, f, 0, :], bh[rows, f, :],
                                                start=True, stop=True)
                    inc(last, "lb_mm")
                for f in range(PAIRS):
                    last = nc.tensor.matmul(bank[2][:, f, :], g_up[:, f * P:(f + 1) * P], gd[:, :],
                                            start=True, stop=True)
                inc(last, "gate_mm")
                w.wait("rk", 2)
                if before:
                    before.wait("std", 1)
                inc(nc.tensor.matmul(flat(bank[1]), consts["headones"][:, :], flat(rk), start=True, stop=True),
                    "bonus_mm")
                w.wait("masked", 8)
                for h in range(2 * PAIRS):
                    last = nc.tensor.matmul(bank[3][:, h // 2, 64 * (h % 2):64 * (h % 2) + 64], gm[:, h, 0, :],
                                            flat(v_t)[:, h * 64:(h + 1) * 64], start=True, stop=True)
                inc(last, "ux")

            def solve(w, prepare_next):
                for l in range(1, 6):
                    for e in range(2):
                        if l == 1 and e == 1:
                            w.wait("bonus", 1)
                        w.wait("level", 2 * (l - 1) + e + 1)
                        w.wait("inv", 2 * (l - 1) + e + 1)
                        for f in range(PAIRS):
                            last = nc.tensor.matmul(bank[e][:, f, :], ll[:, e, l - 1, f, :], xi[e][:, f, :],
                                                    start=True, stop=True)
                        inc(last, "p_mm")
                    if l == 1:
                        w.wait("ux_taken", 1)
                        w.wait("gate", 1)
                    else:
                        prepare_next(l - 1)
                    for e in range(2):
                        w.wait("p_taken", 2 * (l - 1) + e + 1)
                        w.wait("inv_t", 2 * (l - 1) + e + 1)
                        for f in range(PAIRS):
                            last = nc.tensor.matmul(bank[2 + e][:, f, :], yi[e][:, f, :], pe_s[e][:, f, :],
                                                    start=True, stop=True)
                            if l < 5:
                                last = nc.tensor.matmul(bank[4 + e][:, f, :], pe_s[e][:, f, :], yi[e][:, f, :],
                                                        start=True, stop=True)
                        inc(last, "z_mm")
                for e in range(2):
                    w.wait("inv", 10 + e + 1)
                    for f in range(PAIRS):
                        last = nc.tensor.matmul(bank[e][:, f, :], xi[e][:, f, :], rhsU[:, 2 * f + e, :],
                                                start=True, stop=True)
                    inc(last, "u_mm")
                w.wait("nu", 2)
                for c in range(2):
                    rows = slice(64 * c, 64 * c + 64)
                    for f in range(PAIRS):
                        last = nc.tensor.matmul(bank[c][:, f, :],
                                                nu[rows, 0, 2 * f:2 * f + 2, :].rearrange("p h c -> p (h c)"),
                                                br_t[rows, f, :], start=True, stop=True)
                    inc(last, "at_mm")
                    for f in range(PAIRS):
                        nc.tensor.matmul(bank[2 + c][:, f, :], kr_t[rows, f, :], v_t[rows, f, :],
                                         start=True, stop=False)
                        last = nc.tensor.matmul(bank[2 + c][:, f, :], br_t[rows, f, :],
                                                nu[rows, 1, 2 * f:2 * f + 2, :].rearrange("p h c -> p (h c)"),
                                                start=False, stop=True)
                    inc(last, "e_mm")
                for h in range(2 * PAIRS):
                    f, rows = h // 2, slice(64 * (h % 2), 64 * (h % 2) + 64)
                    last = nc.tensor.matmul(bank[4][rows, f, :], nu[:, 0, h, :], gm[:, h, 3, :], start=True, stop=True)
                inc(last, "q_mm")
                for h in range(2 * PAIRS):
                    f, rows = h // 2, slice(64 * (h % 2), 64 * (h % 2) + 64)
                    nc.tensor.matmul(bank[5][rows, f, :], flat(v_t)[:, h * 64:(h + 1) * 64], gm[:, h, 1, :],
                                     start=(h < 2), stop=False, skip_group_check=True)
                    nc.tensor.matmul(bank[5][rows, f, :], nu[:, 1, h, :], gm[:, h, 3, :],
                                     start=False, stop=False, skip_group_check=True)
                w.wait("q1", 1)
                for c in range(2):
                    w.wait("state", c + 1)
                    for f in range(PAIRS):
                        last = nc.tensor.matmul(bank[5][:, f, c * CH:(c + 1) * CH], state[c][:, f, :],
                                                q1[:, f, c * CH:(c + 1) * CH], start=False, stop=(c == 1),
                                                skip_group_check=True)
                    if c == 1:
                        inc(last, "y_mm")
                    w.wait("at", c + 1)
                    if c == 0:
                        prepare_next(5)
                    for f in range(PAIRS):
                        last = nc.tensor.matmul(bank[6 + c][:, f, :], at[c][:, f, :], state[c][:, f, :],
                                                start=True, stop=True)
                    inc(last, "chain")

            pe.wait_ge(w_loaded, 48)
            each_tile(pe, prepare, matrices, solve)
            w = Tile(pe, NT - 1)
            w.wait("y", 1)
            inc(nc.tensor.matmul(flat(bank[0]), consts["headones"][:, :], flat(ysb), start=True, stop=True), "mean")
            w.wait("sqy", 1)
            inc(nc.tensor.matmul(flat(bank[1]), consts["headones"][:, :], flat(sqy), start=True, stop=True), "var")

        @block.scalar
        def _(act):
            def prepare(w, step, before):
                if step == 0:
                    w.wait("loaded", 64)
                    nc.scalar.activation(wad[:, 0, :], wad[:, 0, :], ACT.Tanh)
                    inc(nc.scalar.activation(gd[:, :], gd[:, :], ACT.Sigmoid), "gated")
                if step == 2:
                    w.wait("biased", 1)
                    inc(nc.scalar.activation(flat(sgw), flat(sgw), ACT.Sigmoid), "sig")
                    w.wait("biased", 2)
                    inc(nc.scalar.activation(flat(al), flat(al), ACT.Sigmoid), "sig")
                    w.wait("kk", 1)
                    inc(nc.scalar.activation(flat(sqk), flat(kkr), ACT.Square), "sqk")
                if step == 3:
                    w.wait("norms", 1)
                    inc(nc.scalar.activation(flat(nrm), flat(bank[6]), ACT.Sqrt), "sqrt")
                    w.wait("cums", 1)
                    if before:
                        before.wait("diag", 2)
                    for out, x in ((w_prev, prev), (w_t, cum)):
                        inc(nc.scalar.activation(flat(out), flat(x), ACT.Exp, scale=-decay), "exps")
                if step == 5:
                    for out, x, sign in ((w_inv, cum, 1.0), (w_rem, rem, -1.0)):
                        inc(nc.scalar.activation(flat(out), flat(x), ACT.Exp, scale=sign * decay), "exps")

            def norm_squares(w):
                w.wait("yc", 1)
                inc(nc.scalar.activation(flat(sqy), flat(yc), ACT.Square), "sqy")

            def norm_std(w):
                w.wait("var", 1)
                inc(nc.scalar.activation(flat(std), flat(bank[1]), ACT.Sqrt, bias=consts["eps"][:, 1:2],
                                         scale=1.0 / CH), "std")

            def matrices(w, before):
                for n, dst in enumerate((rhsU[:, :, 0:64], kr_t, br_t, v_t)):
                    w.wait("trans", n + 1)
                    src = bank[6 + n % 2]
                    if n == 0:
                        last = nc.scalar.activation(dst, flat(src).rearrange("p (h c) -> p h c", c=64), ACT.Copy)
                    else:
                        last = nc.scalar.activation(flat(dst), flat(src), ACT.Copy)
                    inc(last, "trans_taken")
                    if n == 1 and before:
                        norm_squares(before)
                if before:
                    norm_std(before)
                    before.wait("q1", 1)
                inc(nc.scalar.activation(rt_keep[:, :, :], ktrt[:, :, 1, :], ACT.Copy), "kept")
                if before:
                    before.wait("done", 1)
                w.wait("gate_mm", 1)
                inc(nc.scalar.activation(flat(gate), flat(bank[2]), ACT.Copy), "gate")
                w.wait("ux", 1)
                inc(nc.scalar.activation(rhsU[:, :, 64:128], flat(bank[3]).rearrange("p (h c) -> p h c", c=64),
                                         ACT.Copy), "ux_taken")

            def solve(w, prepare_next):
                for l in range(1, 6):
                    for e in range(2):
                        w.wait("p_mm", 2 * (l - 1) + e + 1)
                        if l >= 2:
                            w.wait("z_mm", 2 * (l - 2) + e + 1)
                        inc(nc.scalar.activation(flat(pe_s[e]), flat(bank[e]), ACT.Copy), "p_taken")
                    prepare_next(l - 1)
                for e in range(2):
                    w.wait("u_mm", e + 1)
                    inc(nc.scalar.activation(nu[:, :, :, :].rearrange("p w (f e) c -> p e f w c", e=2)[:, e],
                                             bank[e][:, :, :].rearrange("p f (w c) -> p f w c", w=2), ACT.Copy,
                                             scale=-1.0), "nu")
                prepare_next(5)
                w.wait("y_mm", 1)
                inc(nc.scalar.activation(flat(ysb), flat(bank[5]), ACT.Copy), "y")

            each_tile(act, prepare, matrices, solve)
            norm_squares(Tile(act, NT - 1))
            norm_std(Tile(act, NT - 1))

        @block.gpsimd
        def _(pool):
            def prepare(w, step, before):
                if step == 0:
                    w.wait("loaded", 64)
                    inc(nc.gpsimd.tensor_tensor(kkr[:, :, :], rkv[:, 4:8, :], cols_over(consts, "kk", PAIRS, P),
                                                ALU.mult), "kk")
                if step == 4:
                    w.wait("k2", 1)
                    inc(nc.gpsimd.tensor_tensor(rk[:, :, :], rkv[:, 0:4, :], k2[:, :, :], ALU.mult), "rk")
                    w.wait("rk", 1)
                    inc(nc.gpsimd.tensor_tensor(rk[:, :, :], rk[:, :, :], cols_over(consts, "rk", PAIRS, P), ALU.mult),
                        "rk")

            def norm(w):
                w.wait("rstd", 2)
                inc(nc.gpsimd.tensor_tensor(flat(yc), flat(yc), flat(std), ALU.mult), "normed")
                w.wait("normed", 1)
                inc(nc.gpsimd.tensor_tensor(yc[:, :, :], yc[:, :, :], cols_over(consts, "lnw", PAIRS, P), ALU.mult),
                    "normed")
                w.wait("normed", 2)
                inc(nc.gpsimd.tensor_tensor(yc[:, :, :], yc[:, :, :], cols_over(consts, "lnb", PAIRS, P), ALU.add),
                    "normed")
                w.wait("normed", 3)
                inc(nc.gpsimd.tensor_tensor(flat(yc), flat(yc), flat(bonus), ALU.add), "normed")
                w.wait("normed", 4)
                inc(nc.gpsimd.tensor_tensor(mix[:, 4:8, w.tokens()], yc[:, :, :], gate[:, :, :], ALU.mult), "done")

            def matrices(w, before):
                if before:
                    before.wait("at", 2)
                w.wait("exps", 4)
                for c in range(2):
                    end = w_t[:, :, c * CH + CH - 1:c * CH + CH].broadcast_to([P, PAIRS, P])
                    inc(nc.gpsimd.tensor_tensor(diag[c][:, :, :], over_heads(consts["ident"][:, :]), end, ALU.mult),
                        "diag")
                if before:
                    norm(before)
                for l in range(1, 6):
                    for e in range(2):
                        if l == 1:
                            w.wait("lb", e + 1)
                        inc(nc.gpsimd.tensor_tensor(ll[:, e, l - 1, :, :], lb[e][:, :, :],
                                                    over_heads(consts["level"][:, l, :]), ALU.mult), "level")

            def solve(w, prepare_next):
                for step in range(7):
                    prepare_next(step)

            each_tile(pool, prepare, matrices, solve)
            norm(Tile(pool, NT - 1))

        @block.vector
        def _(dve):
            def prepare(w, step, before):
                if step == 1:
                    w.wait("pre", 1)
                    inc(nc.vector.tensor_tensor(sgw[:, :, :], bank[6][:, :, :], cols_over(consts, "w0", PAIRS, P),
                                                ALU.add), "biased")
                    w.wait("pre", 2)
                    inc(nc.vector.tensor_tensor(al[:, :, :], bank[7][:, :, :], cols_over(consts, "a0", PAIRS, P),
                                                ALU.add), "biased")
                if step == 2:
                    w.wait("sig", 1)
                    nc.vector.tensor_tensor_scan(flat(cum), consts["scanmask"][:, :], flat(sgw), 0.0, ALU.mult, ALU.add)
                    dve.drain()
                    nc.vector.tensor_tensor(flat(prev), flat(cum), flat(sgw), ALU.subtract)
                    chunks = flat(cum).rearrange("p (c t) -> p c t", t=CH)
                    inc(nc.vector.tensor_tensor(flat(rem).rearrange("p (c t) -> p c t", t=CH),
                                                chunks[:, :, CH - 1:CH].broadcast_to([P, 2 * PAIRS, CH]), chunks,
                                                ALU.subtract), "cums")
                    w.wait("sig", 2)
                    nc.vector.scalar_tensor_tensor(out=ta[:, :, :], in0=al[:, :, :], scalar=-1.0,
                                                   in1=cols_over(consts, "ka", PAIRS, P), op0=ALU.add, op1=ALU.mult)
                    dve.drain()
                    inc(nc.vector.scalar_tensor_tensor(out=k2[:, :, :], in0=ta[:, :, :], scalar=1.0,
                                                       in1=rkv[:, 4:8, :], op0=ALU.add, op1=ALU.mult), "k2")
                if step == 4:
                    w.wait("sqrt", 1)
                    nc.vector.tensor_scalar(flat(nrm), flat(nrm), 1e-12, None, ALU.max)
                    dve.drain()
                    nc.vector.reciprocal(flat(nrm), flat(nrm))
                    dve.drain()
                    nc.vector.tensor_tensor(flat(kap), flat(kkr), flat(nrm), ALU.mult)
                    dve.drain()
                    nc.vector.tensor_tensor(flat(b), flat(kap), flat(al), ALU.mult)
                    w.wait("exps", 2)
                    if before:
                        before.wait("kept", 1)
                    nc.vector.tensor_tensor(ktrt[:, :, 0, :], kap[:, :, :], w_prev[:, :, :], ALU.mult)
                    inc(nc.vector.tensor_tensor(ktrt[:, :, 1, :], rkv[:, 0:4, :], w_t[:, :, :], ALU.mult), "ktrt")
                if step == 5:
                    dve.drain()
                    w.wait("exps", 4)
                    nc.vector.tensor_tensor(flat(krm), flat(k2), flat(w_rem), ALU.mult)
                    inc(nc.vector.tensor_tensor(flat(brm), flat(b), flat(w_rem), ALU.mult), "rem")
                if step == 6:
                    nc.vector.tensor_tensor(flat(kh), flat(k2), flat(w_inv), ALU.mult)
                    inc(nc.vector.tensor_tensor(flat(bh), flat(b), flat(w_inv), ALU.mult), "khbh")

            def center(w):
                w.wait("mean", 1)
                w.wait("y", 1)
                inc(nc.vector.scalar_tensor_tensor(out=flat(yc), in0=flat(bank[0]), scalar=-1.0 / CH, in1=flat(ysb),
                                                   op0=ALU.mult, op1=ALU.add), "yc")

            def invert_std(w, half):
                w.wait("std", 1)
                part = std[:, half * 2:half * 2 + 2, :]
                inc(nc.vector.reciprocal(part, part), "rstd")

            def matrices(w, before):
                if before:
                    center(before)
                for h in range(2 * PAIRS):
                    w.wait("gram", h + 1)
                    inc(nc.vector.tensor_tensor(gm[:, h, :, :], bank[4 + h % 2][:, :, :], consts["mask4"][:, :, :],
                                                ALU.mult), "masked")
                    if before and h in (3, 4):
                        invert_std(before, h - 3)
                for e in range(2):
                    w.wait("lb_mm", e + 1)
                    inc(nc.vector.tensor_tensor(lb[e][:, :, :], bank[6 + e][:, :, :], over_heads(consts["lower"][:, :]),
                                                ALU.mult), "lb")
                dve.drain()
                gv = gm[:, :, :, :].rearrange("p (f e) w c -> p f e w c", e=2)
                for e in range(2):
                    inc(nc.vector.tensor_tensor(xi[e][:, :, :], gv[:, :, e, 2, :], over_heads(consts["ident"][:, :]),
                                                ALU.add), "inv")
                    nc.vector.tensor_tensor(tmp[e][:, :, :], lb[e][:, :, :], over_heads(consts["level"][:, 0, :]),
                                            ALU.mult)
                dve.drain()
                for e in range(2):
                    inc(nc.vector.scalar_tensor_tensor(out=yi[e][:, :, :], in0=tmp[e][:, :, :], scalar=-1.0,
                                                       in1=over_heads(consts["ident"][:, :]), op0=ALU.mult,
                                                       op1=ALU.add), "inv_t")
                w.wait("bonus_mm", 1)
                if before:
                    before.wait("done", 1)
                inc(nc.vector.tensor_tensor(bonus[:, :, :], bank[1][:, :, :], rkv[:, 8:12, :], ALU.mult), "bonus")
                dve.drain()

            def solve(w, prepare_next):
                for l in range(1, 6):
                    for e in range(2):
                        w.wait("z_mm", 2 * (l - 1) + e + 1)
                        inc(nc.vector.tensor_tensor(flat(xi[e]), flat(xi[e]), flat(bank[2 + e]), ALU.subtract), "inv")
                        if l < 5:
                            inc(nc.vector.tensor_tensor(flat(yi[e]), flat(yi[e]), flat(bank[4 + e]), ALU.subtract),
                                "inv_t")
                    if l > 1:
                        prepare_next(l - 1)
                    dve.drain()
                for c in range(2):
                    w.wait("at_mm", c + 1)
                    nc.vector.tensor_tensor(at[c][:, :, :], bank[c][:, :, :], over_heads(consts["headones"][:, :]),
                                            ALU.mult)
                    w.wait("e_mm", c + 1)
                    nc.vector.tensor_tensor(es[c][:, :, :], bank[2 + c][:, :, :], over_heads(consts["headones"][:, :]),
                                            ALU.mult)
                    dve.drain()
                    w.wait("diag", c + 1)
                    inc(nc.vector.tensor_tensor(flat(at[c]), flat(at[c]), flat(diag[c]), ALU.add), "at")
                w.wait("q_mm", 1)
                inc(nc.vector.tensor_tensor(q1[:, :, :], bank[4][:, :, :], rt_keep[:, :, :], ALU.add), "q1")
                for c in range(2):
                    prepare_next(5 + c)
                    w.wait("chain", c + 1)
                    inc(nc.vector.tensor_tensor(flat(state[1 - c]), flat(bank[6 + c]), flat(es[c]), ALU.add), "state")

            inc(nc.vector.memset(flat(state[0]), 0.0), "state")
            each_tile(dve, prepare, matrices, solve)
            center(Tile(dve, NT - 1))
            for half in range(2):
                invert_std(Tile(dve, NT - 1), half)


def residual_stage(nc, consts, name, weights, acts, src, dst, load=None):
    with Stage(nc, name) as st:
        x = SplitInput(nc, st, consts, acts)
        proj = Projection(nc, st, weights, KC, x)
        loaded = st.sem("loaded")
        block = st.block()

        @block.sync
        def _(sp):
            proj.first_loads(sp)
            if load is not None:
                sp.dma_start(src[:, :, :], load.rearrange("k p t -> p k t")).then_inc(loaded, 16)
            proj.loads(sp)

        @block.tensor
        def _(pe):
            proj.products(pe)

        @block.scalar
        def _(act):
            proj.first_highs(act)
            proj.highs(act)

        @block.vector
        def _(dve):
            proj.first_lows(dve)
            if load is not None:
                dve.wait_ge(loaded, 16)

            def take(i, tile):
                at = bass.ds(tile, 1) if not isinstance(tile, int) else slice(tile, tile + 1)
                nc.vector.tensor_tensor(dst[:, at, :].rearrange("p a t -> p (a t)"),
                                        src[:, at, :].rearrange("p a t -> p (a t)"), proj.product(i),
                                        ALU.add).then_inc(proj.taken, 1)

            proj.takes(dve, take)


def queries_stage(nc, consts, h, weights, q):
    with Stage(nc, "xq") as st:
        x = SplitInput(nc, st, consts, h, "xa")
        proj = Projection(nc, st, weights, KC, x)
        block = st.block()

        @block.sync
        def _(sp):
            proj.first_loads(sp)
            proj.loads(sp)

        @block.gpsimd
        def _(pool):
            x.add_squares(pool)

        @block.tensor
        def _(pe):
            proj.products(pe)

        @block.scalar
        def _(act):
            proj.first_highs(act)
            proj.highs(act)

        @block.vector
        def _(dve):
            proj.first_lows(dve)

            def take(i, tile):
                at = bass.ds(tile, 1) if not isinstance(tile, int) else slice(tile, tile + 1)
                nc.vector.tensor_tensor(q[:, at, :].rearrange("p a t -> p (a t)"), proj.product(i), x.rstd[:, :],
                                        ALU.mult).then_inc(proj.taken, 1)

            proj.takes(dve, take)


def memory_stage(nc, memn, w_k, w_v, k, v):
    hd = D // XH
    with Stage(nc, "kv") as st:
        wk = [st.sb(f"wk{i}", [P, KC, hd]) for i in range(XH)]
        wv = [st.sb(f"wv{i}", [P, KC, hd]) for i in range(XH)]
        ps = [st.psum(f"ps{i}", [P, HALF]) for i in range(4)]
        w_ready, mm_done = st.sem("w_ready"), st.sem("mm_done")
        block = st.block()

        @block.sync
        def _(sp):
            for h in range(XH):
                sp.dma_start(wk[h][:, :, :], w_k[h]).then_inc(w_ready, 16)
                sp.wait_ge(w_ready, 32 * h + 16)
                sp.dma_start(wv[h][:, :, :], w_v[h]).then_inc(w_ready, 16)
                sp.wait_ge(w_ready, 32 * h + 32)

        taken = st.sem("taken")

        @block.tensor
        def _(pe):
            for h in range(XH):
                for kind in range(2):
                    n = 2 * h + kind
                    pe.wait_ge(w_ready, 16 * (n + 1))
                    if n >= 4:
                        pe.wait_ge(taken, n - 3)
                    for a in range(2):
                        part = slice(a * P, (a + 1) * P)
                        for kc in range(KC):
                            lhs, rhs = ((wk[h][:, kc, part], memn[:, kc, :]) if kind == 0 else
                                        (memn[:, kc, part], wv[h][:, kc, :]))
                            last = nc.tensor.matmul(ps[n % 4][:, a * MEM:(a + 1) * MEM], lhs, rhs,
                                                    start=(kc == 0), stop=(kc == KC - 1))
                    last.then_inc(mm_done, 1)

        @block.scalar
        def _(act):
            for h in range(XH):
                for kind, dst in enumerate((k, v)):
                    n = 2 * h + kind
                    act.wait_ge(mm_done, n + 1)
                    nc.scalar.activation(dst[:, h, :], ps[n % 4][:, :], ACT.Copy).then_inc(taken, 1)


def cross_attention_stage(nc, consts, qo, k, v):
    hd = D // XH
    scale = float(hd ** -0.5)
    with Stage(nc, "xa") as st:
        q, vh = st.sb("q", [P, 2, T]), st.sb("vh", [P, 2, hd])
        pr = [st.sb(f"pr{i}", [P, 4, MEM]) for i in range(2)]
        prT = st.sb("prT", [P, 2, HALF])
        mx, rsum = st.sb("mx", [P, 2, 4]), st.sb("rsum", [P, 2, 4])
        x = [st.psum(f"x{i}", [P, 4 * MEM]) for i in range(2)]
        pt = [st.psum(f"pt{i}", [P, 4, P]) for i in range(2)]
        po = [st.psum(f"po{i}", [P, HALF]) for i in range(2)]
        q_in, v_in, s_full, max_ready = st.sem("q_in"), st.sem("v_in"), st.sem("s_full"), st.sem("max_ready")
        exp_done, probs_ready = st.sem("exp_done"), st.sem("probs_ready")
        pt_full, pt_taken, po_full, po_taken = (st.sem("pt_full"), st.sem("pt_taken"), st.sem("po_full"),
                                                st.sem("po_taken"))
        block = st.block()

        def at(i, n=1):
            return slice(i, i + n) if isinstance(i, int) else bass.ds(i, n)

        def each_head(eng, body):
            with eng.Fori(0, XH - 1) as h:
                body(h, True)
            body(XH - 1, False)

        @block.gpsimd
        def _(pool):
            nc.gpsimd.tensor_copy(q[:, :, :], qo[:, 0:2, :]).then_inc(q_in, 1)
            nc.gpsimd.tensor_copy(vh[:, :, :].rearrange("p m c -> p (m c)"), v[:, 0, :]).then_inc(v_in, 1)
            with pool.Fori(0, XH - 1) as h:
                pool.wait_ge(s_full, h * 2 + 2)
                nc.gpsimd.tensor_copy(q[:, :, :], qo[:, at(h * 2 + 2, 2), :]).then_inc(q_in, 1)
                pool.wait_ge(po_full, h * 4 + 4)
                nc.gpsimd.tensor_copy(vh[:, :, :].rearrange("p m c -> p (m c)"),
                                      v[:, at(h + 1), :].rearrange("p a c -> p (a c)")).then_inc(v_in, 1)

        @block.tensor
        def _(pe):
            def scores(h, s):
                if s == 0:
                    pe.wait_ge(q_in, h + 1)
                pe.wait_ge(exp_done, h * 2 + (s + 1))
                for i in range(4):
                    for a in range(2):
                        last = nc.tensor.matmul(x[s][:, i * MEM:(i + 1) * MEM],
                                                q[:, a, (4 * s + i) * P:(4 * s + i + 1) * P],
                                                k[:, at(h), a * MEM:(a + 1) * MEM].rearrange("p a m -> p (a m)"),
                                                start=(a == 0), stop=(a == 1))
                last.then_inc(s_full, 1)

            def values(h, s):
                pe.wait_ge(probs_ready, h * 2 + (s + 1))
                for m in range(2):
                    pe.wait_ge(pt_taken, h * 4 + (2 * s + m + 1))
                    for i in range(4):
                        last = nc.tensor.transpose(pt[m][:, i, :], pr[s][:, i, m * P:(m + 1) * P],
                                                   consts["ident"][:, :])
                    last.then_inc(pt_full, 1)
                if s == 0:
                    pe.wait_ge(v_in, h + 1)
                pe.wait_ge(pt_taken, h * 4 + (2 * s + 4))
                for a in range(2):
                    pe.wait_ge(po_taken, h * 4 + (2 * s + a + 1))
                    for m in range(2):
                        last = nc.tensor.matmul(po[a][:, :], vh[:, m, a * P:(a + 1) * P], prT[:, m, :],
                                                start=(m == 0), stop=(m == 1))
                    last.then_inc(po_full, 1)

            def head(h, more):
                scores(h, 1)
                values(h, 0)
                if more:
                    scores(h + 1, 0)
                values(h, 1)

            scores(0, 0)
            each_head(pe, head)

        @block.scalar
        def _(act):
            def exps(h, s):
                act.wait_ge(max_ready, h * 2 + (s + 1))
                for i in range(4):
                    last = nc.scalar.activation(pr[s][:, i, :], x[s][:, i * MEM:(i + 1) * MEM], ACT.Exp,
                                                bias=mx[:, s, i:i + 1], scale=scale, accum_out=rsum[:, s, i:i + 1])
                last.then_inc(exp_done, 1)

            def transposed(h, s):
                for m in range(2):
                    act.wait_ge(pt_full, h * 4 + (2 * s + m + 1))
                    act.wait_ge(po_taken, h * 4 + (2 * s + 2))
                    nc.scalar.activation(prT[:, m, :], pt[m][:, :, :].rearrange("p a b -> p (a b)"),
                                         ACT.Copy).then_inc(pt_taken, 1)

            def head(h, more):
                transposed(h, 0)
                exps(h, 1)
                transposed(h, 1)
                if more:
                    exps(h + 1, 0)

            act.nop().then_inc(exp_done, 2)
            act.nop().then_inc(pt_taken, 2)
            exps(0, 0)
            each_head(act, head)

        @block.vector
        def _(dve):
            def maxima(h, s):
                dve.drain()
                dve.wait_ge(s_full, h * 2 + (s + 1))
                nc.vector.tensor_reduce(mx[:, s, :], x[s][:, :].rearrange("p (i m) -> p i m", m=MEM), AX.X, ALU.max)
                dve.drain()
                nc.vector.tensor_scalar(mx[:, s, :], mx[:, s, :], -scale, None, ALU.mult).then_inc(max_ready, 1)

            def normalize(h, s):
                dve.wait_ge(exp_done, h * 2 + (s + 3))
                nc.vector.reciprocal(rsum[:, s, :], rsum[:, s, :])
                dve.drain()
                nc.vector.tensor_tensor(pr[s][:, :, :], pr[s][:, :, :],
                                        rsum[:, s, :].unsqueeze(2).broadcast_to([P, 4, MEM]),
                                        ALU.mult).then_inc(probs_ready, 1)

            def outputs(h, s):
                for a in range(2):
                    dve.wait_ge(po_full, h * 4 + (2 * s + a + 1))
                    nc.vector.tensor_copy(qo[:, at(h * 2 + a), s * HALF:(s + 1) * HALF].rearrange(
                        "p a t -> p (a t)"), po[a][:, :]).then_inc(po_taken, 1)

            def head(h, more):
                normalize(h, 0)
                maxima(h, 1)
                outputs(h, 0)
                normalize(h, 1)
                if more:
                    maxima(h + 1, 0)
                outputs(h, 1)

            dve.nop().then_inc(po_taken, 2)
            maxima(0, 0)
            each_head(dve, head)


def expert_scores_stage(nc, consts, h, w_query, keys_d, scores_d, high, low, rstd):
    n_tiles = 2 * PH
    with Stage(nc, "score") as st:
        x = SplitInput(nc, st, consts, h, "ffn", high, low, rstd)
        proj = Projection(nc, st, w_query, n_tiles, x)
        keys = st.sb("keys", [P, n_tiles, NK])
        q = [st.sb(f"q{i}", [P, T]) for i in range(2)]
        s = [st.sb(f"s{i}", [P, NT, NK]) for i in range(2)]
        ss = st.psum("ss", [P, NT, NK])
        stored = [st.sem(f"stored{i}") for i in range(2)]
        by_head = scores_d.rearrange("(h t) p w k -> h p w t k", h=PH)
        keys_ready, s_mm, s_ready = st.sem("keys_ready"), st.sem("s_mm"), st.sem("s_ready")
        block = st.block()

        @block.sync
        def _(sp):
            proj.first_loads(sp)
            sp.dma_start(keys[:, :, :], keys_d).then_inc(keys_ready, 16)
            with sp.Fori(1, n_tiles // 2) as g:
                for i in range(2):
                    sp.wait_ge(proj.w_low, g * 2 + (i - 1))
                    sp.dma_start(proj.raw[i][:, :], w_query[bass.ds(g * 2 + i, 1)].rearrange("a p n -> (a p) n")
                                 ).then_inc(proj.w_ready[i], 16)
                    sp.wait_ge(s_ready, g * 2 + i)
                    sp.dma_start(by_head[bass.ds(g - 1, 1), :, i].rearrange("h p t k -> (h p) t k"),
                                 s[i][:, :, :]).then_inc(stored[i], 16)
            for i in range(2):
                sp.wait_ge(s_ready, n_tiles + i)
                sp.dma_start(by_head[PH - 1, :, i], s[i][:, :, :]).then_inc(stored[i], 16)
                sp.wait_ge(stored[i], 16 * (PH + 1))

        @block.gpsimd
        def _(pool):
            x.add_squares(pool)

        @block.tensor
        def _(pe):
            def scores(i, tile):
                if isinstance(tile, int) and tile == 0:
                    pe.wait_ge(keys_ready, 16)
                pe.wait_ge(proj.taken, tile + 3)
                pe.wait_ge(s_ready, tile + 1)
                at = slice(tile, tile + 1) if isinstance(tile, int) else bass.ds(tile, 1)
                for t in range(NT):
                    last = nc.tensor.matmul(ss[:, t, :], q[i][:, t * P:(t + 1) * P],
                                            keys[:, at, :].rearrange("p a k -> p (a k)"), start=True, stop=True)
                last.then_inc(s_mm, 1)

            pe.nop().then_inc(s_mm, 2)
            proj.products(pe, scores)
            scores(1, n_tiles - 1)

        @block.scalar
        def _(act):
            def scores(i, tile):
                act.wait_ge(s_mm, tile + 3)
                act.wait_ge(stored[i], (tile - i) * 8 + 16)
                nc.scalar.activation(s[i][:, :, :], ss[:, :, :], ACT.Copy).then_inc(s_ready, 1)

            act.nop().then_inc(s_ready, 1)
            for i in range(2):
                act.nop().then_inc(stored[i], 16)
            proj.first_highs(act)
            proj.highs(act, lambda i, tile: scores(i, tile - 2))
            scores(0, n_tiles - 2)
            scores(1, n_tiles - 1)

        @block.vector
        def _(dve):
            proj.first_lows(dve)

            def take(i, tile):
                dve.wait_ge(s_mm, tile + 1)
                nc.vector.tensor_tensor(q[i][:, :], proj.product(i), x.rstd[:, :], ALU.mult).then_inc(proj.taken, 1)

            proj.takes(dve, take)


def experts_in_stage(nc, consts, high, low, rstd, expert_u, scores_d, hidden_d, gates_d):
    LOW = -3.0e38
    heads = NT * PH
    with Stage(nc, "xin") as st:
        raw = [st.sb(f"raw{i}", [P, KC * P]) for i in range(2)]
        uh = [st.sb(f"uh{i}", [P, KC * P], F32R) for i in range(2)]
        ul = [st.sb(f"ul{i}", [P, KC * P], F32R) for i in range(2)]
        hid = [st.sb(f"hid{i}", [P, T]) for i in range(2)]
        ps = [st.psum(f"ps{i}", [P, 2, HALF]) for i in range(2)]
        pre = [st.sb(f"pre{i}", [P, T]) for i in range(2)]
        pre_ready = st.sem("pre_ready")
        sc, scw = st.sb("sc", [P, 2, NK]), st.sb("scw", [P, 2, NK])
        vals, ix, ixf = st.sb("vals", [P, 2, TOPK]), st.sb("ix", [P, 2, TOPK], U32), st.sb("ixf", [P, 2, TOPK])
        cand, candw, cv = st.sb("cand", [P, TOPK, TOPK]), st.sb("candw", [P, TOPK * TOPK]), st.sb("cv", [P, TOPK])
        ci, place, placef = st.sb("ci", [P, TOPK], U32), st.sb("place", [P, 2, TOPK], U32), st.sb("placef", [P, 2, TOPK])
        sel, e12, flat_e = st.sb("sel", [P, 2, TOPK, TOPK]), st.sb("e12", [P, 2, TOPK]), st.sb("flat_e", [P, TOPK])
        iota_i, iota = st.sb("iota_i", [P, TOPK], I32), st.sb("iota", [P, TOPK])
        tok_i, tok, wrap = st.sb("tok_i", [P, 1], I32), st.sb("tok", [P, 1]), st.sb("wrap", [P, 1])
        idx, gates = st.sb("idx", [P, TOPK], U32), st.sb("gates", [P, TOPK])
        gexp, nmax, gsum = st.sb("gexp", [P, TOPK]), st.sb("nmax", [P, 1]), st.sb("gsum", [P, 1])
        raw_ready = [st.sem(f"raw_ready{i}") for i in range(2)]
        stored = [st.sem(f"stored{i}") for i in range(2)]
        high_done, low_done, mm_done, gelu_done = (st.sem(x) for x in ("high_done", "low_done", "mm_done", "gelu_done"))
        sc_ready, sc_used, cv_ready, gate_exp = (st.sem(x) for x in ("sc_ready", "sc_used", "cv_ready", "gate_exp"))
        idx_ready, added, iota_ready = st.sem("idx_ready"), st.sem("added"), st.sem("iota_ready")
        block = st.block()
        gates_flat = gates_d.rearrange("j i t -> (j i t)").unsqueeze(1)

        @block.sync
        def _(sp):
            for i in range(2):
                sp.dma_start(raw[i][:, :], expert_u[i]).then_inc(raw_ready[i], 16)
            sp.dma_start(sc[:, :, :], scores_d[0]).then_inc(sc_ready, 16)
            with sp.Fori(1, NK // 2) as g:
                for i in range(2):
                    sp.wait_ge(low_done, g * 2 + (i - 1))
                    sp.dma_start(raw[i][:, :], expert_u[bass.ds(g * 2 + i, 1)].rearrange("a p n -> (a p) n")
                                 ).then_inc(raw_ready[i], 16)
                    if i == 0:
                        sp.wait_ge(sc_used, g)
                        sp.dma_start(sc[:, :, :], scores_d[bass.ds(g, 1)].rearrange("a p w k -> (a p) w k")
                                     ).then_inc(sc_ready, 16)
                    sp.wait_ge(gelu_done, g * 2 + (i + 1))
                    sp.dma_start(hidden_d[bass.ds(g * 2 + (i - 2), 1)].rearrange("a p t -> (a p) t"), hid[i][:, :]
                                 ).then_inc(stored[i], 16)
            for i in range(2):
                sp.wait_ge(gelu_done, NK + 1 + i)
                sp.dma_start(hidden_d[NK - 2 + i], hid[i][:, :]).then_inc(stored[i], 16)
                sp.wait_ge(stored[i], 16 * (NK // 2 + 1))

        @block.tensor
        def _(pe):
            with pe.Fori(0, NK // 2) as g:
                for i in range(2):
                    pe.wait_ge(low_done, g * 2 + (i + 1))
                    pe.wait_ge(pre_ready, g * 2 + (i + 1))
                    for kc in range(KC):
                        cols = slice(kc * P, kc * P + P)
                        for w, x in ((uh[i], high), (uh[i], low), (ul[i], high)):
                            for h in range(2):
                                last = nc.tensor.matmul(ps[i][:, h, :], w[:, cols], x[:, kc, h * HALF:(h + 1) * HALF],
                                                        start=(kc == 0 and w is uh[i] and x is high),
                                                        stop=(kc == KC - 1 and w is ul[i]))
                    last.then_inc(mm_done, 1)

        @block.scalar
        def _(act):
            def high_part(i, k):
                act.wait_ge(raw_ready[i], k)
                nc.scalar.activation(uh[i][:, :], raw[i][:, :], ACT.Copy).then_inc(high_done, 1)

            def gelu(i, done, free):
                act.wait_ge(pre_ready, done + 2)
                act.wait_ge(stored[i], free)
                nc.scalar.activation(hid[i][:, :], pre[i][:, :], ACT.Gelu).then_inc(gelu_done, 1)

            def gate(k):
                act.wait_ge(cv_ready, k)
                nc.scalar.activation(gexp[:, :], cv[:, :], ACT.Exp, bias=nmax[:, :],
                                     accum_out=gsum[:, :]).then_inc(gate_exp, 1)

            high_part(0, 16)
            high_part(1, 16)
            gate(1)
            with act.Fori(1, NK // 2) as g:
                for i in range(2):
                    act.wait_ge(mm_done, g * 2 + (i - 1))
                    high_part(i, g * 16 + 16)
                    gelu(i, g * 2 + (i - 1), g * 16)
                gate(g + 1)
            for i in range(2):
                gelu(i, NK - 1 + i, 16 * (NK // 2))

        @block.gpsimd
        def _(pool):
            nc.gpsimd.iota(iota_i[:, :], [[1, TOPK]], base=0, channel_multiplier=0).then_inc(iota_ready, 1)
            nc.gpsimd.iota(tok_i[:, :], [[1, 1]], base=0, channel_multiplier=1).then_inc(iota_ready, 1)
            found = pool.alloc_register("found")
            with pool.Fori(0, heads) as n:
                pool.reg_mov(found, n + 1)
                pool.wait_ge(iota_ready, 1)
                pool.wait_ge(idx_ready, found)
                for k in range(TOPK):
                    if k:
                        pool.wait_ge(iota_ready, 1)
                    pool.indirect_dma_start(gates_flat, bass.IndirectOffsetOnAxis(ap=idx[:, k:k + 1], axis=0),
                                            gates[:, k:k + 1], None, compute_op=ALU.add).then_inc(added, 16)
            pool.wait_ge(added, 16 * TOPK * heads)

        @block.vector
        def _(dve):
            def low_part(i, k):
                dve.wait_ge(high_done, k)
                nc.vector.tensor_tensor(ul[i][:, :], raw[i][:, :], uh[i][:, :].bitcast(F32),
                                        ALU.subtract).then_inc(low_done, 1)

            def scale_product(i, done):
                dve.wait_ge(mm_done, done)
                dve.wait_ge(gelu_done, done)
                nc.vector.tensor_tensor(pre[i][:, :], ps[i][:, :, :].rearrange("p a t -> p (a t)"), rstd[:, :],
                                        ALU.mult).then_inc(pre_ready, 1)

            def best_keys(k):
                dve.drain()
                dve.wait_ge(sc_ready, k * 16)
                nc.vector.memset(wrap[:, :], 0.0)
                dve.drain()
                for w in range(2):
                    nc.vector.max(vals[:, w, 0:8], sc[:, w, :])
                dve.drain()
                for w in range(2):
                    nc.vector.max_index(ix[:, w, 0:8], vals[:, w, 0:8], sc[:, w, :])
                    last = nc.vector.match_replace(scw[:, w, :], vals[:, w, 0:8], sc[:, w, :], LOW)
                last.then_inc(sc_used, 1)
                dve.drain()
                for w in range(2):
                    nc.vector.max(vals[:, w, 8:16], scw[:, w, :])
                dve.drain()
                for w in range(2):
                    nc.vector.max_index(ix[:, w, 8:16], vals[:, w, 8:16], scw[:, w, :])
                nc.vector.tensor_tensor(cand[:, :, :], vals[:, 0, :].unsqueeze(2).broadcast_to([P, TOPK, TOPK]),
                                        vals[:, 1, :].unsqueeze(1).broadcast_to([P, TOPK, TOPK]), ALU.add)

            def best_pairs(k, first=False):
                dve.drain()
                flat = cand[:, :, :].rearrange("p a b -> p (a b)")
                nc.vector.max(cv[:, 0:8], flat)
                nc.vector.tensor_copy(ixf[:, :, :], ix[:, :, :])
                dve.drain()
                nc.vector.tensor_scalar(nmax[:, :], cv[:, 0:1], -1.0, None, ALU.mult)
                nc.vector.max_index(ci[:, 0:8], cv[:, 0:8], flat)
                nc.vector.match_replace(candw[:, :], cv[:, 0:8], flat, LOW)
                dve.drain()
                nc.vector.max(cv[:, 8:16], candw[:, :]).then_inc(cv_ready, 1)
                dve.drain()
                nc.vector.max_index(ci[:, 8:16], cv[:, 8:16], candw[:, :])
                dve.drain()
                nc.vector.tensor_scalar(place[:, 0, :], ci[:, :], 4, None, ALU.logical_shift_right)
                nc.vector.tensor_scalar(place[:, 1, :], ci[:, :], 15, None, ALU.bitwise_and)
                dve.drain()
                nc.vector.tensor_copy(placef[:, :, :], place[:, :, :])
                dve.drain()
                nc.vector.tensor_tensor(sel[:, :, :, :], placef[:, :, :].unsqueeze(3).broadcast_to([P, 2, TOPK, TOPK]),
                                        iota[:, :].unsqueeze(1).unsqueeze(1).broadcast_to([P, 2, TOPK, TOPK]),
                                        ALU.is_equal)
                dve.drain()
                nc.vector.tensor_tensor(sel[:, :, :, :], sel[:, :, :, :],
                                        ixf[:, :, :].unsqueeze(2).broadcast_to([P, 2, TOPK, TOPK]), ALU.mult)
                dve.drain()
                nc.vector.tensor_reduce(e12[:, :, :], sel[:, :, :, :], AX.X, ALU.add)
                dve.drain()
                nc.vector.scalar_tensor_tensor(out=flat_e[:, :], in0=e12[:, 1, :], scalar=float(NK), in1=e12[:, 0, :],
                                               op0=ALU.mult, op1=ALU.add)
                dve.wait_ge(gate_exp, k)
                nc.vector.reciprocal(gsum[:, :], gsum[:, :])
                dve.drain()
                if not first:
                    dve.wait_ge(added, (k - 1) * (16 * TOPK))
                nc.vector.tensor_scalar(gates[:, :], gexp[:, :], gsum[:, :], None, ALU.mult)
                nc.vector.tensor_scalar(idx[:, :], flat_e[:, :], float(T), tok[:, :], ALU.mult,
                                        ALU.add).then_inc(idx_ready, 1)
                dve.drain()
                nc.vector.tensor_scalar(tok[:, :], tok[:, :], float(P), None, ALU.add)
                dve.drain()
                nc.vector.tensor_scalar(wrap[:, :], tok[:, :], float(T), -float(T), ALU.is_ge, ALU.mult)
                dve.drain()
                nc.vector.tensor_tensor(tok[:, :], tok[:, :], wrap[:, :], ALU.add)

            dve.wait_ge(iota_ready, 2)
            nc.vector.tensor_copy(iota[:, :], iota_i[:, :])
            nc.vector.tensor_copy(tok[:, :], tok_i[:, :])
            dve.nop().then_inc(gelu_done, 2)
            dve.nop().then_inc(pre_ready, 2)
            for i in range(2):
                dve.nop().then_inc(stored[i], 16)
            low_part(0, 1)
            low_part(1, 2)
            best_keys(1)
            best_pairs(1, first=True)
            with dve.Fori(1, NK // 2) as g:
                scale_product(0, g * 2 - 1)
                low_part(0, g * 2 + 1)
                best_keys(g + 1)
                scale_product(1, g * 2)
                low_part(1, g * 2 + 2)
                best_pairs(g + 1)
            scale_product(0, NK - 1)
            scale_product(1, NK)


def experts_out_stage(nc, consts, hT, expert_v, hidden_d, gates_d, out):
    G = 4
    groups = NK // G
    with Stage(nc, "xout") as st:
        hid = [st.sb(f"hid{i}", [P, T]) for i in range(2)]
        gat = [st.sb(f"gat{i}", [P, T]) for i in range(2)]
        val = [st.sb(f"val{i}", [P, D]) for i in range(2)]
        ah, al, vh, vl = (st.sb(x, [P, 2 * G, T], F32R) for x in ("ah", "al", "vh", "vl"))
        ps = [st.psum(f"ps{i}", [P, 2, HALF]) for i in range(4)]
        in_ready = [st.sem(f"in_ready{i}") for i in range(2)]
        product, act_high, val_high, split_done = (st.sem(x) for x in ("product", "act_high", "val_high", "split_done"))
        pair_done, added = st.sem("pair_done"), st.sem("added")
        sq, acc, rstd = hid, gat[0], val[0]
        sq_ready, sq_added, sums_ready, std_ready = (st.sem(x) for x in ("sq_ready", "sq_added", "sums_ready",
                                                                        "std_ready"))
        rstd_ready, normed, stored = st.sem("rstd_ready"), st.sem("normed"), st.sem("stored")
        block = st.block()

        def each_group(eng, body):
            with eng.Fori(0, groups // 2 - 1) as gg:
                body(gg * 2, 0, True)
                body(gg * 2 + 1, 1, True)
            body(groups - 2, 0, True)
            body(groups - 1, 1, False)

        @block.sync
        def _(sp):
            def load(c, r, index):
                sp.dma_start(val[r][:, :], index(expert_v)).then_inc(in_ready[r], 16)
                sp.dma_start(hid[r][:, :], index(hidden_d)).then_inc(in_ready[r], 16)
                sp.dma_start(gat[r][:, :], index(gates_d)).then_inc(in_ready[r], 16)

            for c in range(2):
                load(c, c, lambda x: x[c])
            with sp.Fori(1, NK // 2) as cc:
                for r in range(2):
                    sp.wait_ge(split_done, cc * 2 + (r - 1))
                    load(cc * 2 + r, r, lambda x: x[bass.ds(cc * 2 + r, 1)].rearrange("a p t -> (a p) t"))
            for f in range(KC):
                sp.wait_ge(normed, f + 1)
                sp.dma_start(out[f * P:(f + 1) * P, :], hT[:, f, :]).then_inc(stored, 16)
            sp.wait_ge(stored, 16 * KC)

        @block.gpsimd
        def _(pool):
            for f in range(KC):
                pool.wait_ge(sq_ready, f + 1)
                if f == 0:
                    nc.gpsimd.tensor_copy(acc[:, :], sq[0][:, :]).then_inc(sq_added, 1)
                else:
                    pool.wait_ge(sq_added, f)
                    nc.gpsimd.tensor_tensor(acc[:, :], acc[:, :], sq[f % 2][:, :], ALU.add).then_inc(sq_added, 1)

        @block.tensor
        def _(pe):
            def group(g, parity, more):
                pe.wait_ge(split_done, g * G + G)
                for f in range(KC):
                    out = ps[f % 4]
                    pe.wait_ge(added, g * KC + (f + 1))
                    for s in range(G):
                        n = parity * G + s
                        for w, x in ((vh, ah), (vh, al), (vl, ah)):
                            for h in range(2):
                                last = nc.tensor.matmul(out[:, h, :], w[:, n, f * P:(f + 1) * P],
                                                        x[:, n, h * HALF:(h + 1) * HALF],
                                                        start=(s == 0 and w is vh and x is ah),
                                                        stop=(s == G - 1 and w is vl))
                    last.then_inc(pair_done, 1)

            each_group(pe, group)
            pe.wait_ge(sq_added, KC)
            for h in range(2):
                last = nc.tensor.matmul(ps[0][:, h, :], consts["ones"][:, :], acc[:, h * HALF:(h + 1) * HALF],
                                        start=True, stop=True)
            last.then_inc(sums_ready, 1)

        @block.scalar
        def _(act):
            def highs(c, n):
                act.wait_ge(in_ready[n % 2], (c - n % 2) * 24 + 48)
                nc.scalar.activation(vh[:, n, :], val[n % 2][:, :], ACT.Copy).then_inc(val_high, 1)
                act.wait_ge(product, c + 1)
                nc.scalar.activation(ah[:, n, :], hid[n % 2][:, :], ACT.Copy).then_inc(act_high, 1)

            for s in range(G):
                highs(s, s)

            def group(g, parity, more):
                if not more:
                    return
                act.wait_ge(added, g * KC + 4)
                for s in range(G):
                    highs(g * G + (G + s), (1 - parity) * G + s)

            each_group(act, group)
            act.wait_ge(split_done, NK)
            for f in range(KC):
                act.wait_ge(added, (groups - 1) * KC + (4 + f + 1))
                if f >= 2:
                    act.wait_ge(sq_added, f - 1)
                nc.scalar.activation(sq[f % 2][:, :], hT[:, f, :], ACT.Square).then_inc(sq_ready, 1)
            act.wait_ge(sums_ready, 1)
            nc.scalar.activation(rstd[:, :], ps[0][:, :, :].rearrange("p a t -> p (a t)"), ACT.Sqrt,
                                 bias=consts["eps"][:, 0:1], scale=1.0 / D).then_inc(std_ready, 1)

        @block.vector
        def _(dve):
            def multiply(c, r):
                dve.wait_ge(in_ready[r], (c - r) * 24 + 48)
                nc.vector.tensor_tensor(hid[r][:, :], hid[r][:, :], gat[r][:, :], ALU.mult).then_inc(product, 1)

            def lows(c, n):
                dve.wait_ge(val_high, c + 1)
                nc.vector.tensor_tensor(vl[:, n, :], val[n % 2][:, :], vh[:, n, :].bitcast(F32), ALU.subtract)
                dve.wait_ge(act_high, c + 1)
                nc.vector.tensor_tensor(al[:, n, :], hid[n % 2][:, :], ah[:, n, :].bitcast(F32),
                                        ALU.subtract).then_inc(split_done, 1)

            dve.nop().then_inc(added, 4)
            for s in range(G):
                multiply(s, s % 2)
                dve.drain()
                lows(s, s)

            def group(g, parity, more):
                for f in range(KC):
                    if more and f % 2 == 0:
                        multiply(g * G + (G + f // 2), (f // 2) % 2)
                    dve.drain()
                    dve.wait_ge(pair_done, g * KC + (f + 1))
                    nc.vector.tensor_tensor(hT[:, f, :], hT[:, f, :], ps[f % 4][:, :, :].rearrange("p a t -> p (a t)"),
                                            ALU.add).then_inc(added, 1)
                    if more and f % 2 == 0:
                        lows(g * G + (G + f // 2), (1 - parity) * G + f // 2)

            each_group(dve, group)
            dve.wait_ge(std_ready, 1)
            nc.vector.reciprocal(rstd[:, :], rstd[:, :]).then_inc(rstd_ready, 1)
            dve.wait_ge(rstd_ready, 1)
            for f in range(KC):
                nc.vector.scalar_tensor_tensor(out=hT[:, f, :], in0=hT[:, f, :], scalar=col(consts, "fin", f),
                                               in1=rstd[:, :], op0=ALU.mult, op1=ALU.mult).then_inc(normed, 1)


def build(nc, a, out):
    with ExitStack() as ctx:
        def sb(name, shape, dt=F32):
            return ctx.enter_context(nc.sbuf_tensor(name, shape, dt))

        consts = {"cols": sb("cols", [P, NCOLS]), "ones": sb("ones", [P, P]), "eps": sb("eps", [P, 2]),
                  "ident": sb("ident", [P, P]), "headones": sb("headones", [P, P]), "rot": sb("rot", [ROPE, P]),
                  "mask4": sb("mask4", [P, 4, P]), "level": sb("level", [P, 6, P]), "lower": sb("lower", [P, P]),
                  "scanmask": sb("scanmask", [P, 4 * P])}
        feats_d = nc.dram_tensor("feats_d", (NF, P, T), F32).ap()
        scores_d = nc.dram_tensor("scores_d", (NT * PH, P, 2, NK), F32).ap()
        hidden_d = nc.dram_tensor("hidden_d", (NK, P, T), F32).ap()
        gates_d = nc.dram_tensor("gates_d", (NK, P, T), F32).ap()
        build_constants(nc, consts, a["cols"])
        lower = sb("act_lower", [P, KC, T])
        project_in_stage(nc, consts, a["x"], lower, a["w_in"], feats_d)
        with ExitStack() as mla:
            feats = mla.enter_context(nc.sbuf_tensor("feats", [P, 3, T], F32))
            cos = mla.enter_context(nc.sbuf_tensor("cos", [ROPE, T], F32))
            sin = mla.enter_context(nc.sbuf_tensor("sin", [ROPE, T], F32))
            krope = mla.enter_context(nc.sbuf_tensor("krope", [ROPE, T], F32))
            mla_prepare_stage(nc, consts, feats, feats_d, a["positions"], cos, sin, krope)
            mla_stage(nc, consts, feats, cos, sin, krope, lower, a["w_uq"], a["w_ukv"], gates_d)
        rwkv_stage(nc, consts, feats_d, a["rw_w_up"], a["rw_a_up"], a["rw_g_up"], lower)
        with ExitStack() as late:
            upper = late.enter_context(nc.sbuf_tensor("act_upper", [P, KC, T], F32))
            k = late.enter_context(nc.sbuf_tensor("k", [P, XH, 2 * MEM], F32))
            v = late.enter_context(nc.sbuf_tensor("v", [P, XH, 2 * MEM], F32))
            residual_stage(nc, consts, "out", a["w_out"], lower, upper, upper, load=a["x"])
            with ExitStack() as memory:
                memn = memory.enter_context(nc.sbuf_tensor("memn", [P, KC, MEM], F32))
                norm_stage(nc, consts, "nmem", memn, "mem", memn, MEM, load=a["mem"])
                memory_stage(nc, memn, a["xa_wk"], a["xa_wv"], k, v)
            queries_stage(nc, consts, upper, a["xa_wq"], lower)
            cross_attention_stage(nc, consts, lower, k, v)
            residual_stage(nc, consts, "xo", a["xa_wo"], lower, upper, lower)
        with ExitStack() as deep:
            high = deep.enter_context(nc.sbuf_tensor("high", [P, KC, T], F32R))
            low = deep.enter_context(nc.sbuf_tensor("low", [P, KC, T], F32R))
            rstd = deep.enter_context(nc.sbuf_tensor("rstd", [P, T], F32))
            expert_scores_stage(nc, consts, lower, a["peer_wq"], a["peer_keys"], scores_d, high, low, rstd)
            experts_in_stage(nc, consts, high, low, rstd, a["expert_u"], scores_d, hidden_d, gates_d)
        experts_out_stage(nc, consts, lower, a["expert_v"], hidden_d, gates_d, out)


def layout(inputs):
    def blocks(w, n):
        k = w.shape[0] // P
        return np.ascontiguousarray(w.reshape(k, P, w.shape[1] // n, n).transpose(2, 1, 0, 3))

    def tiles(w):
        return blocks(w, P).reshape(-1, P, KC * P)

    def vec(name, rows=P):
        return np.asarray(inputs[name]).reshape(-1, rows).T

    a = {k: np.asarray(v) for k, v in inputs.items()}
    w_in = a["w_in"][0]
    m = Q_LORA + KV_LORA
    r = m + ROPE
    out = {"x": np.ascontiguousarray(a["x"][0].T).reshape(KC, P, T)}
    out["positions"] = a["positions"]
    out["w_in"] = tiles(np.concatenate([w_in[:, 0:m], w_in[:, r:r + 3 * RW], w_in[:, r + 3 * RW + 128:],
                                        w_in[:, m:r], w_in[:, r + 3 * RW:r + 3 * RW + 128],
                                        np.zeros((D, 64), np.float32)], 1))
    cols = np.zeros((P, NCOLS), np.float32)

    def put(name, part):
        cols[0:part.shape[0], COLS[name]:COLS[name] + part.shape[1]] = part

    for name, key in (("mix", "norm_mix_g"), ("xa", "norm_xa_g"), ("mem", "norm_mem_g"), ("ffn", "norm_ffn_g"),
                      ("w0", "rw_w0"), ("a0", "rw_a0"), ("kk", "rw_k_k"), ("ka", "rw_k_a"), ("rk", "rw_r_k"),
                      ("lnw", "rw_lnx_w"), ("lnb", "rw_lnx_b"), ("qg", "q_norm_g"), ("kvg", "kv_norm_g"),
                      ("fin", "final_norm_g")):
        put(name, vec(key))
    mu = a["shift_mu"][0]
    cols[:, COLS["mu"] + RT:COLS["mu"] + GT] = mu[0:3 * RW].reshape(-1, P).T
    cols[:, COLS["mu"] + GT] = mu[3 * RW + 128:]
    cols[64:, COLS["mu"] + KRWD] = mu[3 * RW:3 * RW + 64]
    cols[0:64, COLS["mu"] + AD] = mu[3 * RW + 64:3 * RW + 128]
    half = np.float32(10000.0) ** (-np.arange(0, ROPE, 2, dtype=np.float32) / np.float32(ROPE))
    cols[0:ROPE, COLS["inv"]] = np.concatenate([half, half])
    out["cols"] = cols
    out["w_uq"] = blocks(a["w_uq"][0], P + ROPE)
    out["w_ukv"] = np.ascontiguousarray(a["w_ukv"][0].reshape(P, MLA_HEADS, 2 * P).transpose(1, 0, 2))
    for name in ("rw_w_up", "rw_a_up", "rw_g_up"):
        out[name] = a[name][0]
    for name in ("w_out", "xa_wq", "xa_wo", "peer_wq"):
        out[name] = tiles(a[name][0])
    out["xa_wk"], out["xa_wv"] = (blocks(a[x][0], D // XH) for x in ("xa_wk", "xa_wv"))
    out["mem"] = np.ascontiguousarray(a["mem"][0].T).reshape(KC, P, MEM)
    out["peer_keys"] = np.ascontiguousarray(a["peer_keys"][0].reshape(2 * PH, NK, P).transpose(2, 0, 1))
    out["expert_u"] = np.ascontiguousarray(a["expert_u"][0].reshape(NK, NK, KC, P).transpose(1, 3, 2, 0)).reshape(
        NK, P, KC * P)
    out["expert_v"] = np.ascontiguousarray(a["expert_v"][0].reshape(NK, NK, D).transpose(1, 0, 2))
    return out


def kernel(**inputs):
    import concourse.bacc as bacc
    from concourse.bass_utils import run_bass_kernel_spmd

    nc = bacc.Bacc("TRN2", target_bir_lowering=False, num_devices=1)
    arrays, aps = {}, {}
    for name, arr in layout(inputs).items():
        arrays[f"in_{name}"] = arr
        aps[name] = nc.dram_tensor(f"in_{name}", arr.shape, mybir.dt.from_np(arr.dtype), kind="ExternalInput").ap()
    out = nc.dram_tensor("out_0", (T, D), F32, kind="ExternalOutput").ap()
    build(nc, aps, out)
    r = run_bass_kernel_spmd(nc, [arrays], core_ids=[0])
    return np.ascontiguousarray(r.results[0]["out_0"].T).reshape(1, T, D)
```
